# Optimizing a Trainium2 kernel written in Bass

```python
import jax
import jax.numpy as jnp
from jax import lax
import numpy as np
import jax, jax.numpy as jnp

D_MODEL = 1024
BATCH = 1
SEQ = 256
DEPTH = 1

GRID_W = 64
CTX_LEN = 256
N_MOD = 6
H_ATTN = 8
KV_ATTN = 2
HD_ATTN = 64
GQA_GROUP = H_ATTN // KV_ATTN
ATTN_WIDTH = H_ATTN * HD_ATTN
KV_WIDTH = KV_ATTN * HD_ATTN
ROPE_THETA = 10000.0
ROPE_PAIRS_AXIS = HD_ATTN // 4
Q_BLOCK = 128
H_GDN = 4
DK_GDN = 128
DV_GDN = 128
GDN_QK = H_GDN * DK_GDN
GDN_QKV_WIDTH = H_GDN * (2 * DK_GDN + DV_GDN)
GDN_WIDTH = H_GDN * DV_GDN
GDN_CHUNK = 64
SHORT_CONV = 3
MIX_WIDTH = ATTN_WIDTH + GDN_WIDTH
IN_SPLITS = (ATTN_WIDTH, KV_WIDTH, KV_WIDTH, GDN_QKV_WIDTH, GDN_WIDTH, H_GDN, H_GDN, H_GDN, H_GDN)
IN_WIDTH = ATTN_WIDTH + 2 * KV_WIDTH + GDN_QKV_WIDTH + GDN_WIDTH + 4 * H_GDN
D_FF = 2816
FFN_CONV = 3
EPS = 1e-6


def rms_norm(x, g):
    xf = x.astype(jnp.float32)
    y = xf * lax.rsqrt(jnp.mean(xf * xf, axis=-1, keepdims=True) + EPS)
    return (y * g.astype(jnp.float32)).astype(x.dtype)

def l2_norm(x):
    return x * lax.rsqrt(jnp.sum(x * x, axis=-1, keepdims=True) + EPS)

def ada_terms(cvec, w_mod, b_mod):
    m = jax.nn.silu(cvec) @ w_mod + b_mod
    m = m.reshape(m.shape[:-1] + (N_MOD, D_MODEL))
    return [m[..., i, None, :] for i in range(N_MOD)]

def modulate(x, g, shift, scale):
    return rms_norm(x, g) * (1.0 + scale) + shift

def depthwise_conv(x, w):
    pad = w.shape[0] // 2
    return lax.conv_general_dilated(
        x, w[:, None, :].astype(x.dtype), window_strides=(1,), padding=((pad, pad),),
        dimension_numbers=("NWC", "WIO", "NWC"), feature_group_count=x.shape[-1])

def axial_rope_tables(n_tokens):
    rows = n_tokens // GRID_W
    row = jnp.repeat(jnp.arange(rows, dtype=jnp.float32), GRID_W)
    col = jnp.tile(jnp.arange(GRID_W, dtype=jnp.float32), rows)
    inv_freq = ROPE_THETA ** (-jnp.arange(ROPE_PAIRS_AXIS, dtype=jnp.float32) / ROPE_PAIRS_AXIS)
    ang = jnp.concatenate([row[:, None] * inv_freq, col[:, None] * inv_freq], axis=-1)
    return jnp.cos(ang), jnp.sin(ang)

def apply_rope(x, cos, sin):
    half = x.shape[-1] // 2
    x1, x2 = x[..., :half], x[..., half:]
    c, s = cos[None, :, None, :], sin[None, :, None, :]
    return jnp.concatenate([x1 * c - x2 * s, x2 * c + x1 * s], axis=-1)

def attn_q(q, q_norm_g, rope):
    B, T = q.shape[:2]
    q = rms_norm(q.reshape(B, T, H_ATTN, HD_ATTN), q_norm_g).astype(jnp.float32)
    if rope is not None:
        q = apply_rope(q, *rope)
    return q.reshape(B, T, KV_ATTN, GQA_GROUP, HD_ATTN) * (HD_ATTN ** -0.5)

def attn_kv(k, v, k_norm_g, rope):
    B, T = k.shape[:2]
    k = rms_norm(k.reshape(B, T, KV_ATTN, HD_ATTN), k_norm_g).astype(jnp.float32)
    if rope is not None:
        k = apply_rope(k, *rope)
    return k, v.reshape(B, T, KV_ATTN, HD_ATTN).astype(jnp.float32)

def block_attention(q, k, v):
    B, T = q.shape[:2]
    qb = jnp.swapaxes(q.reshape((B, T // Q_BLOCK, Q_BLOCK) + q.shape[2:]), 0, 1)

    def one_block(q_blk):
        s = jnp.einsum("bqkgd,bskd->bkgqs", q_blk, k)
        p = jax.nn.softmax(s, axis=-1)
        return jnp.einsum("bkgqs,bskd->bqkgd", p, v)

    o = lax.map(one_block, qb)
    return jnp.swapaxes(o, 0, 1).reshape(B, T, -1)

def gdn_inputs(qkv_raw, conv_w, with_q):
    if not with_q:
        qkv_raw, conv_w = qkv_raw[..., GDN_QK:], conv_w[:, GDN_QK:]
    y = jax.nn.silu(depthwise_conv(qkv_raw, conv_w).astype(jnp.float32))
    B, T = y.shape[:2]
    q = None
    if with_q:
        q = l2_norm(y[..., :GDN_QK].reshape(B, T, H_GDN, DK_GDN)) * (DK_GDN ** -0.5)
        y = y[..., GDN_QK:]
    k = l2_norm(y[..., :GDN_QK].reshape(B, T, H_GDN, DK_GDN))
    v = y[..., GDN_QK:].reshape(B, T, H_GDN, DV_GDN)
    return q, k, v

def gdn_decay(a, a_log, dt_bias):
    return -jnp.exp(a_log.astype(jnp.float32)) * jax.nn.softplus(a.astype(jnp.float32) + dt_bias.astype(jnp.float32))

def chunk_gated_delta(q, k, v, g, beta, s0):
    with_output = q is not None
    B, T, H, dk = k.shape
    dv = v.shape[-1]
    C = GDN_CHUNK
    N = T // C

    def to_chunks(a):
        a = jnp.moveaxis(a, 2, 1)
        return a.reshape((B, H, N, C) + a.shape[3:])

    k, v, g, beta = to_chunks(k), to_chunks(v), to_chunks(g), to_chunks(beta)
    g_cum = jnp.cumsum(g, axis=-1)
    g_last = g_cum[..., -1]
    idx = jnp.arange(C)
    incl = idx[:, None] >= idx[None, :]
    strict = idx[:, None] > idx[None, :]
    diff = g_cum[..., :, None] - g_cum[..., None, :]
    decay_incl = jnp.exp(jnp.where(incl, diff, -jnp.inf))
    decay_strict = jnp.where(strict, decay_incl, 0.0)
    k_beta = k * beta[..., None]
    lower = jnp.einsum("bhnid,bhnjd->bhnij", k_beta, k) * decay_strict
    eye = jnp.eye(C, dtype=jnp.float32)
    t_inv = lax.linalg.triangular_solve(lower + eye, jnp.broadcast_to(eye, lower.shape),
                                        left_side=True, lower=True, unit_diagonal=True)
    u = t_inv @ (v * beta[..., None])
    w = t_inv @ (k_beta * jnp.exp(g_cum)[..., None])
    k_dec = k * jnp.exp(g_last[..., None] - g_cum)[..., None]
    decay_last = jnp.exp(g_last)
    xs = (k_dec, w, u, decay_last)
    if with_output:
        q = to_chunks(q)
        q_dec = q * jnp.exp(g_cum)[..., None]
        intra = jnp.einsum("bhnid,bhnjd->bhnij", q, k) * decay_incl
        xs = xs + (q_dec, intra)
    xs = tuple(jnp.moveaxis(a, 2, 0) for a in xs)

    def step(state, xs_n):
        k_n, w_n, u_n, d_n = xs_n[:4]
        v_new = u_n - jnp.einsum("bhcd,bhdv->bhcv", w_n, state)
        new_state = state * d_n[..., None, None] + jnp.einsum("bhcd,bhcv->bhdv", k_n, v_new)
        if not with_output:
            return new_state, None
        q_n, a_n = xs_n[4:]
        o_n = jnp.einsum("bhcd,bhdv->bhcv", q_n, state) + jnp.einsum("bhij,bhjv->bhiv", a_n, v_new)
        return new_state, o_n

    state, o = lax.scan(step, s0, xs)
    if not with_output:
        return None, state
    o = jnp.moveaxis(o, 0, 2).reshape(B, H, T, dv)
    return jnp.moveaxis(o, 1, 2), state

def flip(a):
    return None if a is None else a[:, ::-1]

def gated_rms(o, z, g):
    B, T = z.shape[:2]
    zz = z.reshape(B, T, H_GDN, DV_GDN).astype(jnp.float32)
    return (rms_norm(o, g) * jax.nn.silu(zz)).reshape(B, T, GDN_WIDTH).astype(z.dtype)

def hybrid_mixer(h, hc, rope, w_in, q_norm_g, k_norm_g, attn_out_g, conv_qkv_w,
                 a_log_f, a_log_b, dt_bias_f, dt_bias_b, gdn_norm_g, w_out, with_ctx_out):
    B = h.shape[0]
    offs = np.cumsum(IN_SPLITS)[:-1].tolist()
    q_a, k_a, v_a, qkv_d, z_d, a_f, a_b, b_f, b_b = jnp.split(h @ w_in, offs, axis=-1)
    cq_a, ck_a, cv_a, cqkv_d, cz_d, ca_f, ca_b, cb_f, cb_b = jnp.split(hc @ w_in, offs, axis=-1)

    kc, vc = attn_kv(ck_a, cv_a, k_norm_g, None)
    kl, vl = attn_kv(k_a, v_a, k_norm_g, rope)
    ql = attn_q(q_a, q_norm_g, rope)
    o_attn = block_attention(ql, jnp.concatenate([kc, kl], axis=1), jnp.concatenate([vc, vl], axis=1))
    o_attn = rms_norm(o_attn.astype(h.dtype), attn_out_g)

    qd, kd, vd = gdn_inputs(qkv_d, conv_qkv_w, True)
    qdc, kdc, vdc = gdn_inputs(cqkv_d, conv_qkv_w, with_ctx_out)
    g_f, g_b = gdn_decay(a_f, a_log_f, dt_bias_f), gdn_decay(a_b, a_log_b, dt_bias_b)
    gc_f, gc_b = gdn_decay(ca_f, a_log_f, dt_bias_f), gdn_decay(ca_b, a_log_b, dt_bias_b)
    be_f, be_b = jax.nn.sigmoid(b_f.astype(jnp.float32)), jax.nn.sigmoid(b_b.astype(jnp.float32))
    bec_f, bec_b = jax.nn.sigmoid(cb_f.astype(jnp.float32)), jax.nn.sigmoid(cb_b.astype(jnp.float32))
    s0 = jnp.zeros((B, H_GDN, DK_GDN, DV_GDN), jnp.float32)
    oc_f, s_ctx_f = chunk_gated_delta(qdc, kdc, vdc, gc_f, bec_f, s0)
    oc_b, s_ctx_b = chunk_gated_delta(flip(qdc), flip(kdc), flip(vdc), flip(gc_b), flip(bec_b), s0)
    ol_f, _ = chunk_gated_delta(qd, kd, vd, g_f, be_f, s_ctx_f)
    ol_b, _ = chunk_gated_delta(flip(qd), flip(kd), flip(vd), flip(g_b), flip(be_b), s_ctx_b)
    o_gdn = gated_rms(ol_f + flip(ol_b), z_d, gdn_norm_g)

    lat_out = jnp.concatenate([o_attn, o_gdn], axis=-1) @ w_out
    if not with_ctx_out:
        return lat_out, None
    qc = attn_q(cq_a, q_norm_g, None)
    oc_attn = rms_norm(block_attention(qc, kc, vc).astype(hc.dtype), attn_out_g)
    oc_gdn = gated_rms(oc_f + flip(oc_b), cz_d, gdn_norm_g)
    ctx_out = jnp.concatenate([oc_attn, oc_gdn], axis=-1) @ w_out
    return lat_out, ctx_out

def conv_ffn(h, w_up, conv_w, conv_b, w_down):
    u = depthwise_conv(h @ w_up, conv_w) + conv_b
    gate, val = jnp.split(u, 2, axis=-1)
    return (jax.nn.silu(gate) * val) @ w_down

def first_inputs(seed: int = 0) -> dict:
    key = jax.random.key(seed)
    ks = jax.random.split(key, 24)
    f32 = jnp.float32
    L = DEPTH

    def normal(k, shape, scale):
        return scale * jax.random.normal(k, shape, f32)

    def gain(k, shape):
        return 1.0 + 0.05 * jax.random.normal(k, shape, f32)

    a_log = jnp.log(jax.random.uniform(ks[12], (2, L, H_GDN), f32, 1.0, 16.0))
    dt = jnp.exp(jax.random.uniform(ks[13], (2, L, H_GDN), f32, float(np.log(1e-3)), float(np.log(1e-1))))
    dt_bias = dt + jnp.log(-jnp.expm1(-dt))
    return {
        "x": normal(ks[0], (BATCH, SEQ, D_MODEL), 1.0),
        "c": normal(ks[1], (BATCH, D_MODEL), 1.0),
        "ctx": normal(ks[2], (BATCH, CTX_LEN, D_MODEL), 1.0),
        "c_ctx": normal(ks[3], (D_MODEL,), 1.0),
        "w_mod": normal(ks[4], (L, D_MODEL, N_MOD * D_MODEL), 0.5 * D_MODEL ** -0.5),
        "b_mod": normal(ks[5], (L, N_MOD * D_MODEL), 0.02),
        "norm1_g": gain(ks[6], (L, D_MODEL)),
        "w_in": normal(ks[7], (L, D_MODEL, IN_WIDTH), D_MODEL ** -0.5),
        "q_norm_g": gain(ks[8], (L, HD_ATTN)),
        "k_norm_g": gain(ks[9], (L, HD_ATTN)),
        "attn_out_g": gain(ks[10], (L, ATTN_WIDTH)),
        "conv_qkv_w": normal(ks[11], (L, SHORT_CONV, GDN_QKV_WIDTH), SHORT_CONV ** -0.5),
        "a_log_f": a_log[0],
        "a_log_b": a_log[1],
        "dt_bias_f": dt_bias[0],
        "dt_bias_b": dt_bias[1],
        "gdn_norm_g": gain(ks[14], (L, DV_GDN)),
        "w_out": normal(ks[15], (L, MIX_WIDTH, D_MODEL), MIX_WIDTH ** -0.5),
        "norm2_g": gain(ks[16], (L, D_MODEL)),
        "w_up": normal(ks[17], (L, D_MODEL, 2 * D_FF), D_MODEL ** -0.5),
        "ffn_conv_w": normal(ks[18], (L, FFN_CONV, 2 * D_FF), FFN_CONV ** -0.5),
        "ffn_conv_b": normal(ks[19], (L, 2 * D_FF), 0.02),
        "w_down": normal(ks[20], (L, D_FF, D_MODEL), D_FF ** -0.5),
        "final_norm_g": gain(ks[21], (D_MODEL,)),
    }

def first_block(x, c, ctx, c_ctx, w_mod, b_mod, norm1_g, w_in, q_norm_g, k_norm_g, attn_out_g,
              conv_qkv_w, a_log_f, a_log_b, dt_bias_f, dt_bias_b, gdn_norm_g, w_out, norm2_g,
              w_up, ffn_conv_w, ffn_conv_b, w_down, final_norm_g):
    rope = axial_rope_tables(x.shape[1])
    xc = ctx
    for l in range(DEPTH):
        last = l == DEPTH - 1
        sh1, sc1, g1, sh2, sc2, g2 = ada_terms(c, w_mod[l], b_mod[l])
        cmod = ada_terms(c_ctx, w_mod[l], b_mod[l])
        h = modulate(x, norm1_g[l], sh1, sc1)
        hc = modulate(xc, norm1_g[l], cmod[0], cmod[1])
        lat_out, ctx_out = hybrid_mixer(
            h, hc, rope, w_in[l], q_norm_g[l], k_norm_g[l], attn_out_g[l], conv_qkv_w[l],
            a_log_f[l], a_log_b[l], dt_bias_f[l], dt_bias_b[l], gdn_norm_g[l], w_out[l],
            not last)
        x = x + g1 * lat_out
        x = x + g2 * conv_ffn(modulate(x, norm2_g[l], sh2, sc2), w_up[l], ffn_conv_w[l],
                              ffn_conv_b[l], w_down[l])
        if not last:
            xc = xc + cmod[2] * ctx_out
            xc = xc + cmod[5] * conv_ffn(modulate(xc, norm2_g[l], cmod[3], cmod[4]), w_up[l],
                                         ffn_conv_w[l], ffn_conv_b[l], w_down[l])
    return rms_norm(x, final_norm_g)


DEPTH_2 = 2

ATT_HEADS = 8
ATT_HEAD_DIM = 64
ATT_WIDTH = ATT_HEADS * ATT_HEAD_DIM
MOBA_BLOCK = 256
MOBA_TOPK = 3
MOBA_Q_CHUNK = 32
RET_HEADS = 4
RET_HEAD_DIM = 128
RET_WIDTH = RET_HEADS * RET_HEAD_DIM
RET_CHUNK = 128
ROPE_BASE = 10000.0
IN_PROJ_WIDTH = 3 * ATT_WIDTH + 4 * RET_WIDTH
N_EXPERTS = 8
TOP_K = 2
EXPERT_D_FF = 2816
MOE_GROUP = 128


def rms_norm_2(x, g):
    xf = x.astype(jnp.float32)
    y = xf * lax.rsqrt(jnp.mean(xf * xf, axis=-1, keepdims=True) + EPS)
    return (y * g.astype(jnp.float32)).astype(x.dtype)

def rotary(x):
    s, d = x.shape[1], x.shape[-1]
    half = d // 2
    inv_freq = ROPE_BASE ** (-jnp.arange(half, dtype=jnp.float32) / half)
    ang = jnp.arange(s, dtype=jnp.float32)[:, None] * inv_freq[None, :]
    cos = jnp.cos(ang)[None, :, None, :]
    sin = jnp.sin(ang)[None, :, None, :]
    xf = x.astype(jnp.float32)
    x1, x2 = xf[..., :half], xf[..., half:]
    return jnp.concatenate([x1 * cos - x2 * sin, x1 * sin + x2 * cos], axis=-1).astype(x.dtype)

def moba_attention(q, k, v):
    b, h, s, dh = q.shape
    nb = -(-s // MOBA_BLOCK)
    pad = nb * MOBA_BLOCK - s
    kp = jnp.pad(k, ((0, 0), (0, 0), (0, pad), (0, 0)))
    vp = jnp.pad(v, ((0, 0), (0, 0), (0, pad), (0, 0)))
    kb = kp.reshape(b, h, nb, MOBA_BLOCK, dh)
    vb = vp.reshape(b, h, nb, MOBA_BLOCK, dh)
    scale = dh ** -0.5
    n_sel = min(MOBA_TOPK, nb - 1)
    q_block = jnp.arange(s) // MOBA_BLOCK
    if n_sel > 0:
        k_mean = jnp.mean(kb.astype(jnp.float32), axis=3)
        gate = jnp.einsum('bhsd,bhnd->bhsn', q.astype(jnp.float32), k_mean)
        past = jnp.arange(nb)[None, :] < q_block[:, None]
        gate = jnp.where(past[None, None], gate, -1e30)
        _, sel = lax.top_k(gate, n_sel)
        sel_valid = sel < q_block[None, None, :, None]
    bi = jnp.arange(b)[:, None, None, None]
    hi = jnp.arange(h)[None, :, None, None]

    def chunk_fn(ci):
        start = ci * MOBA_Q_CHUNK
        qc = lax.dynamic_slice_in_dim(q, start, MOBA_Q_CHUNK, axis=2)
        pos = start + jnp.arange(MOBA_Q_CHUNK)
        own = start // MOBA_BLOCK
        k_own = lax.dynamic_index_in_dim(kb, own, axis=2, keepdims=False)
        v_own = lax.dynamic_index_in_dim(vb, own, axis=2, keepdims=False)
        key_pos = own * MOBA_BLOCK + jnp.arange(MOBA_BLOCK)
        s_own = jnp.einsum('bhqd,bhkd->bhqk', qc, k_own).astype(jnp.float32) * scale
        s_own = jnp.where(key_pos[None, :] <= pos[:, None], s_own, -jnp.inf)
        if n_sel > 0:
            sel_c = lax.dynamic_slice_in_dim(sel, start, MOBA_Q_CHUNK, axis=2)
            val_c = lax.dynamic_slice_in_dim(sel_valid, start, MOBA_Q_CHUNK, axis=2)
            k_sel = kb[bi, hi, sel_c]
            v_sel = vb[bi, hi, sel_c]
            s_sel = jnp.einsum('bhqd,bhqnkd->bhqnk', qc, k_sel).astype(jnp.float32) * scale
            s_sel = jnp.where(val_c[..., None], s_sel, -jnp.inf)
            s_sel = s_sel.reshape(b, h, MOBA_Q_CHUNK, n_sel * MOBA_BLOCK)
            p = jax.nn.softmax(jnp.concatenate([s_own, s_sel], axis=-1), axis=-1)
            p_own = p[..., :MOBA_BLOCK].astype(v.dtype)
            p_sel = p[..., MOBA_BLOCK:].reshape(b, h, MOBA_Q_CHUNK, n_sel, MOBA_BLOCK).astype(v.dtype)
            o = (jnp.einsum('bhqk,bhkd->bhqd', p_own, v_own)
                 + jnp.einsum('bhqnk,bhqnkd->bhqd', p_sel, v_sel))
        else:
            p_own = jax.nn.softmax(s_own, axis=-1).astype(v.dtype)
            o = jnp.einsum('bhqk,bhkd->bhqd', p_own, v_own)
        return o

    out = lax.map(chunk_fn, jnp.arange(s // MOBA_Q_CHUNK))
    return jnp.transpose(out, (1, 2, 0, 3, 4)).reshape(b, h, s, dh)

def retention(q, k, v):
    b, h, s, d = q.shape
    c = RET_CHUNK
    nc = s // c
    dt = v.dtype
    lg = jnp.log(1.0 - 2.0 ** (-5.0 - jnp.arange(h, dtype=jnp.float32)))
    idx = jnp.arange(c, dtype=jnp.float32)
    qf = q.astype(jnp.float32).reshape(b, h, nc, c, d)
    kf = (k.astype(jnp.float32) * d ** -0.5).reshape(b, h, nc, c, d)
    vf = v.astype(jnp.float32).reshape(b, h, nc, c, d)
    diff = idx[:, None] - idx[None, :]
    dmask = jnp.where(diff >= 0, jnp.exp(jnp.maximum(diff, 0.0)[None] * lg[:, None, None]), 0.0)
    scores = jnp.einsum('bhncd,bhnmd->bhncm', qf, kf) * dmask[None, :, None]
    inner = jnp.einsum('bhncm,bhnme->bhnce', scores, vf)
    k_dec = kf * jnp.exp((c - 1 - idx)[None, :] * lg[:, None])[None, :, None, :, None]
    kv = jnp.einsum('bhnmd,bhnme->bhnde', k_dec, vf)
    chunk_decay = jnp.exp(c * lg)[None, :, None, None]

    def step(state, kv_n):
        return state * chunk_decay + kv_n, state

    _, r_prev = lax.scan(step, jnp.zeros((b, h, d, d), jnp.float32), jnp.moveaxis(kv, 2, 0))
    r_prev = jnp.moveaxis(r_prev, 0, 2)
    q_dec = qf * jnp.exp((idx + 1.0)[None, :] * lg[:, None])[None, :, None, :, None]
    cross = jnp.einsum('bhncd,bhnde->bhnce', q_dec, r_prev)
    return (inner + cross).reshape(b, h, s, d).astype(dt)

def hybrid_mixer_2(h, w_in, w_out, att_out_g, ret_out_g):
    b, s, _ = h.shape
    proj = h @ w_in
    A, R = ATT_WIDTH, RET_WIDTH
    q_a, k_a, v_a, q_r, k_r, v_r, g_r = jnp.split(
        proj, [A, 2 * A, 3 * A, 3 * A + R, 3 * A + 2 * R, 3 * A + 3 * R], axis=-1)

    def att_heads(t):
        return t.reshape(b, s, ATT_HEADS, ATT_HEAD_DIM).transpose(0, 2, 1, 3)

    o_a = moba_attention(att_heads(q_a), att_heads(k_a), att_heads(v_a))
    o_a = o_a.transpose(0, 2, 1, 3).reshape(b, s, A)
    o_a = rms_norm_2(o_a, att_out_g)

    def ret_heads(t):
        return t.reshape(b, s, RET_HEADS, RET_HEAD_DIM)

    qr = rotary(ret_heads(q_r)).transpose(0, 2, 1, 3)
    kr = rotary(ret_heads(k_r)).transpose(0, 2, 1, 3)
    vr = ret_heads(v_r).transpose(0, 2, 1, 3)
    o_r = retention(qr, kr, vr).transpose(0, 2, 1, 3)
    o_r = rms_norm_2(o_r, ret_out_g.reshape(RET_HEADS, RET_HEAD_DIM)).reshape(b, s, R)
    o_r = jax.nn.silu(g_r) * o_r
    return jnp.concatenate([o_a, o_r], axis=-1) @ w_out

def swiglu(x, w_gate, w_up, w_down):
    return (jax.nn.silu(x @ w_gate) * (x @ w_up)) @ w_down

def moe_ffn(h, w_router, w_gate, w_up, w_down):
    b, s, d = h.shape
    xf = h.reshape(-1, d)
    n = xf.shape[0]
    e_count = w_gate.shape[0]
    g = MOE_GROUP
    logits = (xf @ w_router).astype(jnp.float32)
    top_logits, top_idx = lax.top_k(logits, TOP_K)
    top_w = jax.nn.softmax(top_logits, axis=-1)
    a = n * TOP_K
    e_flat = top_idx.reshape(-1)
    t_flat = jnp.repeat(jnp.arange(n, dtype=jnp.int32), TOP_K)
    w_flat = top_w.reshape(-1)
    order = jnp.argsort(e_flat, stable=True)
    e_sorted = e_flat[order]
    counts = jnp.bincount(e_flat, length=e_count)
    starts = jnp.cumsum(counts) - counts
    padded = (counts + g - 1) // g * g
    pad_ends = jnp.cumsum(padded)
    pad_starts = pad_ends - padded
    dest = pad_starts[e_sorted] + (jnp.arange(a) - starts[e_sorted])
    p_total = (-(-a // g) + e_count) * g
    tok_buf = jnp.full((p_total,), n, jnp.int32).at[dest].set(t_flat[order])
    w_buf = jnp.zeros((p_total,), jnp.float32).at[dest].set(w_flat[order])
    nblk = p_total // g
    blk_e = jnp.minimum(jnp.searchsorted(pad_ends, jnp.arange(nblk) * g, side='right'), e_count - 1)
    x_pad = jnp.concatenate([xf, jnp.zeros((1, d), xf.dtype)], axis=0)
    xb = x_pad[tok_buf].reshape(nblk, g, d)

    def expert_block(args):
        xg, e = args
        return swiglu(xg, w_gate[e], w_up[e], w_down[e])

    yb = lax.map(expert_block, (xb, blk_e)).reshape(p_total, d)
    yb = yb * w_buf[:, None].astype(yb.dtype)
    y = jax.ops.segment_sum(yb, tok_buf, num_segments=n + 1)[:n]
    return y.reshape(b, s, d)

def second_inputs(seed: int = 0) -> dict:
    key = jax.random.key(seed)
    ks = jax.random.split(key, 20)
    n_dense = (DEPTH_2 + 1) // 2
    n_moe = DEPTH_2 // 2
    D = D_MODEL

    def nrm(k, shape, scale):
        return jax.random.normal(k, shape, jnp.float32) * scale

    return {
        "x": nrm(ks[0], (BATCH, SEQ, D), 1.0),
        "c": nrm(ks[1], (BATCH, D), 1.0),
        "norm_mix_g": 1.0 + nrm(ks[2], (DEPTH_2, D), 0.05),
        "norm_ffn_g": 1.0 + nrm(ks[3], (DEPTH_2, D), 0.05),
        "ada_w": nrm(ks[4], (DEPTH_2, D, 6 * D), 0.5 * D ** -0.5),
        "ada_b": nrm(ks[5], (DEPTH_2, 6 * D), 0.02),
        "w_in": nrm(ks[6], (DEPTH_2, D, IN_PROJ_WIDTH), D ** -0.5),
        "w_out": nrm(ks[7], (DEPTH_2, ATT_WIDTH + RET_WIDTH, D), (ATT_WIDTH + RET_WIDTH) ** -0.5),
        "att_out_g": 1.0 + nrm(ks[8], (DEPTH_2, ATT_WIDTH), 0.05),
        "ret_out_g": 1.0 + nrm(ks[9], (DEPTH_2, RET_WIDTH), 0.05),
        "ffn_w_gate": nrm(ks[10], (n_dense, D, D_FF), D ** -0.5),
        "ffn_w_up": nrm(ks[11], (n_dense, D, D_FF), D ** -0.5),
        "ffn_w_down": nrm(ks[12], (n_dense, D_FF, D), D_FF ** -0.5),
        "router_w": nrm(ks[13], (n_moe, D, N_EXPERTS), D ** -0.5),
        "moe_w_gate": nrm(ks[14], (n_moe, N_EXPERTS, D, EXPERT_D_FF), D ** -0.5),
        "moe_w_up": nrm(ks[15], (n_moe, N_EXPERTS, D, EXPERT_D_FF), D ** -0.5),
        "moe_w_down": nrm(ks[16], (n_moe, N_EXPERTS, EXPERT_D_FF, D), EXPERT_D_FF ** -0.5),
        "final_norm_g": 1.0 + nrm(ks[17], (D,), 0.05),
    }

def second_block(x, c, norm_mix_g, norm_ffn_g, ada_w, ada_b, w_in, w_out, att_out_g, ret_out_g,
              ffn_w_gate, ffn_w_up, ffn_w_down, router_w, moe_w_gate, moe_w_up, moe_w_down,
              final_norm_g):
    cs = jax.nn.silu(c)
    for l in range(DEPTH_2):
        mod = cs @ ada_w[l] + ada_b[l]
        sh1, sc1, g1, sh2, sc2, g2 = jnp.split(mod, 6, axis=-1)
        h = rms_norm_2(x, norm_mix_g[l]) * (1.0 + sc1[:, None]) + sh1[:, None]
        x = x + g1[:, None] * hybrid_mixer_2(h, w_in[l], w_out[l], att_out_g[l], ret_out_g[l])
        h = rms_norm_2(x, norm_ffn_g[l]) * (1.0 + sc2[:, None]) + sh2[:, None]
        if l % 2 == 0:
            f = swiglu(h, ffn_w_gate[l // 2], ffn_w_up[l // 2], ffn_w_down[l // 2])
        else:
            f = moe_ffn(h, router_w[l // 2], moe_w_gate[l // 2], moe_w_up[l // 2], moe_w_down[l // 2])
        x = x + g2[:, None] * f
    return rms_norm_2(x, final_norm_g)


def setup_inputs(seed=0):
    out = dict(first_inputs(seed))
    for name, value in second_inputs(seed + 1).items():
        if name != "x":
            out[name + "_2"] = value
    return out


def reference(
    x, c, ctx, c_ctx, w_mod, b_mod, norm1_g, w_in, q_norm_g, k_norm_g, attn_out_g, conv_qkv_w,
    a_log_f, a_log_b, dt_bias_f, dt_bias_b, gdn_norm_g, w_out, norm2_g, w_up, ffn_conv_w,
    ffn_conv_b, w_down, final_norm_g, c_2, norm_mix_g_2, norm_ffn_g_2, ada_w_2, ada_b_2, w_in_2,
    w_out_2, att_out_g_2, ret_out_g_2, ffn_w_gate_2, ffn_w_up_2, ffn_w_down_2, router_w_2,
    moe_w_gate_2, moe_w_up_2, moe_w_down_2, final_norm_g_2,
):
    x = first_block(
        x, c, ctx, c_ctx, w_mod, b_mod, norm1_g, w_in, q_norm_g, k_norm_g, attn_out_g,
        conv_qkv_w, a_log_f, a_log_b, dt_bias_f, dt_bias_b, gdn_norm_g, w_out, norm2_g, w_up,
        ffn_conv_w, ffn_conv_b, w_down, final_norm_g,
    )
    return second_block(
        x, c_2, norm_mix_g_2, norm_ffn_g_2, ada_w_2, ada_b_2, w_in_2, w_out_2, att_out_g_2,
        ret_out_g_2, ffn_w_gate_2, ffn_w_up_2, ffn_w_down_2, router_w_2, moe_w_gate_2,
        moe_w_up_2, moe_w_down_2, final_norm_g_2,
    )


_drawn_inputs = setup_inputs


def setup_inputs(seed=0):
    import zlib

    import numpy as np

    out = dict(_drawn_inputs(seed))
    spreads = {}
    factors = {'norm1_g': 3.181,
     'q_norm_g': 8.0,
     'k_norm_g': 6.398,
     'attn_out_g': 2.716,
     'gdn_norm_g': 4.358,
     'norm2_g': 2.714,
     'ffn_conv_b': 6.168,
     'att_out_g_2': 2.773,
     'ret_out_g_2': 4.119,
     'norm_ffn_g_2': 2.72}
    for name, (base, spread) in spreads.items():
        noise = np.random.default_rng([zlib.crc32(name.encode()), seed]).standard_normal(out[name].shape)
        drawn = base * np.exp(spread * noise) if base else spread * noise
        out[name] = jnp.asarray(drawn.astype(out[name].dtype))
    for name, factor in factors.items():
        out[name] = (out[name] * factor).astype(out[name].dtype)
    return out
```

```python
from contextlib import ExitStack

import numpy as np

import concourse.bass as bass
from concourse import mybir

ALU = mybir.AluOpType
ACT = mybir.ActivationFunctionType
F32 = mybir.dt.float32
I32 = mybir.dt.int32
U32 = mybir.dt.uint32
AX_X = mybir.AxisListType.X

P = 128
D = 1024
KT = D // P
T = 256
TT = T // P
EPS = 1e-6
NEG = -1e30

HD = 64
GH = 4
MIX_T = 4
GRID_W = 64
FF = 2816
UW = 256
FC = FF // UW
FT = FF // P
NE = 8
RING = 11
NARROW = 128

C_ALL = dict(ident=0, ones=128, ustrict=256, iota=384)
C_ALL_W = 640
C_ONE = dict(ones64=0, rot64=128, sel=256, u_fwd=512, u_bwd=640, strict_fwd=768, strict_bwd=896,
             incl_fwd=1024, incl_bwd=1152, level=1280, cos=2176, sin=2432)
C_ONE_W = 2688
C_TWO = dict(rot128=0, cos=128, sin=384, ret=640, causal=2176)
C_TWO_W = 2304

V_C, V_CCTX, V_BMOD, V_N1, V_ATTG, V_GDNG, V_N2, V_CONV, V_QG, V_KG = 0, 8, 16, 64, 72, 76, 77, 85, 121, 122
V0_ROWS = 123
V_FW01, V_C2, V_NMIX, V_NFFN = 0, 88, 96, 112
V1_ROWS = 128
V_FW2, V_FB, V_FIN1, V_FIN2 = 0, 44, 88, 96
V2_ROWS = 104
V_BADA, V_ATTG2, V_RETG = 0, 96, 104
V3_ROWS = 112


def shape_constants():
    i = np.arange(P)
    row, col = i[:, None], i[None, :]
    f = np.float32
    allc = np.zeros((P, C_ALL_W), f)
    allc[:, 0:128] = np.eye(P)
    allc[:, 128:256] = 1.0
    allc[:, 256:384] = row < col
    allc[:, 384:640] = np.arange(256)[None, :]

    def rotation(hd):
        r = np.zeros((P, P), f)
        for m in range(P):
            if m % hd < hd // 2:
                r[m + hd // 2, m] = -1.0
            else:
                r[m - hd // 2, m] = 1.0
        return r

    one = np.zeros((P, C_ONE_W), f)
    c = C_ONE
    one[:, c["ones64"]:c["ones64"] + P] = (row // HD) == (col // HD)
    one[:, c["rot64"]:c["rot64"] + P] = rotation(HD)
    for kv in range(2):
        one[:, c["sel"] + kv * P:c["sel"] + (kv + 1) * P] = row == (HD * kv + col % HD)
    one[:, c["u_fwd"]:c["u_fwd"] + P] = row <= col
    one[:, c["u_bwd"]:c["u_bwd"] + P] = row >= col
    one[:, c["strict_fwd"]:c["strict_fwd"] + P] = np.where(row > col, 0, NEG)
    one[:, c["strict_bwd"]:c["strict_bwd"] + P] = np.where(row < col, 0, NEG)
    one[:, c["incl_fwd"]:c["incl_fwd"] + P] = np.where(row <= col, 0, NEG)
    one[:, c["incl_bwd"]:c["incl_bwd"] + P] = np.where(row >= col, 0, NEG)
    for lv in range(7):
        s = 1 << lv
        pair = (row // (2 * s) == col // (2 * s)) & (row // s != col // s)
        one[:, c["level"] + lv * P:c["level"] + (lv + 1) * P] = pair * (-1.0 if lv == 0 else 1.0)
    t = np.arange(T)
    quarter = HD // 4
    inv = 10000.0 ** (-np.arange(quarter, dtype=f) / f(quarter))
    inv = inv.astype(f)
    ang = np.concatenate([(t // GRID_W).astype(f)[:, None] * inv, (t % GRID_W).astype(f)[:, None] * inv], 1)
    lane = (i % HD) % (HD // 2)
    one[:, c["cos"]:c["cos"] + T] = np.cos(ang).T[lane]
    one[:, c["sin"]:c["sin"] + T] = np.sin(ang).T[lane]

    two = np.zeros((P, C_TWO_W), f)
    c = C_TWO
    two[:, 0:P] = rotation(P)
    half = P // 2
    inv = (10000.0 ** (-np.arange(half, dtype=f) / f(half))).astype(f)
    ang = t.astype(f)[:, None] * inv[None, :]
    two[:, c["cos"]:c["cos"] + T] = np.cos(ang).T[i % half]
    two[:, c["sin"]:c["sin"] + T] = np.sin(ang).T[i % half]
    for h in range(GH):
        lg = np.log(1.0 - 2.0 ** (-5.0 - h))
        for b, (j0, i0, n) in enumerate(((0, 0, 256), (128, 128, 128))):
            dist = (i0 + np.arange(n))[None, :] - (j0 + i)[:, None]
            m = np.where(dist >= 0, np.exp(np.maximum(dist, 0) * lg), 0.0) * P ** -0.5
            at = c["ret"] + h * 384 + b * 256
            two[:, at:at + n] = m
    two[:, c["causal"]:c["causal"] + P] = np.where(col <= row, 0, NEG)
    return np.concatenate([allc, one, two], 1)


class BankRing:

    def __init__(self, banks, full, free):
        self.banks, self.sem_full, self.sem_free = banks, full, free
        self.taken = 0
        self.uses = [0] * len(banks)
        self.frees = [0] * len(banks)
        self.where = {}

    def take(self, pe, name, readers=1):
        b = self.taken % len(self.banks)
        if self.frees[b]:
            pe.wait_ge(self.sem_free[b], self.frees[b])
        self.taken += 1
        self.uses[b] += 1
        self.frees[b] += readers
        self.where[name] = (b, self.uses[b], self.frees[b])
        return self.banks[b]

    def done(self, name, ins):
        ins.then_inc(self.sem_full[self.where[name][0]], 1)

    def full(self, eng, name):
        b, n, _ = self.where[name]
        eng.wait_ge(self.sem_full[b], n)
        return self.banks[b]

    def free(self, name, ins):
        ins.then_inc(self.sem_free[self.where[name][0]], 1)

    def moved(self, eng, name, but=0):
        b, _, n = self.where[name]
        eng.wait_ge(self.sem_free[b], n - but)

    def all_free(self, pe):
        for b, n in enumerate(self.frees):
            if n:
                pe.wait_ge(self.sem_free[b], n)


def build(nc, t, out):
    ctx = ExitStack()
    with ctx:
        def sb(name, shape, dt=F32):
            return ctx.enter_context(nc.sbuf_tensor(name, shape, dt))

        def sem(name):
            return ctx.enter_context(nc.semaphore(name))

        banks = [ctx.enter_context(nc.psum_tensor(f"bank{b}", [P, 512], F32)) for b in range(8)]

        ring = sb("ring", [P, RING, KT * UW])
        con = sb("con", [P, C_ALL_W])
        con2 = sb("con2", [P, C_ONE_W])
        vec = sb("vec", [P, 4, P])
        xT = sb("xT", [P, KT, T])[:, :, :]
        sq = sb("sq", [P, 2048])
        rstd = sb("rstd", [P, T])
        hroot = sb("hroot", [P, 2, 512])
        m1 = sb("m1", [P, 48, 2])
        m2 = sb("m2", [P, 2, 48])
        amul = sb("amul", [P, 7, 8])
        cs = sb("cs", [P, 8, 2])
        cs2 = sb("cs2", [P, 8])
        wab = sb("wab", [P, KT, 16])
        wrt = sb("wrt", [P, KT, NE])
        gconst = sb("gconst", [P, 2, 8])
        gates = sb("gates", [P, 12, 32])
        stat = sb("stat", [P, 4, 4])
        ARENA = 24064
        arena = sb("arena", [P, ARENA])

        def at(a, *shape):
            n = int(np.prod(shape))
            assert a + n <= ARENA, (a, n)
            v = arena[:, a:a + n]
            if len(shape) == 2:
                return v.rearrange("p (a b) -> p a b", a=shape[0])
            if len(shape) == 3:
                return v.rearrange("p (a b c) -> p a b c", a=shape[0], b=shape[1])
            return v

        def c_all(name, w=P):
            return con[:, C_ALL[name]:C_ALL[name] + w]

        def c_one(name, w=P, i=0):
            a = C_ONE[name] + i * P
            return con2[:, a:a + w]

        def c_two(name, w=P, i=0):
            a = C_TWO[name] + i
            return con2[:, a:a + w]

        ident, ones = c_all("ident"), c_all("ones")

        def over(ap, n):
            w = ap.shape[-1]
            return ap.rearrange("p (a w) -> p a w", a=1).to_broadcast([ap.shape[0], n, w])

        mixT = at(0, 8, T)
        zs = at(2048, 4, T)
        qF = at(3072, 4, T)
        kF = at(4096, 4, 512)
        k_tm = at(6144, 4, 4, P)
        v_tm = at(8192, 4, 4, P)
        G0 = 10240
        hT = at(G0, KT, 512)
        xraw = at(G0 + 4096, 4, D)
        ctxT = at(G0 + 8192, KT, T)
        ybuf = at(G0 + 10240, 4, 512)
        qA = at(G0 + 12288, 4, T)
        kA = at(G0 + 13312, 512)
        vA = at(G0 + 6656, 4, P)
        kdup = at(G0 + 0, 2, 512)
        prob = at(G0 + 1024, 3, 512)
        probT = at(G0 + 2560, 2, 512)
        oA = at(G0 + 4096, 4, T)
        atmp = at(G0 + 5120, 2, 512)
        kroot = at(G0 + 6144, 512)
        Tm = at(G0 + 0, 2, 512)
        TTm = at(G0 + 1024, 2, 512)
        LTm = at(G0 + 2048, 2, 512)
        M1 = at(G0 + 3072, 2, 512)
        LsT = at(G0 + 4096, 4, 512)
        kbe = at(G0 + 6144, 2, 512)
        kdec = at(G0 + 7168, 2, 512)
        nwT = at(G0 + 8192, 2, 512)
        vnew = at(G0 + 9216, 2, 512)
        ATm = at(G0 + 10240, 2, 512)
        qdec = at(G0 + 11264, 2, 512)
        S = at(G0 + 12288, 2, 512)
        oG = mixT[:, 4:8, :]
        dec = sq[:, 0:1024].rearrange("p (a b) -> p a b", a=2)
        egb = sq[:, 1024:2048].rearrange("p (a b) -> p a b", a=2)
        hF = at(0, KT, T)
        gT = at(2048, 4, T)
        yc = at(3072, 3, 512)
        h2 = at(0, KT, T)
        mix2 = at(2048, 8, T)
        qA2 = at(4096, 4, T)
        kA2 = at(5120, 4, T)
        vA2 = at(6144, 2, 512)
        qR = at(7168, 4, T)
        kR = at(8192, 4, T)
        vR = at(9216, 2, 512)
        sgr = at(10240, 4, T)
        prob2 = at(11264, 3, 512)
        probT2 = at(12800, 2, 512)
        oA2 = at(13824, 4, T)
        rtmp = at(14848, 2, 512)
        AR = at(15872, 2, 512)
        oR = at(16896, 4, T)
        Pg = at(2048, 2, NE, 256)
        PwT = at(6144, 2, NE, 256)
        h_tm = at(10240, 2, D)
        xg = at(12288, KT, 256)
        ye = at(14336, 2, D)
        facc = at(16384, KT, T)
        gTe = at(18432, 4, 256)
        sge = at(19456, 2, 256)
        Pw = at(19968, 2, 512)
        rout = at(20992, 24, 8)
        cnt_i = sb("cnt_i", [P, 8], I32)
        idx_u = sb("idx_u", [P, 2, 8], U32)
        outT = at(20992 + 192, 2, D)

        full = [sem(f"full{b}") for b in range(8)]
        free = [sem(f"free{b}") for b in range(8)]
        landed = [sem(f"landed{s}") for s in range(RING)]
        unit_used = sem("unit_used")
        x_landed, v_landed = sem("x_landed"), sem("v_landed")
        con_landed, con1_landed, con2_landed = sem("con_landed"), sem("con1_landed"), sem("con2_landed")
        gc_landed, wab_landed, wrt_landed = sem("gc_landed"), sem("wab_landed"), sem("wrt_landed")
        out_landed = sem("out_landed")
        dve_step, act_step, pool_step = sem("dve_step"), sem("act_step"), sem("pool_step")
        cs_ready, sq_ready, root_ready, norm_out = sem("cs_ready"), sem("sq_ready"), sem("root_ready"), sem("norm_out")
        x_updated = sem("x_updated")
        centre_ready, d_ready = sem("centre_ready"), sem("d_ready")
        sqd_ready, l2_ready = sem("sqd_ready"), sem("l2_ready")
        ansq, qk_normed, rope_done = sem("ansq"), sem("qk_normed"), sem("rope_done")
        max_ready, exp_done, prob_ready = sem("max_ready"), sem("exp_done"), sem("prob_ready")
        sp_abs, sp_ln, g_ready, tmg_ready, gate_ready, ngl_ready = (
            sem("sp_abs"), sem("sp_ln"), sem("g_ready"), sem("tmg_ready"), sem("gate_ready"), sem("ngl_ready"))
        dec_ready, att_ready, kb_ready, seed_ready, ls_ready, ttb_ready, qdec_ready = (
            sem("dec_ready"), sem("att_ready"), sem("kb_ready"), sem("seed_ready"), sem("ls_ready"),
            sem("ttb_ready"), sem("qdec_ready"))
        hn_sq, hn_out = sem("hn_sq"), sem("hn_out")
        silu_ready, gT_ready = sem("silu_ready"), sem("gT_ready")
        rrope = sem("rrope")
        top_ready, wt_ready, sel_ready, pw_ready = sem("top_ready"), sem("wt_ready"), sem("sel_ready"), sem("pw_ready")
        xj_full, moved, gu_full, gated = sem("xj_full"), sem("moved"), sem("gu_full"), sem("gated")
        sge_ready, ye_ready = sem("sge_ready"), sem("ye_ready")
        out_ready = sem("out_ready")
        fin_ready = sem("fin_ready")

        A = BankRing(banks[0:4], full[0:4], free[0:4])
        B = BankRing(banks[4:7], full[4:7], free[4:7])
        C = BankRing(banks[7:8], full[7:8], free[7:8])

        w_cols = lambda w, u: w[:, u * UW:(u + 1) * UW].rearrange("(k p) n -> p k n", p=P)
        w_rows = lambda w, c: w[c * UW:(c + 1) * UW, :].rearrange("(k p) n -> p k n", p=P)
        units = []

        def add(name, ap):
            units.append((name, ap))

        def add_ffn(tag, gate, up, down):
            for c in range(FC + 1):
                if c < FC:
                    add((tag, "g", c), gate(c))
                    add((tag, "u", c), up(c))
                if c >= 1:
                    add((tag, "d", c - 1), down(c - 1))

        for u in range(8):
            add(("mod", 0, u), w_cols(t["w_mod"][0], u))
        for u in range(11):
            add(("in1", u), w_cols(t["w_in"][0], u))
        FILL = [(0, u) for u in range(8, 24)] + [(1, u) for u in range(24)] + [(2, u) for u in range(24)]
        for part, u in FILL:
            w = t["w_mod"][0] if part == 0 else t["ada_w_2"][part - 1]
            add(("mod", part, u), w_cols(w, u))
        for u in range(4):
            add(("out1", u), w_cols(t["w_out"][0], u))
        add_ffn("ffn1", lambda c: w_cols(t["w_up"][0], c), lambda c: w_cols(t["w_up"][0], FC + c),
                lambda c: w_rows(t["w_down"][0], c))
        for l in range(2):
            for u in range(14):
                add(("in2", l, u), w_cols(t["w_in_2"][l], u))
            for u in range(4):
                add(("out2", l, u), w_cols(t["w_out_2"][l], u))
            if l == 0:
                add_ffn("ffn2", lambda c: w_cols(t["ffn_w_gate_2"][0], c), lambda c: w_cols(t["ffn_w_up_2"][0], c),
                        lambda c: w_rows(t["ffn_w_down_2"][0], c))
        U0 = len(units)
        order = {name: k for k, (name, _) in enumerate(units)}
        EU = 3 * FC
        e_order = {}
        for c in range(FC + 1):
            if c < FC:
                e_order["g", c] = len(e_order)
                e_order["u", c] = len(e_order)
            if c >= 1:
                e_order["d", c - 1] = len(e_order)

        fills = {}
        left = list(FILL)
        for u in range(16):
            fills["att", u] = [left.pop(0)]
        for s in range(4):
            for lv in range(1, 7):
                fills["gdn", s, lv] = [left.pop(0) for _ in range(2)]
        assert not left

        def v(i, r, n=1):
            return vec[:, i, r:r + n]

        def last_of(*name):
            return lambda eng: (C if name[0] in ("ffn1", "ffn2") else A).moved(eng, name)

        norms = [
            dict(src=xT, nt=8, wait=last_of("xt", 0, 1, 1), gain=amul[:, 0, :], shift=m1[:, 0:8, 0], dst=hT[:, :, 0:T]),
            dict(src=ctxT, nt=8, wait=last_of("xt", 1, 1, 1), gain=amul[:, 1, :], shift=m1[:, 0:8, 1], dst=hT[:, :, T:512]),
            dict(src=oA, nt=4, wait=last_of("a1", "o", 3), gain=v(0, V_ATTG, 4), shift=None, dst=mixT[:, 0:4, :]),
            dict(src=xT, nt=8, wait=last_of("xo1", 7), gain=amul[:, 2, :], shift=m1[:, 24:32, 0], dst=hF),
            dict(src=xT, nt=8, wait=last_of("ffn1", "acc", 3), gain=v(2, V_FIN1, 8), shift=None, dst=xT),
        ]
        for l in range(2):
            norms += [
                dict(src=xT, nt=8, wait=(lambda eng: eng.wait_ge(norm_out, 36)) if l == 0 else last_of("ffn2", "acc", 3),
                     gain=amul[:, 3 + 2 * l, :], shift=m2[:, l, 0:8], dst=h2),
                dict(src=oA2, nt=4, wait=last_of(("a2", l), "o", 3), gain=v(3, V_ATTG2 + 4 * l, 4), shift=None,
                     dst=mix2[:, 0:4, :]),
                dict(src=xT, nt=8, wait=last_of(("xo2", l), 7), gain=amul[:, 4 + 2 * l, :], shift=m2[:, l, 24:32], dst=hF),
            ]
        norms.append(dict(src=xT, nt=8, wait=lambda eng: eng.wait_ge(x_updated, 8), gain=v(2, V_FIN2, 8), shift=None, dst=xT))
        total = 0
        for n in norms:
            total += n["nt"]
            n["out"] = total
        assert norms[4]["out"] == 36

        TILE = [[2, 3, 0, 1], [3, 2, 1, 0]]

        def gcol(buf, d, tt, h=0, n=1):
            a = (d * 4 + tt) * 4 + h
            return gates[:, buf, a:a + n]
        G_G, G_BETA, G_CUM, G_NCUM, G_TOT, G_EG, G_NEG, G_KD, G_DL, G_T0, G_T1, G_EA = range(12)

        HQ = 8
        block = ctx.enter_context(nc.Block())

        @block.tensor
        def _(pe):
            mm = nc.tensor.matmul
            owed = [0]

            def owe():
                owed[0] += 1

            def pay(ins):
                if owed[0]:
                    ins.then_inc(unit_used, owed[0])
                    owed[0] = 0

            def unit(name):
                k = order[name]
                pe.wait_ge(landed[k % RING], 16 * (k // RING + 1))
                return ring[:, k % RING, :]

            def ada(part, u):
                w = unit(("mod", part, u)).rearrange("p (k n) -> p k n", k=KT)
                if (part, u) in ((0, 0), (1, 0), (2, 0)):
                    pe.wait_ge(cs_ready, 1)
                bank = C.take(pe, ("ada", part, u))
                two = part == 0 and u < 8
                for j in range(2):
                    for k in range(KT):
                        rhs = cs[:, k, 0:2] if two else (cs[:, k, 0:1] if part == 0 else cs2[:, k:k + 1])
                        o = bank[:, 2 * j:2 * j + 2] if two else bank[:, j:j + 1]
                        ins = mm(o, w[:, k, j * P:(j + 1) * P], rhs, start=k == 0, stop=k == KT - 1)
                        if k == 0:
                            pay(ins)
                owe()
                C.done(("ada", part, u), ins)

            def norm_sum(n):
                N = norms[n]
                pe.wait_ge(sq_ready, n + 1)
                bank = A.take(pe, ("ss", n))
                for k in range(N["nt"]):
                    ins = mm(bank[:, 0:T], ones, sq[:, k * T:(k + 1) * T], start=k == 0, stop=k == N["nt"] - 1)
                    if k == 0:
                        pay(ins)
                A.done(("ss", n), ins)

            def proj(name, w, j, h, width):
                bank = A.take(pe, name)
                for k in range(KT):
                    ins = mm(bank[:, 0:width], w[:, k, j * P:(j + 1) * P], h[:, k, 0:width],
                             start=k == 0, stop=k == KT - 1)
                    if k == 0:
                        pay(ins)
                A.done(name, ins)

            pe.wait_ge(con_landed, 16)
            pe.wait_ge(v_landed, 16 * 26)
            bank = A.take(pe, "vec")
            for i, rows in enumerate((V0_ROWS, V1_ROWS, V2_ROWS, V3_ROWS)):
                ins = nc.tensor.transpose(bank[:, i * P:i * P + rows], sq[0:rows, i * P:(i + 1) * P],
                                          ident[0:rows, 0:rows])
            A.done("vec", ins)
            pe.wait_ge(x_landed, 32)
            for s in range(2):
                for tt in range(TT):
                    for kg in range(2):
                        bank = A.take(pe, ("xt", s, tt, kg))
                        for k in range(4):
                            ins = nc.tensor.transpose(bank[:, k * P:(k + 1) * P],
                                                      xraw[:, 2 * s + tt, (4 * kg + k) * P:(4 * kg + k + 1) * P], ident)
                        A.done(("xt", s, tt, kg), ins)
            norm_sum(0)
            norm_sum(1)
            for u in range(8):
                ada(0, u)

            pe.wait_ge(norm_out, norms[1]["out"])
            for u in range(11):
                w = unit(("in1", u)).rearrange("p (k n) -> p k n", k=KT)
                if u < 2:
                    for j in range(2):
                        proj(("q", 2 * u + j), w, j, hT, T)
                elif u == 2:
                    proj("k", w, 0, hT, 512)
                    bank = A.take(pe, "v")
                    for tt in range(4):
                        for k in range(KT):
                            ins = mm(bank[:, tt * P:(tt + 1) * P], hT[:, k, tt * P:(tt + 1) * P], w[:, k, P:2 * P],
                                     start=k == 0, stop=k == KT - 1)
                    A.done("v", ins)
                elif u < 9:
                    for j in range(2):
                        i = 2 * (u - 3) + j
                        proj(("d", i), w, j, hT, T if i < 4 else 512)
                else:
                    for j in range(2):
                        proj(("z", 2 * (u - 9) + j), w, j, hT, T)
                owe()
            pe.wait_ge(wab_landed, 16)
            bank = A.take(pe, "ab", readers=2)
            for tt in range(4):
                for k in range(KT):
                    ins = mm(bank[:, tt * 16:(tt + 1) * 16], hT[:, k, tt * P:(tt + 1) * P], wab[:, k, :],
                             start=k == 0, stop=k == KT - 1)
            A.done("ab", ins)
            for h in range(4):
                pe.wait_ge(d_ready, 9 + h)
                bank = A.take(pe, ("vtm", h))
                for tt in range(4):
                    ins = nc.tensor.transpose(bank[:, tt * P:(tt + 1) * P], ybuf[:, h, tt * P:(tt + 1) * P], ident)
                A.done(("vtm", h), ins)
            for i in range(8):
                wd = T if i < 4 else 512
                pe.wait_ge(sqd_ready, i + 1)
                bank = A.take(pe, ("l2", i))
                ins = mm(bank[:, 0:wd], ones, sq[:, (i % 4) * 512:(i % 4) * 512 + wd], start=True, stop=True)
                A.done(("l2", i), ins)
            for h in range(4):
                pe.wait_ge(l2_ready, 5 + h)
                bank = A.take(pe, ("ktm", h))
                for tt in range(4):
                    ins = nc.tensor.transpose(bank[:, tt * P:(tt + 1) * P], kF[:, h, tt * P:(tt + 1) * P], ident)
                A.done(("ktm", h), ins)

            pe.wait_ge(ansq, 1)
            for j in range(3):
                bank = A.take(pe, ("an", j))
                src = sq[:, j * 512:(j + 1) * 512]
                ins = mm(bank[:, :], c_one("ones64"), src, start=True, stop=True)
                A.done(("an", j), ins)
            for j in range(3):
                pe.wait_ge(qk_normed, j + 1)
                bank = A.take(pe, ("rot", j))
                if j < 2:
                    src = qA[:, 2 * j:2 * j + 2, :].rearrange("p a b -> p (a b)")
                    ins = mm(bank[:, :], c_one("rot64"), src, start=True, stop=True)
                else:
                    ins = mm(bank[:, 0:T], c_one("rot64"), kA[:, 0:T], start=True, stop=True)
                A.done(("rot", j), ins)
            pe.wait_ge(rope_done, 3)
            for kv in range(2):
                bank = A.take(pe, ("dup", kv))
                ins = mm(bank[:, :], c_one("sel", P, kv), kA[:, :], start=True, stop=True)
                A.done(("dup", kv), ins)

            def attention(tag, base, scores, values, pbuf, ptbuf, fill):
                def score(u):
                    bank = B.take(pe, (tag, "s", u))
                    l, r, n = scores(u)
                    ins = mm(bank[:, 0:n], l, r, start=True, stop=True)
                    B.done((tag, "s", u), ins)

                def turn(u):
                    nk = scores(u)[2] // P
                    pe.wait_ge(prob_ready, base + u + 1)
                    bank = A.take(pe, (tag, "pt", u))
                    for k in range(nk):
                        ins = nc.tensor.transpose(bank[:, k * P:(k + 1) * P], pbuf[:, u % 3, k * P:(k + 1) * P], ident)
                    A.done((tag, "pt", u), ins)

                def weigh(u):
                    nk = scores(u)[2] // P
                    h, qt = u // 2, u % 2
                    r0 = HD * (h % 2)
                    if u % 4 == 0:
                        A.take(pe, (tag, "o", h // 2))
                    bank = A.banks[A.where[tag, "o", h // 2][0]]
                    A.moved(pe, (tag, "pt", u))
                    for k in range(nk):
                        ins = mm(bank[r0:r0 + HD, qt * P:(qt + 1) * P], values(u, k), ptbuf[:, u % 2, k * P:(k + 1) * P],
                                 start=k == 0, stop=k == nk - 1)
                    if u % 4 == 3:
                        A.done((tag, "o", h // 2), ins)

                for i in range(2 * HQ + 2):
                    if i < 2 * HQ:
                        score(i)
                        for f in fill(i):
                            ada(*f)
                    if 1 <= i <= 2 * HQ:
                        turn(i - 1)
                    if i >= 2:
                        weigh(i - 2)

            for n in ("v", ("dup", 0), ("dup", 1)):
                A.moved(pe, n)

            def s1(u):
                h, qt = u // 2, u % 2
                r0 = HD * (h % 2)
                return qA[r0:r0 + HD, h // 2, qt * P:(qt + 1) * P], kdup[r0:r0 + HD, h // 4, :], 512

            attention("a1", 0, s1, lambda u, k: vA[:, k, HD * (u // 8):HD * (u // 8) + HD], prob, probT,
                      lambda u: fills["att", u])
            norm_sum(2)

            pe.wait_ge(g_ready, 1)
            bank = A.take(pe, "gc")
            for d, um in enumerate(("u_fwd", "u_bwd")):
                mm(bank[:, d * 16:(d + 1) * 16], c_one(um), gates[:, G_G, d * 16:(d + 1) * 16], start=True, stop=True)
            ins = mm(bank[:, 32:64], ones, gates[:, G_G, :], start=True, stop=True)
            A.done("gc", ins)
            for h in range(4):
                A.moved(pe, ("ktm", h))
                A.moved(pe, ("vtm", h))
            for s in range(4):
                for d in range(2):
                    g, tt = 2 * s + d, TILE[d][s]
                    lat = tt < 2
                    bank = A.take(pe, ("gb", g), readers=2 if lat else 1)
                    for h in range(4):
                        ins = mm(bank[:, h * P:(h + 1) * P], gcol(G_G, d, tt, h).to_broadcast([P, P]),
                                 c_one(("u_fwd", "u_bwd")[d]), start=True, stop=True)
                    A.done(("gb", g), ins)
                    bank = A.take(pe, ("kk", g))
                    for h in range(4):
                        k = kF[:, h, tt * P:(tt + 1) * P]
                        ins = mm(bank[:, h * P:(h + 1) * P], k, k, start=True, stop=True)
                    A.done(("kk", g), ins)
                    if lat:
                        bank = B.take(pe, ("kq", g))
                        for h in range(4):
                            ins = mm(bank[:, h * P:(h + 1) * P], kF[:, h, tt * P:(tt + 1) * P],
                                     qF[:, h, tt * P:(tt + 1) * P], start=True, stop=True)
                        B.done(("kq", g), ins)
                for d in range(2):
                    g = 2 * s + d
                    A.moved(pe, ("kk", g))
                    bank = A.take(pe, ("lt", g))
                    for h in range(4):
                        ins = nc.tensor.transpose(bank[:, h * P:(h + 1) * P], dec[:, d, h * P:(h + 1) * P], ident)
                    A.done(("lt", g), ins)
                for lv in range(1, 7):
                    n = s * 6 + lv - 1
                    for d in range(2):
                        g = 2 * s + d
                        pe.wait_ge(ls_ready, 2 * n + d + 1)
                        if lv == 1:
                            pe.wait_ge(seed_ready, g + 1)
                        else:
                            A.moved(pe, ("dt", g, lv - 1))
                        bank = A.take(pe, ("m1", g, lv))
                        for h in range(4):
                            c = slice(h * P, (h + 1) * P)
                            ins = mm(bank[:, c], LsT[:, 2 * d + lv % 2, c], Tm[:, d, c], start=True, stop=True)
                        A.done(("m1", g, lv), ins)
                    for f in fills["gdn", s, lv][0:1]:
                        ada(*f)
                    for d in range(2):
                        g = 2 * s + d
                        A.moved(pe, ("m1", g, lv))
                        if lv > 1:
                            A.moved(pe, ("dtt", g, lv - 1))
                        if lv < 6:
                            bank = A.take(pe, ("dt", g, lv))
                            for h in range(4):
                                c = slice(h * P, (h + 1) * P)
                                ins = mm(bank[:, c], TTm[:, d, c], M1[:, d, c], start=True, stop=True)
                            A.done(("dt", g, lv), ins)
                        bank = A.take(pe, ("dtt", g, lv))
                        for h in range(4):
                            c = slice(h * P, (h + 1) * P)
                            ins = mm(bank[:, c], M1[:, d, c], TTm[:, d, c], start=True, stop=True)
                        A.done(("dtt", g, lv), ins)
                    for f in fills["gdn", s, lv][1:2]:
                        ada(*f)
                for d in range(2):
                    g, tt = 2 * s + d, TILE[d][s]
                    pe.wait_ge(ttb_ready, g + 1)
                    pe.wait_ge(kb_ready, g + 1)
                    if s:
                        bank = A.take(pe, ("nw", g))
                        for h in range(4):
                            c = slice(h * P, (h + 1) * P)
                            ins = mm(bank[:, c], kbe[:, d, c], TTm[:, d, c], start=True, stop=True)
                        A.done(("nw", g), ins)
                for d in range(2):
                    g, tt = 2 * s + d, TILE[d][s]
                    if s:
                        A.moved(pe, ("nw", g))
                        A.moved(pe, ("st", g - 2))
                    bank = B.take(pe, ("vn", g))
                    for h in range(4):
                        c = slice(h * P, (h + 1) * P)
                        ins = mm(bank[:, c], TTm[:, d, c], v_tm[:, tt, h, :], start=True, stop=s == 0)
                        if s:
                            ins = mm(bank[:, c], nwT[:, d, c], S[:, d, c], start=False, stop=True)
                    B.done(("vn", g), ins)
                for d in range(2):
                    g, tt = 2 * s + d, TILE[d][s]
                    B.moved(pe, ("vn", g))
                    if tt < 2:
                        pe.wait_ge(qdec_ready, g - 3)
                        B.moved(pe, ("kq", g))
                        bank = B.take(pe, ("og", g))
                        for h in range(4):
                            c = slice(h * P, (h + 1) * P)
                            mm(bank[:, c], S[:, d, c], qdec[:, d, c], start=True, stop=False)
                            ins = mm(bank[:, c], vnew[:, d, c], ATm[:, d, c], start=False, stop=True)
                        B.done(("og", g), ins)
                    if s < 3:
                        bank = A.take(pe, ("st", g))
                        for h in range(4):
                            c = slice(h * P, (h + 1) * P)
                            ins = mm(bank[:, c], kdec[:, d, c], vnew[:, d, c], start=True, stop=True)
                        A.done(("st", g), ins)

            def head_norm_sum(j):
                pe.wait_ge(hn_sq, j + 1)
                for i in range(2):
                    bank = A.take(pe, ("hn", j, i))
                    ins = mm(bank[:, :], ones, sq[:, i * 512:(i + 1) * 512], start=True, stop=True)
                    A.done(("hn", j, i), ins)
            head_norm_sum(0)

            def project_out(tag, names, mix, ready):
                for s_, n_ in ready:
                    pe.wait_ge(s_, n_)
                for u in range(4):
                    w = unit(names + (u,)).rearrange("p (k n) -> p k n", k=KT)
                    for j in range(2):
                        proj((tag, 2 * u + j), w, j, mix, T)
                    owe()

            project_out("xo1", ("out1",), mixT, [(hn_out, 4), (norm_out, norms[2]["out"])])

            def ffn(tag, h):
                accs = []

                def up(f):
                    c, j = f // 2, f % 2
                    bank = A.take(pe, (tag, "gu", f))
                    for i, m in enumerate("gu"):
                        w = unit((tag, m, c)).rearrange("p (k n) -> p k n", k=KT)
                        for k in range(KT):
                            ins = mm(bank[:, i * T:(i + 1) * T], w[:, k, j * P:(j + 1) * P], h[:, k, :],
                                     start=k == 0, stop=k == KT - 1)
                            if k == 0:
                                pay(ins)
                        if j == 1 and i == 0:
                            ins.then_inc(unit_used, 1)
                    if j == 1:
                        owe()
                    A.done((tag, "gu", f), ins)

                def down(f):
                    if f == 0:
                        accs.extend(B.take(pe, (tag, "acc", i)) for i in range(3))
                        accs.append(C.take(pe, (tag, "acc", 3)))
                    w = unit((tag, "d", f // 2)).rearrange("p (r n) -> p r n", r=2)
                    if tag == "ffn1":
                        pe.wait_ge(gT_ready, f + 1)
                    else:
                        A.moved(pe, (tag, "gu", f))
                    for dt in range(KT):
                        ins = mm(accs[dt // 2][:, (dt % 2) * T:(dt % 2 + 1) * T], w[:, f % 2, dt * P:(dt + 1) * P],
                                 gT[:, f % 4, :], start=f == 0 and dt % 2 == 0, stop=f == FT - 1,
                                 skip_group_check=True)
                        if dt == 0:
                            pay(ins)
                        if f == FT - 1 and dt % 2 == 1:
                            rg = B if dt < 6 else C
                            rg.done((tag, "acc", dt // 2), ins)
                    if f == FT - 1:
                        owe()
                    elif f % 2:
                        ins.then_inc(unit_used, 1)

                for f in range(FT + 2):
                    if f < FT:
                        up(f)
                    if f >= 2 and f % 2 == 1:
                        down(f - 3)
                        down(f - 2)

            norm_sum(3)
            pe.wait_ge(norm_out, norms[3]["out"])
            ffn("ffn1", hF)
            norm_sum(4)

            for l in range(2):
                n0 = 5 + 3 * l
                norm_sum(n0)
                pe.wait_ge(norm_out, norms[n0]["out"])
                for u in range(14):
                    w = unit(("in2", l, u)).rearrange("p (k n) -> p k n", k=KT)
                    kind, half = "qa ka va qr kr vr gr".split()[u // 2], u % 2
                    if kind[0] == "v":
                        bank = A.take(pe, (l, kind, half))
                        for tt in range(TT):
                            for k in range(KT):
                                ins = mm(bank[:, tt * UW:(tt + 1) * UW], h2[:, k, tt * P:(tt + 1) * P], w[:, k, :],
                                         start=k == 0, stop=k == KT - 1)
                        A.done((l, kind, half), ins)
                    else:
                        for j in range(2):
                            proj((l, kind, 2 * half + j), w, j, h2, T)
                    owe()

                pe.wait_ge(con2_landed, 16)
                for j in range(4):
                    for i in range(2):
                        A.moved(pe, (l, "qr" if j < 2 else "kr", 2 * (j % 2) + i))
                    bank = A.take(pe, (l, "rr", j))
                    src = (qR if j < 2 else kR)[:, 2 * (j % 2):2 * (j % 2) + 2, :].rearrange("p a b -> p (a b)")
                    ins = mm(bank[:, :], c_two("rot128"), src, start=True, stop=True)
                    A.done((l, "rr", j), ins)
                for n in [(l, "qa", i) for i in range(4)] + [(l, "ka", i) for i in range(4)] + [(l, "va", 0), (l, "va", 1)]:
                    A.moved(pe, n)

                def s2(u):
                    h, qt = u // 2, u % 2
                    r0 = HD * (h % 2)
                    return qA2[r0:r0 + HD, h // 2, qt * P:(qt + 1) * P], kA2[r0:r0 + HD, h // 2, 0:(qt + 1) * P], (qt + 1) * P

                attention(("a2", l), 16 * (l + 1), s2,
                          lambda u, k: vA2[:, k, HD * (u // 2):HD * (u // 2) + HD], prob2, probT2, lambda u: [])
                norm_sum(n0 + 1)
                pe.wait_ge(rrope, 4 * (l + 1))
                A.moved(pe, (l, "vr", 0))
                A.moved(pe, (l, "vr", 1))

                def ret_scores(h):
                    bank = B.take(pe, (l, "rs", h))
                    mm(bank[:, 0:256], kR[:, h, 0:P], qR[:, h, :], start=True, stop=True)
                    ins = mm(bank[:, 256:384], kR[:, h, P:T], qR[:, h, P:T], start=True, stop=True)
                    B.done((l, "rs", h), ins)
                ret_scores(0)
                for h in range(4):
                    if h < 3:
                        ret_scores(h + 1)
                    B.moved(pe, (l, "rs", h))
                    bank = A.take(pe, (l, "ro", h))
                    a = AR[:, h % 2, :]
                    mm(bank[:, 0:P], vR[:, 0, h * P:(h + 1) * P], a[:, 0:P], start=True, stop=True)
                    mm(bank[:, P:T], vR[:, 0, h * P:(h + 1) * P], a[:, P:T], start=True, stop=False)
                    ins = mm(bank[:, P:T], vR[:, 1, h * P:(h + 1) * P], a[:, 256:384], start=False, stop=True)
                    A.done((l, "ro", h), ins)
                head_norm_sum(1 + l)
                project_out(("xo2", l), ("out2", l), mix2, [(hn_out, 4 * (l + 2)), (norm_out, norms[n0 + 1]["out"])])
                norm_sum(n0 + 2)
                pe.wait_ge(norm_out, norms[n0 + 2]["out"])
                if l == 0:
                    ffn("ffn2", hF)

            pe.wait_ge(wrt_landed, 16)
            bank = A.take(pe, "logits")
            for tt in range(TT):
                for k in range(KT):
                    ins = mm(bank[:, tt * NE:(tt + 1) * NE], hF[:, k, tt * P:(tt + 1) * P], wrt[:, k, :],
                             start=k == 0, stop=k == KT - 1)
            A.done("logits", ins)
            for tt in range(TT):
                for kg in range(2):
                    bank = A.take(pe, ("htm", tt, kg))
                    for k in range(4):
                        ins = nc.tensor.transpose(bank[:, k * P:(k + 1) * P],
                                                  hF[:, 4 * kg + k, tt * P:(tt + 1) * P], ident)
                    A.done(("htm", tt, kg), ins)
            pe.wait_ge(sel_ready, 1)
            bank = A.take(pe, "pos")
            sel = [rout[:, 4 + tt, :] for tt in range(2)]
            mm(bank[:, 0:8], c_all("ustrict"), sel[0], start=True, stop=True)
            mm(bank[:, 8:16], ones, sel[0], start=True, stop=False)
            mm(bank[:, 8:16], c_all("ustrict"), sel[1], start=False, stop=True)
            mm(bank[:, 16:24], ones, sel[0], start=True, stop=False)
            ins = mm(bank[:, 16:24], ones, sel[1], start=False, stop=True)
            A.done("pos", ins)
            for e in range(NE):
                pe.wait_ge(pw_ready, e + 1)
                bank = A.take(pe, ("pwT", e))
                for s in range(2):
                    for tt in range(TT):
                        ins = nc.tensor.transpose(bank[:, s * T + tt * P:s * T + (tt + 1) * P],
                                                  Pw[:, e % 2, tt * 256 + s * P:tt * 256 + (s + 1) * P], ident)
                A.done(("pwT", e), ins)
            for rg in (A, B, C):
                rg.all_free(pe)

            def expert(e, ns):
                st = ns // P

                def eunit(name):
                    k = U0 + e_order[name]
                    pe.wait_ge(landed[k % RING], e * (16 * EU // RING) + 16 * (k // RING + 1))
                    return ring[:, k % RING, :]

                for j in range(KT):
                    pe.wait_ge(moved, e * 16 + (j + 1))
                    bank = banks[2 + j % 2]
                    for tt in range(TT):
                        ins = mm(bank[:, 0:ns], h_tm[:, tt, j * P:(j + 1) * P], Pg[:, tt, e, 0:ns],
                                 start=tt == 0, stop=tt == TT - 1)
                    ins.then_inc(xj_full, 1)
                pe.wait_ge(moved, e * 16 + (KT + 2))

                def up(f):
                    c, j = f // 2, f % 2
                    pe.wait_ge(gated, e * FT + (f + 1))
                    bank = banks[f % 2]
                    for i, m in enumerate("gu"):
                        w = eunit((m, c)).rearrange("p (k n) -> p k n", k=KT)
                        for k in range(KT):
                            ins = mm(bank[:, i * ns:(i + 1) * ns], w[:, k, j * P:(j + 1) * P], xg[:, k, 0:ns],
                                     start=k == 0, stop=k == KT - 1)
                            if k == 0:
                                pay(ins)
                        if j == 1 and i == 0:
                            ins.then_inc(unit_used, 1)
                    if j == 1:
                        owe()
                    ins.then_inc(gu_full, 1)

                def down(f):
                    w = eunit(("d", f // 2)).rearrange("p (r n) -> p r n", r=2)
                    pe.wait_ge(gated, e * FT + (f + 3))
                    for s in range(st):
                        for half in range(2):
                            ins = mm(banks[4 + 2 * s + half][:, :], gTe[:, f % 4, s * P:(s + 1) * P],
                                     w[:, f % 2, half * 512:(half + 1) * 512], start=f == 0, stop=f == FT - 1,
                                     skip_group_check=True)
                            if s == 0 and half == 0:
                                pay(ins)
                    if f % 2:
                        ins.then_inc(unit_used, 1)

                for f in range(FT + 2):
                    if f < FT:
                        up(f)
                    if f >= 2 and f % 2 == 1:
                        down(f - 3)
                        down(f - 2)
                pe.wait_ge(ye_ready, e + 1)
                for j in range(KT):
                    pe.wait_ge(moved, e * 16 + (8 + j + 1))
                    bank = banks[2 + j % 2]
                    for s in range(st):
                        ins = mm(bank[:, 0:T], ye[:, s, j * P:(j + 1) * P], PwT[:, s, e, :],
                                 start=s == 0, stop=s == st - 1)
                    ins.then_inc(xj_full, 1)

            with pe.Fori(0, NE) as e:
                count = pe.value_load(cnt_i[0:1, bass.ts(e, 1)], min_val=0, max_val=T)
                with pe.If(count > NARROW):
                    expert(e, T)
                with pe.Else():
                    expert(e, NARROW)
                pe.nop()

            pe.wait_ge(sq_ready, 12)
            for k in range(KT):
                ins = mm(banks[0][:, 0:T], ones, sq[:, k * T:(k + 1) * T], start=k == 0, stop=k == KT - 1)
            ins.then_inc(fin_ready, 1)
            pe.wait_ge(norm_out, norms[11]["out"])
            for tt in range(TT):
                for kg in range(2):
                    for k in range(4):
                        ins = nc.tensor.transpose(banks[4 + 2 * tt + kg][:, k * P:(k + 1) * P],
                                                  xT[:, 4 * kg + k, tt * P:(tt + 1) * P], ident)
                    ins.then_inc(fin_ready, 1)

        @block.scalar
        def _(act):
            steps = [0]

            def step(ins):
                steps[0] += 1
                ins.then_inc(act_step, 1)
                act.wait_ge(act_step, steps[0])
            F = nc.scalar.activation

            rows = sq[:, :]

            def vrow(table, row, ap):
                n = ap.shape[0]
                act.dma_start(rows[row:row + n, table * P:(table + 1) * P], ap).then_inc(v_landed, 16)

            def tiles(ap):
                return ap.rearrange("(a p) -> a p", p=P)
            vrow(0, V_C, tiles(t["c"][0]))
            vrow(0, V_CCTX, tiles(t["c_ctx"]))
            vrow(0, V_BMOD, tiles(t["b_mod"][0]))
            vrow(0, V_N1, tiles(t["norm1_g"][0]))
            vrow(0, V_ATTG, tiles(t["attn_out_g"][0]))
            vrow(0, V_GDNG, t["gdn_norm_g"])
            vrow(0, V_N2, tiles(t["norm2_g"][0]))
            vrow(0, V_CONV, t["conv_qkv_w"][0].rearrange("k (a p) -> (k a) p", p=P))
            for row, name in ((V_QG, "q_norm_g"), (V_KG, "k_norm_g")):
                for half in range(2):
                    act.dma_start(rows[row:row + 1, half * HD:(half + 1) * HD], t[name]).then_inc(v_landed, 16)
            cw = t["ffn_conv_w"][0].rearrange("k (a p) -> k a p", p=P)
            vrow(1, V_FW01, cw[0])
            vrow(1, V_FW01 + 44, cw[1])
            vrow(1, V_C2, tiles(t["c_2"][0]))
            vrow(1, V_NMIX, t["norm_mix_g_2"].rearrange("l (a p) -> (l a) p", p=P))
            vrow(1, V_NFFN, t["norm_ffn_g_2"].rearrange("l (a p) -> (l a) p", p=P))
            vrow(2, V_FW2, cw[2])
            vrow(2, V_FB, tiles(t["ffn_conv_b"][0]))
            vrow(2, V_FIN1, tiles(t["final_norm_g"]))
            vrow(2, V_FIN2, tiles(t["final_norm_g_2"]))
            vrow(3, V_BADA, t["ada_b_2"][0:1].rearrange("l (a p) -> (l a) p", p=P))
            vrow(3, V_BADA + 48, t["ada_b_2"][1:2].rearrange("l (a p) -> (l a) p", p=P))
            vrow(3, V_ATTG2, t["att_out_g_2"][0:1].rearrange("l (a p) -> (l a) p", p=P))
            vrow(3, V_ATTG2 + 4, t["att_out_g_2"][1:2].rearrange("l (a p) -> (l a) p", p=P))
            vrow(3, V_RETG, t["ret_out_g_2"].rearrange("l (a p) -> (l a) p", p=P))
            act.dma_start(con2[:, :], t["constants"][:, C_ALL_W:C_ALL_W + C_ONE_W]).then_inc(con1_landed, 16)
            for i, (f, b) in enumerate((("a_log_f", "a_log_b"), ("dt_bias_f", "dt_bias_b"))):
                for j, name in enumerate((f, b)):
                    act.dma_start(gconst[:, i, 4 * j:4 * j + 4], t[name].to_broadcast([P, 4])).then_inc(gc_landed, 16)
            with nc.allow_non_contiguous_dma(reason="small"):
                act.dma_start(wab[:, :, :], t["w_in"][0][:, 11 * UW:].rearrange("(k p) n -> p k n", p=P)).then_inc(wab_landed, 16)
                act.dma_start(wrt[:, :, :], t["router_w_2"][0].rearrange("(k p) n -> p k n", p=P)).then_inc(wrt_landed, 16)

            A.moved(act, "vec")
            F(cs[:, :, 0], v(0, V_C, 8), ACT.Silu)
            F(cs[:, :, 1], v(0, V_CCTX, 8), ACT.Silu)
            F(cs2[:, :], v(1, V_C2, 8), ACT.Silu).then_inc(cs_ready, 1)
            for s in range(2):
                dst = (xT, ctxT)[s]
                for tt in range(TT):
                    for kg in range(2):
                        n = ("xt", s, tt, kg)
                        bank = A.full(act, n)
                        ins = F(dst[:, 4 * kg:4 * kg + 4, tt * P:(tt + 1) * P],
                                bank[:, :].rearrange("p (a b) -> p a b", a=4), ACT.Copy)
                        A.free(n, ins)

            def norm(n):
                N = norms[n]
                N["wait"](act)
                w = N["nt"] * T
                F(sq[:, 0:w].rearrange("p (a b) -> p a b", b=T), N["src"], ACT.Square).then_inc(sq_ready, 1)
                if n == 11:
                    act.wait_ge(fin_ready, 1)
                    bank = banks[0]
                else:
                    bank = A.full(act, ("ss", n))
                if n:
                    act.wait_ge(norm_out, norms[n - 1]["out"])
                ins = F(rstd[:, 0:T], bank[:, 0:T], ACT.Sqrt, bias=EPS, scale=1.0 / (N["nt"] * P))
                if n == 11:
                    ins.then_inc(root_ready, 1)
                else:
                    A.free(("ss", n), ins)
            norm(0)
            norm(1)

            for i in range(4):
                ins = F(qA[:, i, :], A.full(act, ("q", i))[:, 0:T], ACT.Copy)
                A.free(("q", i), ins)
            ins = F(kA[:, :], A.full(act, "k")[:, :], ACT.Copy)
            A.free("k", ins)
            ins = F(vA[:, :, :].rearrange("p a b -> p (a b)"), A.full(act, "v")[:, :], ACT.Copy)
            A.free("v", ins)

            def conv_out(i):
                A.moved(act, ("d", i))
                wd = T if i < 4 else 512
                y = ybuf[:, i % 4, 0:wd]
                dst = qF[:, i, :] if i < 4 else kF[:, i - 4, :] if i < 8 else y
                F(dst, y, ACT.Silu).then_inc(d_ready, 1)
            for i in range(12):
                if i >= 4:
                    act.wait_ge(d_ready, i - 3)
                wd = T if i < 4 else 512
                bank = A.full(act, ("d", i))
                F(ybuf[:, i % 4, 0:wd], bank[:, 0:wd], ACT.Copy, scale=v(0, V_CONV + 12 + i)).then_inc(centre_ready, 1)
                if i >= 1:
                    conv_out(i - 1)
            conv_out(11)
            for i in range(4):
                ins = F(zs[:, i, :], A.full(act, ("z", i))[:, 0:T], ACT.Silu)
                A.free(("z", i), ins)
            bank = A.full(act, "ab")
            act.wait_ge(sp_abs, 1)
            ins = F(gates[:, G_BETA, :].rearrange("p (d t h) -> p t d h", d=2, t=4),
                    bank[:, 0:64].rearrange("p (t x d h) -> p t x d h", t=4, x=2, d=2)[:, :, 1, :, :], ACT.Sigmoid)
            A.free("ab", ins)
            step(F(gates[:, G_T1, :], gates[:, G_T1, :], ACT.Exp, scale=-1.0))
            act.wait_ge(gc_landed, 64)
            F(gates[:, G_EA, 0:8], gconst[:, 0, :], ACT.Exp)
            F(gates[:, G_T1, :], gates[:, G_T1, :], ACT.Ln, bias=1.0).then_inc(sp_ln, 1)
            for h in range(4):
                n = ("vtm", h)
                ins = F(v_tm[:, :, h, :], A.full(act, n)[:, :].rearrange("p (a b) -> p a b", a=4), ACT.Copy)
                A.free(n, ins)
            def l2_root(i):
                wd = T if i < 4 else 512
                bank = A.full(act, ("l2", i))
                if i >= 2:
                    act.wait_ge(l2_ready, i - 1)
                c = float(P) if i < 4 else 1.0
                ins = F(hroot[:, i % 2, 0:wd], bank[:, 0:wd], ACT.Sqrt, bias=EPS * c, scale=c)
                A.free(("l2", i), ins)
            act.wait_ge(d_ready, 12)
            for i in range(9):
                if i < 8:
                    wd = T if i < 4 else 512
                    if i >= 4:
                        A.full(act, ("l2", i - 4))
                    F(sq[:, (i % 4) * 512:(i % 4) * 512 + wd], qF[:, i, :] if i < 4 else kF[:, i - 4, :],
                      ACT.Square).then_inc(sqd_ready, 1)
                if i:
                    l2_root(i - 1)
            for h in range(4):
                n = ("ktm", h)
                ins = F(k_tm[:, :, h, :], A.full(act, n)[:, :].rearrange("p (a b) -> p a b", a=4), ACT.Copy)
                A.free(n, ins)
            for n in [("q", i) for i in range(4)] + ["k"]:
                A.moved(act, n)
            F(sq[:, 0:1024], qA[:, :, :].rearrange("p a b -> p (a b)"), ACT.Square)
            F(sq[:, 1024:1536], kA[:, :], ACT.Square).then_inc(ansq, 1)
            act.wait_ge(l2_ready, 8)
            for j in range(3):
                n = ("an", j)
                ins = F(hroot[:, j, :] if j < 2 else kroot, A.full(act, n)[:, :], ACT.Sqrt, bias=EPS, scale=1.0 / HD)
                A.free(n, ins)
            for kv in range(2):
                n = ("dup", kv)
                ins = F(kdup[:, kv, :], A.full(act, n)[:, :], ACT.Copy)
                A.free(n, ins)

            def attention(tag, base, keys, scaled, pbuf, ptbuf, o):
                def expo(u):
                    n = keys(u)
                    act.wait_ge(max_ready, base + u + 1)
                    st = stat[:, u % 4, :]
                    if scaled:
                        F(pbuf[:, u % 3, 0:n], pbuf[:, u % 3, 0:n], ACT.Exp, bias=st[:, 1:2],
                          accum_out=st[:, 2:3]).then_inc(exp_done, 1)
                    else:
                        bank = B.full(act, (tag, "s", u))
                        if u >= 3:
                            A.full(act, (tag, "pt", u - 3))
                        ins = F(pbuf[:, u % 3, 0:n], bank[:, 0:n], ACT.Exp, bias=st[:, 1:2], scale=HD ** -0.5,
                                accum_out=st[:, 2:3])
                        B.free((tag, "s", u), ins)

                def turned(u):
                    n = keys(u)
                    name = (tag, "pt", u)
                    ins = F(ptbuf[:, u % 2, 0:n], A.full(act, name)[:, 0:n], ACT.Copy)
                    A.free(name, ins)

                def output(j):
                    name = (tag, "o", j)
                    ins = F(o[:, j, :], A.full(act, name)[:, 0:T], ACT.Copy)
                    A.free(name, ins)
                for i in range(2 * HQ + 2):
                    if i < 2 * HQ:
                        expo(i)
                    if 1 <= i <= 2 * HQ:
                        turned(i - 1)
                    if i >= 5 and i % 4 == 1:
                        output((i - 5) // 4)

            attention("a1", 0, lambda u: 512, False, prob, probT, oA)
            norm(2)

            act.wait_ge(tmg_ready, 1)
            F(gates[:, G_EG, :], gates[:, G_CUM, :], ACT.Exp)
            F(gates[:, G_KD, :], gates[:, G_T0, :], ACT.Exp)
            F(gates[:, G_DL, :], gates[:, G_TOT, :], ACT.Exp).then_inc(gate_ready, 1)

            def head_norm(j, src, wait):
                wait()
                F(sq[:, 0:1024], src.rearrange("p a b -> p (a b)"), ACT.Square).then_inc(hn_sq, 1)
                if j == 0:
                    act.wait_ge(qk_normed, 3)
                else:
                    act.wait_ge(hn_out, 4 * j)
                for i in range(2):
                    n = ("hn", j, i)
                    ins = F(hroot[:, i, :], A.full(act, n)[:, :], ACT.Sqrt, bias=EPS, scale=1.0 / P)
                    A.free(n, ins)

            for s in range(4):
                for d in range(2):
                    g, tt = 2 * s + d, TILE[d][s]
                    if tt < 2:
                        A.moved(act, ("gb", g), 1)
                        ins = F(egb[:, d, :], A.full(act, ("gb", g))[:, :], ACT.Exp)
                        A.free(("gb", g), ins)
                    A.moved(act, ("gb", g))
                    for h in range(4):
                        c = slice(h * P, (h + 1) * P)
                        ins = F(dec[:, d, c], dec[:, d, c], ACT.Exp, bias=gcol(G_CUM, d, tt, h))
                    ins.then_inc(dec_ready, 1)
                    if tt < 2:
                        for h in range(4):
                            c = slice(h * P, (h + 1) * P)
                            ins = F(ATm[:, d, c], ATm[:, d, c], ACT.Exp, bias=gcol(G_NCUM, d, tt, h))
                        ins.then_inc(att_ready, 1)
                for d in range(2):
                    n = ("lt", 2 * s + d)
                    A.free(n, F(LTm[:, d, :], A.full(act, n)[:, :], ACT.Copy))
                for lv in range(1, 7):
                    for d in range(2):
                        n = ("m1", 2 * s + d, lv)
                        A.free(n, F(M1[:, d, :], A.full(act, n)[:, :], ACT.Copy))
                if s:
                    for d in range(2):
                        n = ("nw", 2 * s + d)
                        A.free(n, F(nwT[:, d, :], A.full(act, n)[:, :], ACT.Copy))
                for d in range(2):
                    n = ("vn", 2 * s + d)
                    B.free(n, F(vnew[:, d, :], B.full(act, n)[:, :], ACT.Copy))

            def last_og():
                B.moved(act, ("og", 7))
                B.moved(act, ("og", 6))
            head_norm(0, oG, last_og)
            norm(3)
            act.dma_start(con2[:, 0:C_TWO_W], t["constants"][:, C_ALL_W + C_ONE_W:]).then_inc(con2_landed, 16)

            for f in range(FT + 1):
                if f < FT:
                    bank = A.full(act, ("ffn1", "gu", f))
                    if f >= 3:
                        act.wait_ge(gT_ready, f - 2)
                    F(yc[:, f % 3, 0:T], bank[:, 0:T], ACT.Identity, scale=v(1, V_FW01 + 44 + f), bias=v(2, V_FB + f))
                    F(yc[:, f % 3, T:512], bank[:, T:512], ACT.Identity, scale=v(1, V_FW01 + 44 + FT + f),
                      bias=v(2, V_FB + FT + f)).then_inc(centre_ready, 1)
                if f:
                    A.moved(act, ("ffn1", "gu", f - 1))
                    y = yc[:, (f - 1) % 3, 0:T]
                    F(y, y, ACT.Silu).then_inc(silu_ready, 1)
            norm(4)

            for l in range(2):
                n0 = 5 + 3 * l
                norm(n0)
                for u in range(14):
                    kind, half = "qa ka va qr kr vr gr".split()[u // 2], u % 2
                    if kind[0] == "v":
                        n = (l, kind, half)
                        dst = vA2 if kind == "va" else vR
                        A.free(n, F(dst[:, :, half * UW:(half + 1) * UW],
                                    A.full(act, n)[:, :].rearrange("p (a b) -> p a b", a=2), ACT.Copy))
                    else:
                        dst = dict(qa=qA2, ka=kA2, qr=qR, kr=kR, gr=sgr)[kind]
                        for j in range(2):
                            n = (l, kind, 2 * half + j)
                            A.free(n, F(dst[:, 2 * half + j, :], A.full(act, n)[:, 0:T],
                                        ACT.Silu if kind == "gr" else ACT.Copy))
                attention(("a2", l), 16 * (l + 1), lambda u: (u % 2 + 1) * P, True, prob2, probT2, oA2)
                norm(n0 + 1)
                for h in range(4):
                    n = (l, "ro", h)
                    A.free(n, F(oR[:, h, :], A.full(act, n)[:, 0:T], ACT.Copy))

                def last_ro():
                    for h in range(4):
                        A.moved(act, (l, "ro", h))
                head_norm(1 + l, oR, last_ro)
                norm(n0 + 2)
                if l == 0:
                    for f in range(FT):
                        bank = A.full(act, ("ffn2", "gu", f))
                        if f >= 3:
                            A.moved(act, ("ffn2", "gu", f - 3))
                        F(yc[:, f % 3, 0:T], bank[:, 0:T], ACT.Silu).then_inc(silu_ready, 1)

            for tt in range(TT):
                for kg in range(2):
                    n = ("htm", tt, kg)
                    A.free(n, F(h_tm[:, tt, kg * 512:(kg + 1) * 512], A.full(act, n)[:, :], ACT.Copy))
            act.wait_ge(top_ready, 1)
            for tt in range(TT):
                F(rout[:, 14 + tt, 0:1], rout[:, 12 + tt, 0:1], ACT.Sigmoid)
                ins = F(rout[:, 14 + tt, 1:2], rout[:, 12 + tt, 0:1], ACT.Sigmoid, scale=-1.0)
            ins.then_inc(wt_ready, 1)
            for e in range(NE):
                n = ("pwT", e)
                A.free(n, F(PwT[:, :, e, :], A.full(act, n)[:, :].rearrange("p (a b) -> p a b", a=2), ACT.Copy))
            A.moved(act, "pos")

            def expert(e, ns):
                for f in range(FT):
                    act.wait_ge(gu_full, e * FT + (f + 1))
                    act.wait_ge(gated, e * FT + (f + 1))
                    F(sge[:, f % 2, 0:ns], banks[f % 2][:, 0:ns], ACT.Silu).then_inc(sge_ready, 1)
                act.wait_ge(unit_used, e * EU + (U0 + EU))
                for i in range(2 * ns // P):
                    ins = F(ye[:, i // 2, (i % 2) * 512:(i % 2 + 1) * 512], banks[4 + i][:, :], ACT.Copy)
                ins.then_inc(ye_ready, 1)

            with act.Fori(0, NE) as e:
                count = act.value_load(cnt_i[0:1, bass.ts(e, 1)], min_val=0, max_val=T)
                with act.If(count > NARROW):
                    expert(e, T)
                with act.Else():
                    expert(e, NARROW)
                act.nop()
            norm(11)

        @block.vector
        def _(dve):
            steps = [0]
            V = nc.vector

            def step(ins):
                steps[0] += 1
                ins.then_inc(dve_step, 1)
                dve.wait_ge(dve_step, steps[0])

            n = "vec"
            bank = A.full(dve, n)
            for i, rows in enumerate((V0_ROWS, V1_ROWS, V2_ROWS, V3_ROWS)):
                ins = V.tensor_copy(vec[:, i, 0:rows], bank[:, i * P:i * P + rows])
            A.free(n, ins)
            A.moved(dve, n)

            def norm(n, gains=None):
                N = norms[n]
                nt = N["nt"]
                if n == 11:
                    dve.wait_ge(root_ready, 1)
                else:
                    A.moved(dve, ("ss", n))
                step(V.reciprocal(rstd[:, 0:T], rstd[:, 0:T]))
                step(V.tensor_tensor(N["dst"], N["src"], over(rstd[:, 0:T], nt), ALU.mult))
                for k in range(nt):
                    y = N["dst"][:, k, :]
                    if N["shift"] is None:
                        ins = V.tensor_scalar(y, y, N["gain"][:, k:k + 1], None, ALU.mult)
                    else:
                        ins = V.tensor_scalar(y, y, N["gain"][:, k:k + 1], N["shift"][:, k:k + 1], ALU.mult, ALU.add)
                    ins.then_inc(norm_out, 1)

            def ada(part, u):
                n = ("ada", part, u)
                bank = C.full(dve, n)
                c = slice(2 * u, 2 * u + 2)
                if part == 0 and u < 8:
                    b = v(0, V_BMOD + 2 * u, 2).rearrange("p (a b) -> p a b", b=1).to_broadcast([P, 2, 2])
                    ins = V.tensor_tensor(m1[:, c, :], bank[:, 0:4].rearrange("p (a b) -> p a b", a=2), b, ALU.add)
                elif part == 0:
                    ins = V.tensor_tensor(m1[:, c, 0], bank[:, 0:2], v(0, V_BMOD + 2 * u, 2), ALU.add)
                else:
                    ins = V.tensor_tensor(m2[:, part - 1, c], bank[:, 0:2], v(3, V_BADA + 48 * (part - 1) + 2 * u, 2), ALU.add)
                C.free(n, ins)

            def gain(i, scale, g):
                return V.scalar_tensor_tensor(out=amul[:, i, :], in0=scale, scalar=1.0, in1=g, op0=ALU.add, op1=ALU.mult)

            for u in range(8):
                ada(0, u)
            C.moved(dve, ("ada", 0, 7))
            gain(0, m1[:, 8:16, 0], v(0, V_N1, 8))
            step(gain(1, m1[:, 8:16, 1], v(0, V_N1, 8)))
            norm(0)
            norm(1)

            def side_taps(y, p, w0, w2, last):
                for i, (yy, pp) in enumerate(zip(y, p)):
                    ins = V.scalar_tensor_tensor(out=yy[..., 1:T], in0=pp[..., 0:T - 1], scalar=w0[i], in1=yy[..., 1:T],
                                                 op0=ALU.mult, op1=ALU.add)
                step(ins)
                for i, (yy, pp) in enumerate(zip(y, p)):
                    ins = V.scalar_tensor_tensor(out=yy[..., 0:T - 1], in0=pp[..., 1:T], scalar=w2[i], in1=yy[..., 0:T - 1],
                                                 op0=ALU.mult, op1=ALU.add)
                last(ins)

            for i in range(12):
                nseg = 1 if i < 4 else 2
                n = ("d", i)
                dve.wait_ge(centre_ready, i + 1)
                bank = A.full(dve, n)
                y = ybuf[:, i % 4, 0:nseg * T].rearrange("p (a b) -> p a b", a=nseg)
                side_taps([y], [bank[:, 0:nseg * T].rearrange("p (a b) -> p a b", a=nseg)],
                          [v(0, V_CONV + i)], [v(0, V_CONV + 24 + i)], lambda ins: A.free(n, ins))

            bank = A.full(dve, "ab")
            dve.wait_ge(gc_landed, 64)
            bias = gconst[:, 1, :].rearrange("p (a d h) -> p a d h", a=1, d=2).to_broadcast([P, 4, 2, 4])
            ins = V.tensor_tensor(gates[:, G_T0, :].rearrange("p (d t h) -> p t d h", d=2, t=4),
                                  bank[:, 0:64].rearrange("p (t x d h) -> p t x d h", t=4, x=2, d=2)[:, :, 0, :, :],
                                  bias, ALU.add)
            A.free("ab", ins)
            A.moved(dve, "ab", 1)
            V.scalar_tensor_tensor(out=gates[:, G_T1, :], in0=gates[:, G_T0, :], scalar=-1.0, in1=gates[:, G_T0, :],
                                   op0=ALU.mult, op1=ALU.max).then_inc(sp_abs, 1)
            dve.wait_ge(sp_ln, 1)
            V.tensor_scalar(gates[:, G_EA, 0:8], gates[:, G_EA, 0:8], -1.0, None, ALU.mult)
            step(V.scalar_tensor_tensor(out=gates[:, G_T0, :], in0=gates[:, G_T0, :], scalar=0.0, in1=gates[:, G_T1, :],
                                        op0=ALU.max, op1=ALU.add))
            ea = gates[:, G_EA, 0:8].rearrange("p (d a h) -> p d a h", d=2, a=1).to_broadcast([P, 2, 4, 4])
            V.tensor_tensor(gates[:, G_G, :].rearrange("p (d t h) -> p d t h", d=2, t=4),
                            gates[:, G_T0, :].rearrange("p (d t h) -> p d t h", d=2, t=4), ea, ALU.mult).then_inc(g_ready, 1)

            for i in range(8):
                wd = T if i < 4 else 512
                r = hroot[:, i % 2, 0:wd]
                A.moved(dve, ("l2", i))
                step(V.reciprocal(r, r))
                x = qF[:, i, :] if i < 4 else kF[:, i - 4, :]
                V.tensor_tensor(x, x, r, ALU.mult).then_inc(l2_ready, 1)

            pair = lambda ap: ap.rearrange("p a b -> p (a b)")
            for j in range(3):
                A.moved(dve, ("an", j))
                r = hroot[:, j, :] if j < 2 else kroot
                step(V.reciprocal(r, r))
                x = pair(qA[:, 2 * j:2 * j + 2, :]) if j < 2 else kA[:, :]
                V.scalar_tensor_tensor(out=x, in0=x, scalar=v(0, V_QG if j < 2 else V_KG), in1=r,
                                       op0=ALU.mult, op1=ALU.mult).then_inc(qk_normed, 1)

            def rotary(rg, n, x, cos, sin, tmp, signal):
                m = x.shape[1]
                bank = rg.full(dve, n)
                A.free(n, V.tensor_tensor(tmp, bank[:, 0:m * T].rearrange("p (a b) -> p a b", a=m), over(sin, m), ALU.mult))
                step(V.tensor_tensor(x, x, over(cos, m), ALU.mult))
                V.tensor_tensor(x, x, tmp, ALU.add).then_inc(signal, 1)
            dve.wait_ge(con1_landed, 16)
            for j in range(3):
                x = qA[:, 2 * j:2 * j + 2, :] if j < 2 else kA[:, 0:T].rearrange("p (a b) -> p a b", a=1)
                m = x.shape[1]
                tmp = atmp[:, j % 2, 0:m * T].rearrange("p (a b) -> p a b", a=m)
                rotary(A, ("rot", j), x, c_one("cos", T), c_one("sin", T), tmp, rope_done)

            def attention(tag, base, keys, scaled, pbuf, fill, mask=None):
                def maxima(u):
                    n = keys(u)
                    st = stat[:, u % 4, :]
                    name = (tag, "s", u)
                    bank = B.full(dve, name)
                    if scaled:
                        p = pbuf[:, u % 3, :]
                        if u >= 3:
                            A.full(dve, (tag, "pt", u - 3))
                        if n > P:
                            V.tensor_scalar(p[:, 0:n - P], bank[:, 0:n - P], HD ** -0.5, None, ALU.mult)
                        ins = V.scalar_tensor_tensor(out=p[:, n - P:n], in0=bank[:, n - P:n], scalar=HD ** -0.5,
                                                     in1=mask, op0=ALU.mult, op1=ALU.add)
                        B.free(name, ins)
                        B.moved(dve, name)
                        step(V.tensor_reduce(st[:, 0:1], p[:, 0:n], AX_X, ALU.max))
                        V.tensor_scalar(st[:, 1:2], st[:, 0:1], -1.0, None, ALU.mult).then_inc(max_ready, 1)
                    else:
                        step(V.tensor_reduce(st[:, 0:1], bank[:, 0:n], AX_X, ALU.max))
                        V.tensor_scalar(st[:, 1:2], st[:, 0:1], -HD ** -0.5, None, ALU.mult).then_inc(max_ready, 1)

                def divide(u):
                    n = keys(u)
                    st = stat[:, u % 4, :]
                    if scaled:
                        dve.wait_ge(exp_done, base + u + 1)
                    else:
                        B.moved(dve, (tag, "s", u))
                    step(V.reciprocal(st[:, 3:4], st[:, 2:3]))
                    p = pbuf[:, u % 3, 0:n]
                    V.tensor_scalar(p, p, st[:, 3:4], None, ALU.mult).then_inc(prob_ready, 1)
                for i in range(2 * HQ + 1):
                    if i < 2 * HQ:
                        maxima(i)
                    if i:
                        divide(i - 1)
                    if i < 2 * HQ:
                        for f in fill(i):
                            ada(*f)
            attention("a1", 0, lambda u: 512, False, prob, lambda u: fills["att", u])
            norm(2)

            bank = A.full(dve, "gc")
            V.tensor_copy(gates[:, G_CUM, :], bank[:, 0:32])
            V.tensor_scalar(gates[:, G_NCUM, :], bank[:, 0:32], -1.0, None, ALU.mult)
            A.free("gc", V.tensor_copy(gates[:, G_TOT, :], bank[:, 32:64]))
            A.moved(dve, "gc")
            V.tensor_tensor(gates[:, G_T0, :], gates[:, G_TOT, :], gates[:, G_CUM, :], ALU.subtract).then_inc(tmg_ready, 1)
            dve.wait_ge(gate_ready, 1)
            V.tensor_scalar(gates[:, G_NEG, :], gates[:, G_EG, :], -1.0, None, ALU.mult).then_inc(ngl_ready, 1)

            heads = lambda ap: ap.rearrange("p (a b) -> p a b", a=4)
            for s in range(4):
                for d in range(2):
                    g, tt = 2 * s + d, TILE[d][s]
                    way = ("fwd", "bwd")[d]
                    bank = A.full(dve, ("gb", g))
                    ins = V.scalar_tensor_tensor(out=heads(dec[:, d, :]), in0=heads(bank[:, :]), scalar=-1.0,
                                                 in1=over(c_one("strict_" + way), 4), op0=ALU.mult, op1=ALU.add)
                    if tt < 2:
                        ins = V.tensor_tensor(heads(ATm[:, d, :]), heads(bank[:, :]), over(c_one("incl_" + way), 4), ALU.add)
                    A.free(("gb", g), ins)
                for d in range(2):
                    g, tt = 2 * s + d, TILE[d][s]
                    dve.wait_ge(dec_ready, g + 1)
                    bank = A.full(dve, ("kk", g))
                    for h in range(4):
                        c = slice(h * P, (h + 1) * P)
                        ins = V.scalar_tensor_tensor(out=dec[:, d, c], in0=bank[:, c], scalar=gcol(G_BETA, d, tt, h),
                                                     in1=dec[:, d, c], op0=ALU.mult, op1=ALU.mult)
                    A.free(("kk", g), ins)
                    if tt < 2:
                        dve.wait_ge(att_ready, g - 3)
                        n = ("kq", g)
                        B.free(n, V.tensor_tensor(ATm[:, d, :], B.full(dve, n)[:, :], ATm[:, d, :], ALU.mult))
                for lv in range(1, 7):
                    for f in fills["gdn", s, lv][0:1]:
                        ada(*f)
                    for d in range(2):
                        g, tt = 2 * s + d, TILE[d][s]
                        if lv < 6:
                            n = ("dt", g, lv)
                            A.free(n, V.tensor_tensor(Tm[:, d, :], Tm[:, d, :], A.full(dve, n)[:, :], ALU.subtract))
                        n = ("dtt", g, lv)
                        A.free(n, V.tensor_tensor(TTm[:, d, :], TTm[:, d, :], A.full(dve, n)[:, :], ALU.subtract))
                        if lv == 6:
                            A.moved(dve, n)
                            for h in range(4):
                                c = slice(h * P, (h + 1) * P)
                                ins = V.tensor_scalar(TTm[:, d, c], TTm[:, d, c], gcol(G_BETA, d, tt, h), None, ALU.mult)
                            ins.then_inc(ttb_ready, 1)
                    for f in fills["gdn", s, lv][1:2]:
                        ada(*f)
                for d in range(2):
                    g, tt = 2 * s + d, TILE[d][s]
                    if tt < 2:
                        n = ("og", g)
                        bank = B.full(dve, n)
                        o = oG[:, :, tt * P:(tt + 1) * P]
                        if s == 2:
                            ins = V.tensor_copy(o, heads(bank[:, :]))
                        else:
                            B.moved(dve, ("og", 5 - d))
                            ins = V.tensor_tensor(o, heads(bank[:, :]), o, ALU.add)
                        B.free(n, ins)
                    if s < 3:
                        n = ("st", g)
                        bank = A.full(dve, n)
                        if s == 0:
                            ins = V.tensor_copy(S[:, d, :], bank[:, :])
                        else:
                            A.moved(dve, ("st", g - 2))
                            for h in range(4):
                                c = slice(h * P, (h + 1) * P)
                                ins = V.scalar_tensor_tensor(out=S[:, d, c], in0=S[:, d, c], scalar=gcol(G_DL, d, tt, h),
                                                             in1=bank[:, c], op0=ALU.mult, op1=ALU.add)
                        A.free(n, ins)
            gain(2, m1[:, 32:40, 0], v(0, V_N2, 8))
            for l in range(2):
                gain(3 + 2 * l, m2[:, l, 8:16], v(1, V_NMIX + 8 * l, 8))
                ins = gain(4 + 2 * l, m2[:, l, 32:40], v(1, V_NFFN + 8 * l, 8))
            step(ins)

            def head_norm(j, o, gains, gate, dst):
                for i in range(2):
                    A.moved(dve, ("hn", j, i))
                    step(V.reciprocal(hroot[:, i, :], hroot[:, i, :]))
                    for h in (2 * i, 2 * i + 1):
                        ins = V.scalar_tensor_tensor(out=o[:, h, :], in0=o[:, h, :], scalar=gains(h),
                                                     in1=hroot[:, i, (h % 2) * T:(h % 2 + 1) * T], op0=ALU.mult, op1=ALU.mult)
                    step(ins)
                    for h in (2 * i, 2 * i + 1):
                        V.tensor_tensor(dst[:, 4 + h, :], o[:, h, :], gate[:, h, :], ALU.mult).then_inc(hn_out, 1)
            A.moved(dve, ("z", 3))
            head_norm(0, oG, lambda h: v(0, V_GDNG), zs, mixT)

            def residual(jobs, gate):
                for dt, (rg, name, part) in enumerate(jobs):
                    bank = rg.full(dve, name)
                    ins = V.scalar_tensor_tensor(out=xT[:, dt, :], in0=bank[:, part * T:(part + 1) * T],
                                                 scalar=gate[:, dt:dt + 1], in1=xT[:, dt, :], op0=ALU.mult, op1=ALU.add)
                    if dt == KT - 1 or jobs[dt + 1][1] != name:
                        rg.free(name, ins)

            def acc_jobs(tag):
                return [(B if dt < 6 else C, (tag, "acc", dt // 2), dt % 2) for dt in range(KT)]
            residual([(A, ("xo1", dt), 0) for dt in range(KT)], m1[:, 16:24, 0])
            norm(3)
            for f in range(FT + 1):
                if f < FT:
                    n = ("ffn1", "gu", f)
                    bank = A.full(dve, n)
                    dve.wait_ge(centre_ready, 12 + f + 1)
                    y = yc[:, f % 3, :]
                    side_taps([y[:, 0:T], y[:, T:512]], [bank[:, 0:T], bank[:, T:512]],
                              [v(1, V_FW01 + f), v(1, V_FW01 + FT + f)], [v(2, V_FW2 + f), v(2, V_FW2 + FT + f)],
                              lambda ins: A.free(n, ins))
                if f:
                    y = yc[:, (f - 1) % 3, :]
                    dve.wait_ge(silu_ready, f)
                    V.tensor_tensor(gT[:, (f - 1) % 4, :], y[:, 0:T], y[:, T:512], ALU.mult).then_inc(gT_ready, 1)
            residual(acc_jobs("ffn1"), m1[:, 40:48, 0])
            norm(4)

            dve.wait_ge(con2_landed, 16)
            for l in range(2):
                n0 = 5 + 3 * l
                norm(n0)
                for j in range(4):
                    x = (qR if j < 2 else kR)[:, 2 * (j % 2):2 * (j % 2) + 2, :]
                    rotary(A, (l, "rr", j), x, c_two("cos", T), c_two("sin", T),
                           rtmp[:, j % 2, :].rearrange("p (a b) -> p a b", a=2), rrope)
                attention(("a2", l), 16 * l, lambda u: (u % 2 + 1) * P, True, prob2, lambda u: [], c_two("causal"))
                norm(n0 + 1)
                for h in range(4):
                    n = (l, "rs", h)
                    B.free(n, V.tensor_tensor(AR[:, h % 2, 0:384], B.full(dve, n)[:, 0:384],
                                              c_two("ret", 384, h * 384), ALU.mult))
                for i in range(4):
                    A.moved(dve, (l, "gr", i))
                head_norm(1 + l, oR, lambda h: v(3, V_RETG + 4 * l + h), sgr, mix2)
                residual([(A, (("xo2", l), dt), 0) for dt in range(KT)], m2[:, l, 16:24])
                norm(n0 + 2)
                if l == 0:
                    for f in range(FT):
                        n = ("ffn2", "gu", f)
                        bank = A.full(dve, n)
                        dve.wait_ge(silu_ready, FT + f + 1)
                        A.free(n, V.tensor_tensor(gT[:, f % 4, :], yc[:, f % 3, 0:T], bank[:, T:512], ALU.mult))
                    residual(acc_jobs("ffn2"), m2[:, 0, 40:48])

            bank = A.full(dve, "logits")
            A.free("logits", V.tensor_copy(rout[:, 0:2, :], bank[:, 0:16].rearrange("p (a b) -> p a b", a=2)))
            A.moved(dve, "logits")
            R = lambda i, tt, a=0, b=8: rout[:, i + tt, a:b]
            both = range(TT)
            for tt in both:
                ins = V.max(R(2, tt), R(0, tt))
            step(ins)
            for tt in both:
                V.max_index(idx_u[:, tt, :], R(2, tt), R(0, tt))
                ins = V.tensor_tensor(R(12, tt, 0, 1), R(2, tt, 0, 1), R(2, tt, 1, 2), ALU.subtract)
            ins.then_inc(top_ready, 1)
            dve.wait_ge(top_ready, 1)
            for tt in both:
                ins = V.tensor_copy(R(6, tt), idx_u[:, tt, :])
            step(ins)
            for tt in both:
                V.tensor_scalar(R(8, tt), c_all("iota", 8), R(6, tt, 0, 1), None, ALU.is_equal)
                ins = V.tensor_scalar(R(10, tt), c_all("iota", 8), R(6, tt, 1, 2), None, ALU.is_equal)
            step(ins)
            for tt in both:
                ins = V.tensor_tensor(R(4, tt), R(8, tt), R(10, tt), ALU.add)
            ins.then_inc(sel_ready, 1)
            dve.wait_ge(wt_ready, 1)
            for tt in both:
                ins = V.tensor_scalar(R(16, tt), R(8, tt), R(14, tt, 0, 1), None, ALU.mult)
            step(ins)
            for tt in both:
                ins = V.scalar_tensor_tensor(out=R(16, tt), in0=R(10, tt), scalar=R(14, tt, 1, 2), in1=R(16, tt),
                                             op0=ALU.mult, op1=ALU.add)
            step(ins)
            dve.wait_ge(sel_ready, 1)
            bank = A.full(dve, "pos")
            for tt in both:
                V.scalar_tensor_tensor(out=R(18, tt), in0=bank[:, tt * 8:(tt + 1) * 8], scalar=1.0, in1=R(4, tt),
                                       op0=ALU.add, op1=ALU.mult)
            A.free("pos", V.tensor_copy(cnt_i[:, :], bank[:, 16:24]))
            A.moved(dve, "pos")
            for tt in both:
                ins = V.tensor_scalar(R(18, tt), R(18, tt), -1.0, None, ALU.add)
            step(ins)
            for e in range(NE):
                for tt in both:
                    V.tensor_scalar(Pg[:, tt, e, :], c_all("iota", 256), R(18, tt, e, e + 1), None, ALU.is_equal)
                if e >= 2:
                    A.full(dve, ("pwT", e - 2))
                for tt in both:
                    ins = V.tensor_scalar(Pw[:, e % 2, tt * 256:(tt + 1) * 256], c_all("iota", 256), R(18, tt, e, e + 1),
                                          R(16, tt, e, e + 1), ALU.is_equal, ALU.mult)
                ins.then_inc(pw_ready, 1)
            V.memset(facc, 0.0).then_inc(moved, 2)
            V.memset(stat[:, 0, 0:1], 0.0).then_inc(gated, 2)

            def expert(e, ns):
                for j in range(KT):
                    dve.wait_ge(xj_full, e * 16 + (j + 1))
                    V.tensor_copy(xg[:, j, 0:ns], banks[2 + j % 2][:, 0:ns]).then_inc(moved, 1)
                for f in range(FT):
                    dve.wait_ge(sge_ready, e * FT + (f + 1))
                    V.tensor_tensor(gTe[:, f % 4, 0:ns], sge[:, f % 2, 0:ns], banks[f % 2][:, ns:2 * ns],
                                    ALU.mult).then_inc(gated, 1)
                for j in range(KT):
                    dve.wait_ge(xj_full, e * 16 + (KT + j + 1))
                    V.tensor_tensor(facc[:, j, :], banks[2 + j % 2][:, 0:T], facc[:, j, :], ALU.add).then_inc(moved, 1)

            with dve.Fori(0, NE) as e:
                count = dve.value_load(cnt_i[0:1, bass.ts(e, 1)], min_val=0, max_val=T)
                with dve.If(count > NARROW):
                    expert(e, T)
                with dve.Else():
                    expert(e, NARROW)
                dve.nop()
            dve.wait_ge(moved, 16 * NE + 2)
            for dt in range(KT):
                V.scalar_tensor_tensor(out=xT[:, dt, :], in0=facc[:, dt, :], scalar=m2[:, 1, 40 + dt:41 + dt],
                                       in1=xT[:, dt, :], op0=ALU.mult, op1=ALU.add).then_inc(x_updated, 1)
            norm(11)
            for i in range(4):
                dve.wait_ge(fin_ready, i + 2)
                V.tensor_copy(outT[:, i // 2, (i % 2) * 512:(i % 2 + 1) * 512], banks[4 + i][:, :]).then_inc(out_ready, 1)

        @block.gpsimd
        def _(pool):
            steps = [0]
            G = nc.gpsimd

            def step(ins):
                steps[0] += 1
                ins.then_inc(pool_step, 1)
                pool.wait_ge(pool_step, steps[0])
            heads = lambda ap: ap.rearrange("p (a b) -> p a b", a=4)
            pool.wait_ge(con_landed, 16)
            pool.wait_ge(con1_landed, 16)
            pool.wait_ge(ngl_ready, 1)
            for h in range(4):
                A.moved(pool, ("ktm", h))
            for s in range(4):
                for d in range(2):
                    g, tt = 2 * s + d, TILE[d][s]
                    if s:
                        A.full(pool, ("st", g - 2))
                    for h in range(4):
                        c = slice(h * P, (h + 1) * P)
                        G.tensor_scalar(kbe[:, d, c], k_tm[:, tt, h, :], gcol(G_NEG, d, tt, h), None, ALU.mult)
                        ins = G.tensor_scalar(kdec[:, d, c], k_tm[:, tt, h, :], gcol(G_KD, d, tt, h), None, ALU.mult)
                    ins.then_inc(kb_ready, 1)
                for d in range(2):
                    g, tt = 2 * s + d, TILE[d][s]
                    nb, eye = over(c_one("level"), 4), over(ident, 4)
                    A.moved(pool, ("kk", g))
                    G.tensor_tensor(heads(Tm[:, d, :]), heads(dec[:, d, :]), nb, ALU.mult)
                    A.moved(pool, ("lt", g))
                    step(G.tensor_tensor(heads(TTm[:, d, :]), heads(LTm[:, d, :]), nb, ALU.mult))
                    G.tensor_tensor(heads(Tm[:, d, :]), heads(Tm[:, d, :]), eye, ALU.add)
                    G.tensor_tensor(heads(TTm[:, d, :]), heads(TTm[:, d, :]), eye, ALU.add).then_inc(seed_ready, 1)
                for lv in range(1, 7):
                    for d in range(2):
                        g, tt = 2 * s + d, TILE[d][s]
                        if lv > 2:
                            A.full(pool, ("m1", g, lv - 2))
                        G.tensor_tensor(heads(LsT[:, 2 * d + lv % 2, :]), heads(LTm[:, d, :]),
                                        over(c_one("level", P, lv), 4), ALU.mult).then_inc(ls_ready, 1)
                        if lv == 2 and tt < 2:
                            A.moved(pool, ("gb", g))
                            G.tensor_tensor(heads(qdec[:, d, :]), qF[:, :, tt * P:(tt + 1) * P], heads(egb[:, d, :]),
                                            ALU.mult).then_inc(qdec_ready, 1)

        @block.sync
        def _(sp):
            sp.dma_start(con[:, :], t["constants"][:, 0:C_ALL_W]).then_inc(con_landed, 16)
            sp.dma_start(xraw[:, 0:2, :], t["x"][0].rearrange("(a p) n -> p a n", p=P)).then_inc(x_landed, 16)
            sp.dma_start(xraw[:, 2:4, :], t["ctx"][0].rearrange("(a p) n -> p a n", p=P)).then_inc(x_landed, 16)
            for k, (name, ap) in enumerate(units):
                if k >= RING:
                    sp.wait_ge(unit_used, k - RING + 1)
                n = ap.shape[1]
                sp.dma_start(ring[:, k % RING, :].rearrange("p (a b) -> p a b", a=n), ap).then_inc(landed[k % RING], 16)
            src = dict(g=t["moe_w_gate_2"], u=t["moe_w_up_2"], d=t["moe_w_down_2"])
            with sp.Fori(0, NE) as e:
                for (m, c), j in e_order.items():
                    k = U0 + j
                    w = src[m][0][e, :, :]
                    ap = w_rows(w, c) if m == "d" else w_cols(w, c)
                    sp.wait_ge(unit_used, e * EU + (k - RING + 1))
                    sp.dma_start(ring[:, k % RING, :].rearrange("p (a b) -> p a b", a=ap.shape[1]), ap).then_inc(landed[k % RING], 16)
            for tt in range(TT):
                sp.wait_ge(out_ready, 2 * tt + 2)
                sp.dma_start(out[0, tt * P:(tt + 1) * P, :], outT[:, tt, :]).then_inc(out_landed, 16)
            sp.wait_ge(out_landed, 16 * TT)


_INS = ["x", "c", "ctx", "c_ctx", "w_mod", "b_mod", "norm1_g", "w_in", "q_norm_g", "k_norm_g", "attn_out_g",
        "conv_qkv_w", "a_log_f", "a_log_b", "dt_bias_f", "dt_bias_b", "gdn_norm_g", "w_out", "norm2_g", "w_up",
        "ffn_conv_w", "ffn_conv_b", "w_down", "final_norm_g", "c_2", "norm_mix_g_2", "norm_ffn_g_2", "ada_w_2",
        "ada_b_2", "w_in_2", "w_out_2", "att_out_g_2", "ret_out_g_2", "ffn_w_gate_2", "ffn_w_up_2",
        "ffn_w_down_2", "router_w_2", "moe_w_gate_2", "moe_w_up_2", "moe_w_down_2", "final_norm_g_2"]


def kernel(**inputs):
    import concourse.bacc as _bacc
    from concourse.bass_utils import run_bass_kernel_spmd as _run

    nc = _bacc.Bacc("TRN2", target_bir_lowering=False, num_devices=1, dynamic_dma_scratch_size=1024)
    arrays, t = {}, {}
    for name in _INS + ["constants"]:
        a = shape_constants() if name == "constants" else np.ascontiguousarray(inputs[name])
        arrays[f"in_{name}_dram"] = a
        t[name] = nc.dram_tensor(f"in_{name}_dram", a.shape, mybir.dt.from_np(a.dtype), kind="ExternalInput").ap()
    out = nc.dram_tensor("out_0_dram", (1, T, D), F32, kind="ExternalOutput").ap()
    build(nc, t, out)
    r = _run(nc, [arrays], core_ids=[0])
    return r.results[0]["out_0_dram"]
```

```python
from contextlib import ExitStack

import numpy as np

import concourse.bass as bass
from concourse import mybir

ALU = mybir.AluOpType
ACT = mybir.ActivationFunctionType
F32 = mybir.dt.float32
I32 = mybir.dt.int32
U32 = mybir.dt.uint32
AX_X = mybir.AxisListType.X

P = 128
D = 1024
KT = D // P
T = 256
TT = T // P
EPS = 1e-6
NEG = -1e30

HD = 64
GH = 4
MIX_T = 4
GRID_W = 64
FF = 2816
UW = 256
FC = FF // UW
FT = FF // P
NE = 8
RING = 11
RING1 = 8
NARROW = 128

C_ALL = dict(ident=0, ones=128, ustrict=256, iota=384)
C_ALL_W = 640
C_ONE = dict(ones64=0, rot64=128, sel=256, u_fwd=512, u_bwd=640, strict_fwd=768, strict_bwd=896,
             incl_fwd=1024, incl_bwd=1152, level=1280, cos=2176, sin=2432)
C_ONE_W = 2688
C_TWO = dict(rot128=0, cos=128, sin=384, ret=640, causal=2176)
C_TWO_W = 2304

V_C, V_CCTX, V_BMOD, V_N1, V_ATTG, V_GDNG, V_N2, V_CONV, V_QG, V_KG = 0, 8, 16, 64, 72, 76, 77, 85, 121, 122
V0_ROWS = 123
V_FW01, V_C2, V_NMIX, V_NFFN = 0, 88, 96, 112
V1_ROWS = 128
V_FW2, V_FB, V_FIN1, V_FIN2 = 0, 44, 88, 96
V2_ROWS = 104
V_BADA, V_ATTG2, V_RETG = 0, 96, 104
V3_ROWS = 112


def shape_constants():
    i = np.arange(P)
    row, col = i[:, None], i[None, :]
    f = np.float32
    allc = np.zeros((P, C_ALL_W), f)
    allc[:, 0:128] = np.eye(P)
    allc[:, 128:256] = 1.0
    allc[:, 256:384] = row < col
    allc[:, 384:640] = np.arange(256)[None, :]

    def rotation(hd):
        r = np.zeros((P, P), f)
        for m in range(P):
            if m % hd < hd // 2:
                r[m + hd // 2, m] = -1.0
            else:
                r[m - hd // 2, m] = 1.0
        return r

    one = np.zeros((P, C_ONE_W), f)
    c = C_ONE
    one[:, c["ones64"]:c["ones64"] + P] = (row // HD) == (col // HD)
    one[:, c["rot64"]:c["rot64"] + P] = rotation(HD)
    for kv in range(2):
        one[:, c["sel"] + kv * P:c["sel"] + (kv + 1) * P] = row == (HD * kv + col % HD)
    one[:, c["u_fwd"]:c["u_fwd"] + P] = row <= col
    one[:, c["u_bwd"]:c["u_bwd"] + P] = row >= col
    one[:, c["strict_fwd"]:c["strict_fwd"] + P] = np.where(row > col, 0, NEG)
    one[:, c["strict_bwd"]:c["strict_bwd"] + P] = np.where(row < col, 0, NEG)
    one[:, c["incl_fwd"]:c["incl_fwd"] + P] = np.where(row <= col, 0, NEG)
    one[:, c["incl_bwd"]:c["incl_bwd"] + P] = np.where(row >= col, 0, NEG)
    for lv in range(7):
        s = 1 << lv
        pair = (row // (2 * s) == col // (2 * s)) & (row // s != col // s)
        one[:, c["level"] + lv * P:c["level"] + (lv + 1) * P] = pair * (-1.0 if lv == 0 else 1.0)
    t = np.arange(T)
    quarter = HD // 4
    inv = 10000.0 ** (-np.arange(quarter, dtype=f) / f(quarter))
    inv = inv.astype(f)
    ang = np.concatenate([(t // GRID_W).astype(f)[:, None] * inv, (t % GRID_W).astype(f)[:, None] * inv], 1)
    lane = (i % HD) % (HD // 2)
    one[:, c["cos"]:c["cos"] + T] = np.cos(ang).T[lane]
    one[:, c["sin"]:c["sin"] + T] = np.sin(ang).T[lane]

    two = np.zeros((P, C_TWO_W), f)
    c = C_TWO
    two[:, 0:P] = rotation(P)
    half = P // 2
    inv = (10000.0 ** (-np.arange(half, dtype=f) / f(half))).astype(f)
    ang = t.astype(f)[:, None] * inv[None, :]
    two[:, c["cos"]:c["cos"] + T] = np.cos(ang).T[i % half]
    two[:, c["sin"]:c["sin"] + T] = np.sin(ang).T[i % half]
    for h in range(GH):
        lg = np.log(1.0 - 2.0 ** (-5.0 - h))
        for b, (j0, i0, n) in enumerate(((0, 0, 256), (128, 128, 128))):
            dist = (i0 + np.arange(n))[None, :] - (j0 + i)[:, None]
            m = np.where(dist >= 0, np.exp(np.maximum(dist, 0) * lg), 0.0) * P ** -0.5
            at = c["ret"] + h * 384 + b * 256
            two[:, at:at + n] = m
    two[:, c["causal"]:c["causal"] + P] = np.where(col <= row, 0, NEG)
    return np.concatenate([allc, one, two], 1)


class BankRing:

    def __init__(self, banks, full, free):
        self.banks, self.sem_full, self.sem_free = banks, full, free
        self.taken = 0
        self.uses = [0] * len(banks)
        self.frees = [0] * len(banks)
        self.where = {}

    def take(self, pe, name, readers=1):
        b = self.taken % len(self.banks)
        if self.frees[b]:
            pe.wait_ge(self.sem_free[b], self.frees[b])
        self.taken += 1
        self.uses[b] += 1
        self.frees[b] += readers
        self.where[name] = (b, self.uses[b], self.frees[b])
        return self.banks[b]

    def done(self, name, ins):
        ins.then_inc(self.sem_full[self.where[name][0]], 1)

    def full(self, eng, name):
        b, n, _ = self.where[name]
        eng.wait_ge(self.sem_full[b], n)
        return self.banks[b]

    def free(self, name, ins):
        ins.then_inc(self.sem_free[self.where[name][0]], 1)

    def moved(self, eng, name, but=0):
        b, _, n = self.where[name]
        eng.wait_ge(self.sem_free[b], n - but)

    def all_free(self, pe):
        for b, n in enumerate(self.frees):
            if n:
                pe.wait_ge(self.sem_free[b], n)


def build(nc, t, out):
    ctx = ExitStack()
    with ctx:
        def sb(name, shape, dt=F32):
            return ctx.enter_context(nc.sbuf_tensor(name, shape, dt))

        def sem(name):
            return ctx.enter_context(nc.semaphore(name))

        banks = [ctx.enter_context(nc.psum_tensor(f"bank{b}", [P, 512], F32)) for b in range(8)]

        ring = sb("ring", [P, RING, KT * UW])
        con = sb("con", [P, C_ALL_W])
        con2 = sb("con2", [P, C_ONE_W])
        vec = sb("vec", [P, 4, P])
        xT = sb("xT", [P, KT, T])[:, :, :]
        sq = sb("sq", [P, 2048])
        rstd = sb("rstd", [P, T])
        hroot = sb("hroot", [P, 2, 512])
        m1 = sb("m1", [P, 48, 2])
        m2 = sb("m2", [P, 2, 48])
        amul = sb("amul", [P, 7, 8])
        cs = sb("cs", [P, 8, 2])
        cs2 = sb("cs2", [P, 8])
        wab = sb("wab", [P, KT, 16])
        wrt = sb("wrt", [P, KT, NE])
        gconst = sb("gconst", [P, 2, 8])
        gates = sb("gates", [P, 12, 32])
        stat = sb("stat", [P, 4, 4])
        facc2 = sb("facc2", [P, 2, 2, UW])
        ARENA = 23296
        arena = sb("arena", [P, ARENA])

        def at(a, *shape):
            n = int(np.prod(shape))
            assert a + n <= ARENA, (a, n)
            v = arena[:, a:a + n]
            if len(shape) == 2:
                return v.rearrange("p (a b) -> p a b", a=shape[0])
            if len(shape) == 3:
                return v.rearrange("p (a b c) -> p a b c", a=shape[0], b=shape[1])
            return v

        def c_all(name, w=P):
            return con[:, C_ALL[name]:C_ALL[name] + w]

        def c_one(name, w=P, i=0):
            a = C_ONE[name] + i * P
            return con2[:, a:a + w]

        def c_two(name, w=P, i=0):
            a = C_TWO[name] + i
            return con2[:, a:a + w]

        ident, ones = c_all("ident"), c_all("ones")

        def over(ap, n):
            w = ap.shape[-1]
            return ap.rearrange("p (a w) -> p a w", a=1).to_broadcast([ap.shape[0], n, w])

        mixT = at(0, 8, T)
        zs = at(2048, 4, T)
        qF = at(3072, 4, T)
        kF = at(4096, 4, 512)
        k_tm = at(6144, 4, 4, P)
        v_tm = at(8192, 4, 4, P)
        G0 = 10240
        hT = at(G0, KT, 512)
        xraw = at(G0 + 4096, 4, D)
        ctxT = at(G0 + 8192, KT, T)
        vrows = at(G0 + 10240, 512)
        ybuf = at(G0 + 10240, 4, 512)
        qA = at(G0 + 4096, 4, T)
        kA = at(G0 + 7168, 512)
        vA = at(G0 + 6656, 4, P)
        extra = ring[:, RING1:RING, :].rearrange("p a b -> p (a b)")

        def ex(a, n, w):
            return extra[:, a:a + n * w].rearrange("p (a b) -> p a b", a=n)
        kdup = ex(0, 2, 512)
        prob = ex(1024, 3, 512)
        probT = ex(2560, 2, 512)
        oA = ex(3584, 4, T)
        atmp = ex(4608, 2, 512)
        kroot = extra[:, 5632:6144]
        TTm = at(G0 + 0, 8, 512)
        Tm = at(G0 + 4096, 4, 512)
        LTm = at(G0 + 6144, 4, 512)
        dec = at(G0 + 8192, 4, 512)
        kbe = at(G0 + 10240, 2, 512)
        kdec = at(G0 + 11264, 2, 512)
        S = hroot[:, :, :]
        ATm = ex(0, 4, 512)
        qdec = ex(2048, 4, 512)
        nwT = ex(4096, 2, 512)
        vnew = ex(5120, 2, 512)
        egb = sq[:, :].rearrange("p (a b) -> p a b", a=4)
        oG = mixT[:, 4:8, :]
        hF = at(0, KT, T)
        gT = at(2048, 4, T)
        yc = at(3072, 3, 512)
        h2 = at(0, KT, T)
        mix2 = at(2048, 8, T)
        qA2 = at(4096, 4, T)
        kA2 = at(5120, 4, T)
        vA2 = at(6144, 2, 512)
        qR = at(7168, 4, T)
        kR = at(8192, 4, T)
        vR = at(9216, 2, 512)
        sgr = at(10240, 4, T)
        prob2 = at(11264, 3, 512)
        probT2 = at(12800, 2, 512)
        oA2 = at(13824, 4, T)
        rtmp = at(14848, 2, 512)
        AR = at(15872, 2, 512)
        oR = at(16896, 4, T)
        Pg = at(2048, 2, NE, 256)
        PwT = at(6144, 2, NE, 256)
        h_tm = at(10240, 2, D)
        xg = at(12288, KT, 256)
        ye = at(14336, 2, D)
        facc = at(16384, KT, T)
        gTe = at(18432, 4, 256)
        sge = at(19456, 2, 256)
        Pw = at(19968, 2, 512)
        rout = at(20992, 24, 8)
        cnt_i = sb("cnt_i", [P, 8], I32)
        idx_u = sb("idx_u", [P, 2, 8], U32)
        outT = at(20992 + 192, 2, D)

        full = [sem(f"full{b}") for b in range(8)]
        free = [sem(f"free{b}") for b in range(8)]
        landed = [sem(f"landed{s}") for s in range(RING)]
        unit_used = sem("unit_used")
        x_landed, v_landed = sem("x_landed"), sem("v_landed")
        con_landed, con1_landed, con2_landed = sem("con_landed"), sem("con1_landed"), sem("con2_landed")
        gc_landed, wab_landed, wrt_landed = sem("gc_landed"), sem("wab_landed"), sem("wrt_landed")
        out_landed = sem("out_landed")
        dve_step, act_step, pool_step = sem("dve_step"), sem("act_step"), sem("pool_step")
        fill_ready = sem("fill_ready")
        cs_ready, sq_ready, root_ready, norm_out = sem("cs_ready"), sem("sq_ready"), sem("root_ready"), sem("norm_out")
        x_updated = sem("x_updated")
        centre_ready, d_ready = sem("centre_ready"), sem("d_ready")
        sqd_ready, l2_ready = sem("sqd_ready"), sem("l2_ready")
        ansq, qk_normed, rope_done = sem("ansq"), sem("qk_normed"), sem("rope_done")
        max_ready, exp_done, prob_ready = sem("max_ready"), sem("exp_done"), sem("prob_ready")
        sp_abs, sp_ln, g_ready, tmg_ready, gate_ready, ngl_ready = (
            sem("sp_abs"), sem("sp_ln"), sem("g_ready"), sem("tmg_ready"), sem("gate_ready"), sem("ngl_ready"))
        dec_ready, att_ready, kb_ready, seed_ready, ls_ready, ttb_ready, qdec_ready = (
            sem("dec_ready"), sem("att_ready"), sem("kb_ready"), sem("seed_ready"), sem("ls_ready"),
            sem("ttb_ready"), sem("qdec_ready"))
        hn_sq, hn_out = sem("hn_sq"), sem("hn_out")
        silu_ready, gT_ready = sem("silu_ready"), sem("gT_ready")
        rrope, sg_ready = sem("rrope"), sem("sg_ready")
        top_ready, wt_ready, sel_ready, pw_ready = sem("top_ready"), sem("wt_ready"), sem("sel_ready"), sem("pw_ready")
        xj_full, moved, gu_full, gated = sem("xj_full"), sem("moved"), sem("gu_full"), sem("gated")
        sge_ready, ye_ready = sem("sge_ready"), sem("ye_ready")
        out_ready = sem("out_ready")
        fin_ready = sem("fin_ready")

        A = BankRing(banks[0:4], full[0:4], free[0:4])
        B = BankRing(banks[4:7], full[4:7], free[4:7])
        C = BankRing(banks[7:8], full[7:8], free[7:8])

        w_cols = lambda w, u: w[:, u * UW:(u + 1) * UW].rearrange("(k p) n -> p k n", p=P)
        w_rows = lambda w, c: w[c * UW:(c + 1) * UW, :].rearrange("(k p) n -> p k n", p=P)
        units = []

        def add(name, ap):
            units.append((name, ap))

        def add_ffn(tag, gate, up, down, fill=None):
            for f in range(FT + 3):
                if f % 2 and f < FT:
                    add((tag, "g", f // 2), gate(f // 2))
                    add((tag, "u", f // 2), up(f // 2))
                if f and fill:
                    add(*fill(f - 1))
                if f % 2 and 3 <= f < FT + 2:
                    add((tag, "d", (f - 3) // 2), down((f - 3) // 2))

        for u in range(8):
            add(("mod", 0, u), w_cols(t["w_mod"][0], u))
        for u in range(11):
            add(("in1", u), w_cols(t["w_in"][0], u))
        for u in range(8, 24):
            add(("mod", 0, u), w_cols(t["w_mod"][0], u))
        for u in range(4):
            add(("out1", u), w_cols(t["w_out"][0], u))
        K1 = len(units)
        ada2 = lambda l: lambda u: (("mod", 1 + l, u), w_cols(t["ada_w_2"][l], u))
        add_ffn("ffn1", lambda c: w_cols(t["w_up"][0], c), lambda c: w_cols(t["w_up"][0], FC + c),
                lambda c: w_rows(t["w_down"][0], c), ada2(0))
        for l in range(2):
            for u in range(14):
                add(("in2", l, u), w_cols(t["w_in_2"][l], u))
            for u in range(4):
                add(("out2", l, u), w_cols(t["w_out_2"][l], u))
            if l == 0:
                add_ffn("ffn2", lambda c: w_cols(t["ffn_w_gate_2"][0], c), lambda c: w_cols(t["ffn_w_up_2"][0], c),
                        lambda c: w_rows(t["ffn_w_down_2"][0], c), ada2(1))
        U0 = len(units)
        order = {name: k for k, (name, _) in enumerate(units)}
        EU = 3 * FC
        e_order = {}
        for c in range(FC + 1):
            if c < FC:
                e_order["g", c] = len(e_order)
                e_order["u", c] = len(e_order)
            if c >= 1:
                e_order["d", c - 1] = len(e_order)

        slot, turn, need, last = [], [], [], {}
        for k in range(U0 + EU):
            sl = k % RING1 if k < K1 else (k - K1) % RING
            before = last.get(sl)
            slot.append(sl)
            turn.append(1 if before is None else turn[before] + 1)
            need.append(before + 1 if before is not None else order["out1", 0] + 1 if k >= K1 else 0)
            last[sl] = k
        assert all(need[k] == k - RING + 1 for k in range(U0, U0 + EU))

        def v(i, r, n=1):
            return vec[:, i, r:r + n]

        def last_of(*name):
            return lambda eng: (C if name[0] in ("ffn1", "ffn2") else A).moved(eng, name)

        norms = [
            dict(src=xT, nt=8, wait=last_of("xt", 0, 1, 1), gain=amul[:, 0, :], shift=m1[:, 0:8, 0], dst=hT[:, :, 0:T]),
            dict(src=ctxT, nt=8, wait=last_of("xt", 1, 1, 1), gain=amul[:, 1, :], shift=m1[:, 0:8, 1], dst=hT[:, :, T:512]),
            dict(src=oA, nt=4, wait=lambda eng: C.moved(eng, ("a1", "o", 3)), gain=v(0, V_ATTG, 4), shift=None, dst=mixT[:, 0:4, :]),
            dict(src=xT, nt=8, wait=last_of("xo1", 7), gain=amul[:, 2, :], shift=m1[:, 24:32, 0], dst=hF),
            dict(src=xT, nt=8, wait=last_of("ffn1", "acc", 3), gain=v(2, V_FIN1, 8), shift=None, dst=xT),
        ]
        for l in range(2):
            norms += [
                dict(src=xT, nt=8, wait=(lambda eng: eng.wait_ge(norm_out, 36)) if l == 0 else last_of("ffn2", "acc", 3),
                     gain=amul[:, 3 + 2 * l, :], shift=m2[:, l, 0:8], dst=h2),
                dict(src=oA2, nt=4, wait=(lambda l: lambda eng: C.moved(eng, (("a2", l), "o", 3)))(l), gain=v(3, V_ATTG2 + 4 * l, 4), shift=None,
                     dst=mix2[:, 0:4, :]),
                dict(src=xT, nt=8, wait=last_of(("xo2", l), 7), gain=amul[:, 4 + 2 * l, :], shift=m2[:, l, 24:32], dst=hF),
            ]
        norms.append(dict(src=xT, nt=8, wait=lambda eng: eng.wait_ge(x_updated, 8), gain=v(2, V_FIN2, 8), shift=None, dst=xT))
        total = 0
        for n in norms:
            total += n["nt"]
            n["out"] = total
        assert norms[4]["out"] == 36

        def root(n):
            return hroot[:, 0, 0:T] if n == 1 else rstd[:, 0:T]

        TILE = [[2, 3, 0, 1], [3, 2, 1, 0]]

        def gcol(buf, d, tt, h=0, n=1):
            a = (d * 4 + tt) * 4 + h
            return gates[:, buf, a:a + n]
        G_G, G_BETA, G_CUM, G_NCUM, G_TOT, G_EG, G_NEG, G_KD, G_DL, G_T0, G_T1, G_EA = range(12)

        HQ = 8
        GROUPS = [[(s, d) for s in (2 * half, 2 * half + 1) for d in range(2)] for half in range(2)]
        DELTA = [("prepare", 0)]
        for lv in range(1, 7):
            DELTA += [("level", 0, lv), ("fill", lv - 1)]
        DELTA += [("prepare", 1)]
        for lv in range(1, 7):
            DELTA += [("level", 1, lv), ("fill", 5 + lv)]
            if lv in (2, 4):
                DELTA += [("advance", lv // 2 - 1)]
        DELTA += [("fill", 12), ("fill", 13), ("advance", 2), ("fill", 14), ("fill", 15), ("advance", 3), ("fill", 16)]
        SLOTS2 = [("qr", 6, i) for i in range(4)] + [("kr", 8, i) for i in range(4)] + \
                 [("vr", 10, i) for i in range(2)] + [("gr", 12, i) for i in range(4)] + [("rr", 0, i) for i in range(4)]
        block = ctx.enter_context(nc.Block())

        @block.tensor
        def _(pe):
            mm = nc.tensor.matmul
            owed = [0]

            def owe():
                owed[0] += 1

            def pay(ins):
                if owed[0]:
                    ins.then_inc(unit_used, owed[0])
                    owed[0] = 0

            def unit(name):
                k = order[name]
                pe.wait_ge(landed[slot[k]], 16 * turn[k])
                return ring[:, slot[k], :]

            def ada_rows(u):
                w = unit(("mod", 0, u)).rearrange("p (k n) -> p k n", k=KT)
                bank = A.take(pe, ("ada", 0, u))
                for k in range(KT):
                    ins = mm(bank[0:2, 0:UW], cs[:, k, 0:2], w[:, k, :], start=k == 0, stop=k == KT - 1)
                    if k == 0:
                        pay(ins)
                owe()
                A.done(("ada", 0, u), ins)

            fills = [0]

            def fill_sum(rg, part, u):
                pe.wait_ge(fill_ready, fills[0] + 1)
                acc = facc2[:, fills[0] % 2, 0, :]
                fills[0] += 1
                bank = rg.take(pe, ("ada", part, u))
                for j in range(2):
                    ins = mm(bank[:, j:j + 1], acc[:, j * P:(j + 1) * P], ones[:, 0:1], start=True, stop=True)
                    if j == 0:
                        pay(ins)
                owe()
                rg.done(("ada", part, u), ins)

            def norm_sum(n):
                N = norms[n]
                pe.wait_ge(sq_ready, n + 1)
                bank = A.take(pe, ("ss", n))
                for k in range(N["nt"]):
                    ins = mm(bank[:, 0:T], ones, sq[:, k * T:(k + 1) * T], start=k == 0, stop=k == N["nt"] - 1)
                    if k == 0:
                        pay(ins)
                A.done(("ss", n), ins)

            def proj(name, w, j, h, width):
                bank = A.take(pe, name)
                for k in range(KT):
                    ins = mm(bank[:, 0:width], w[:, k, j * P:(j + 1) * P], h[:, k, 0:width],
                             start=k == 0, stop=k == KT - 1)
                    if k == 0:
                        pay(ins)
                A.done(name, ins)

            pe.wait_ge(con_landed, 16)
            pe.wait_ge(x_landed, 32)
            for s in range(2):
                for tt in range(TT):
                    for kg in range(2):
                        bank = A.take(pe, ("xt", s, tt, kg))
                        for k in range(4):
                            ins = nc.tensor.transpose(bank[:, k * P:(k + 1) * P],
                                                      xraw[:, 2 * s + tt, (4 * kg + k) * P:(4 * kg + k + 1) * P], ident)
                        A.done(("xt", s, tt, kg), ins)
            pe.wait_ge(v_landed, 16 * 26)
            bank = A.take(pe, "vec")
            for i, rows in enumerate((V0_ROWS, V1_ROWS, V2_ROWS, V3_ROWS)):
                ins = nc.tensor.transpose(bank[:, i * P:i * P + rows], vrows[0:rows, i * P:(i + 1) * P],
                                          ident[0:rows, 0:rows])
            A.done("vec", ins)
            norm_sum(0)
            norm_sum(1)
            pe.wait_ge(cs_ready, 1)
            for u in range(8):
                ada_rows(u)
            A.moved(pe, ("ada", 0, 7))
            bank = A.take(pe, "adat")
            for j in range(16):
                ins = nc.tensor.transpose(bank[:, 2 * j:2 * j + 2], sq[0:2, j * P:(j + 1) * P], ident[0:2, 0:2])
            A.done("adat", ins)

            def attention(tag, base, scores, values, pbuf, ptbuf):
                def score(u):
                    bank = B.take(pe, (tag, "s", u))
                    l, r, n = scores(u)
                    ins = mm(bank[:, 0:n], l, r, start=True, stop=True)
                    B.done((tag, "s", u), ins)

                def turn(u):
                    nk = scores(u)[2] // P
                    pe.wait_ge(prob_ready, base + u + 1)
                    bank = A.take(pe, (tag, "pt", u))
                    for k in range(nk):
                        ins = nc.tensor.transpose(bank[:, k * P:(k + 1) * P], pbuf[:, u % 3, k * P:(k + 1) * P], ident)
                    A.done((tag, "pt", u), ins)

                def weigh(u):
                    nk = scores(u)[2] // P
                    h, qt = u // 2, u % 2
                    r0 = HD * (h % 2)
                    bank = C.take(pe, (tag, "o", h // 2)) if u % 4 == 0 else C.banks[0]
                    A.moved(pe, (tag, "pt", u))
                    for k in range(nk):
                        ins = mm(bank[r0:r0 + HD, qt * P:(qt + 1) * P], values(u, k), ptbuf[:, u % 2, k * P:(k + 1) * P],
                                 start=k == 0, stop=k == nk - 1)
                    if u % 4 == 3:
                        C.done((tag, "o", h // 2), ins)

                def stage(i):
                    if i < 2 * HQ:
                        score(i)
                    if 2 <= i < 2 * HQ + 2:
                        turn(i - 2)
                    if 3 <= i < 2 * HQ + 3:
                        weigh(i - 3)
                return stage

            def s1(u):
                h, qt = u // 2, u % 2
                r0 = HD * (h % 2)
                return qA[r0:r0 + HD, h // 2, qt * P:(qt + 1) * P], kdup[r0:r0 + HD, h // 4, :], 512

            pe.wait_ge(norm_out, norms[1]["out"])
            w_in = lambda u: unit(("in1", u)).rearrange("p (k n) -> p k n", k=KT)
            for u in range(2):
                for j in range(2):
                    proj(("q", 2 * u + j), w_in(u), j, hT, T)
                owe()
            w = w_in(2)
            proj("k", w, 0, hT, 512)
            bank = A.take(pe, "v")
            for tt in range(4):
                for k in range(KT):
                    ins = mm(bank[:, tt * P:(tt + 1) * P], hT[:, k, tt * P:(tt + 1) * P], w[:, k, P:2 * P],
                             start=k == 0, stop=k == KT - 1)
            A.done("v", ins)
            owe()
            stage = attention("a1", 0, s1, lambda u, k: vA[:, k, HD * (u // 8):HD * (u // 8) + HD], prob, probT)
            for i in range(2 * HQ):
                w = w_in(3 + i // 2)
                if i < 12:
                    proj(("d", i), w, i % 2, hT, T if i < 4 else 512)
                else:
                    proj(("z", i - 12), w, i % 2, hT, T)
                if i % 2:
                    owe()
                if i == 0:
                    pe.wait_ge(con1_landed, 16)
                    pe.wait_ge(ansq, 1)
                    for j in range(3):
                        bank = B.take(pe, ("an", j))
                        ins = mm(bank[:, :], c_one("ones64"), sq[:, j * 512:(j + 1) * 512], start=True, stop=True)
                        B.done(("an", j), ins)
                elif i == 1:
                    for j in range(3):
                        pe.wait_ge(qk_normed, j + 1)
                        bank = B.take(pe, ("rot", j))
                        if j < 2:
                            src = qA[:, 2 * j:2 * j + 2, :].rearrange("p a b -> p (a b)")
                            ins = mm(bank[:, :], c_one("rot64"), src, start=True, stop=True)
                        else:
                            ins = mm(bank[:, 0:T], c_one("rot64"), kA[:, 0:T], start=True, stop=True)
                        B.done(("rot", j), ins)
                elif i == 2:
                    pe.wait_ge(rope_done, 3)
                    for kv in range(2):
                        bank = B.take(pe, ("dup", kv))
                        ins = mm(bank[:, :], c_one("sel", P, kv), kA[:, :], start=True, stop=True)
                        B.done(("dup", kv), ins)
                    A.moved(pe, "v")
                    B.moved(pe, ("dup", 0))
                    B.moved(pe, ("dup", 1))
                else:
                    stage(i - 3)
            for i in range(2 * HQ - 3, 2 * HQ + 3):
                stage(i)
            pe.wait_ge(wab_landed, 16)
            bank = A.take(pe, "ab", readers=2)
            for tt in range(4):
                for k in range(KT):
                    ins = mm(bank[:, tt * 16:(tt + 1) * 16], hT[:, k, tt * P:(tt + 1) * P], wab[:, k, :],
                             start=k == 0, stop=k == KT - 1)
                    if tt == 0 and k == 0:
                        pay(ins)
            A.done("ab", ins)
            for h in range(4):
                pe.wait_ge(d_ready, 1 + h)
                bank = A.take(pe, ("vtm", h))
                for tt in range(4):
                    ins = nc.tensor.transpose(bank[:, tt * P:(tt + 1) * P], ybuf[:, h, tt * P:(tt + 1) * P], ident)
                A.done(("vtm", h), ins)
            for i in range(8):
                wd = T if i < 4 else 512
                pe.wait_ge(sqd_ready, i + 1)
                bank = A.take(pe, ("l2", i))
                ins = mm(bank[:, 0:wd], ones, sq[:, (i % 4) * 512:(i % 4) * 512 + wd], start=True, stop=True)
                A.done(("l2", i), ins)
            for h in range(4):
                pe.wait_ge(l2_ready, 5 + h)
                bank = A.take(pe, ("ktm", h))
                for tt in range(4):
                    ins = nc.tensor.transpose(bank[:, tt * P:(tt + 1) * P], kF[:, h, tt * P:(tt + 1) * P], ident)
                A.done(("ktm", h), ins)
            norm_sum(2)

            pe.wait_ge(g_ready, 1)
            bank = A.take(pe, "gc")
            for d, um in enumerate(("u_fwd", "u_bwd")):
                mm(bank[:, d * 16:(d + 1) * 16], c_one(um), gates[:, G_G, d * 16:(d + 1) * 16], start=True, stop=True)
            ins = mm(bank[:, 32:64], ones, gates[:, G_G, :], start=True, stop=True)
            A.done("gc", ins)
            for h in range(4):
                A.moved(pe, ("ktm", h))
                A.moved(pe, ("vtm", h))

            def prepare(half):
                for s, d in GROUPS[half]:
                    g, tt = 2 * s + d, TILE[d][s]
                    lat = tt < 2
                    bank = A.take(pe, ("gb", g), readers=2 if lat else 1)
                    for h in range(4):
                        ins = mm(bank[:, h * P:(h + 1) * P], gcol(G_G, d, tt, h).to_broadcast([P, P]),
                                 c_one(("u_fwd", "u_bwd")[d]), start=True, stop=True)
                    A.done(("gb", g), ins)
                    bank = A.take(pe, ("kk", g))
                    for h in range(4):
                        k = kF[:, h, tt * P:(tt + 1) * P]
                        ins = mm(bank[:, h * P:(h + 1) * P], k, k, start=True, stop=True)
                    A.done(("kk", g), ins)
                    if lat:
                        bank = B.take(pe, ("kq", g))
                        for h in range(4):
                            ins = mm(bank[:, h * P:(h + 1) * P], kF[:, h, tt * P:(tt + 1) * P],
                                     qF[:, h, tt * P:(tt + 1) * P], start=True, stop=True)
                        B.done(("kq", g), ins)
                for s, d in GROUPS[half]:
                    g = 2 * s + d
                    A.moved(pe, ("kk", g))
                    bank = A.take(pe, ("lt", g))
                    for h in range(4):
                        ins = nc.tensor.transpose(bank[:, h * P:(h + 1) * P], dec[:, g % 4, h * P:(h + 1) * P], ident)
                    A.done(("lt", g), ins)

            def level(half, lv):
                for s, d in GROUPS[half]:
                    g = 2 * s + d
                    if lv == 1:
                        pe.wait_ge(seed_ready, g + 1)
                    else:
                        A.moved(pe, ("dt", g, lv - 1))
                    bank = A.take(pe, ("m1", g, lv))
                    for h in range(4):
                        c = slice(h * P, (h + 1) * P)
                        ins = mm(bank[:, c], LTm[:, g % 4, c], Tm[:, g % 4, c], start=True, stop=True)
                    A.done(("m1", g, lv), ins)
                for s, d in GROUPS[half]:
                    g = 2 * s + d
                    A.moved(pe, ("m1", g, lv))
                    if lv > 1:
                        A.moved(pe, ("dtt", g, lv - 1))
                    if lv < 6:
                        bank = A.take(pe, ("dt", g, lv))
                        for h in range(4):
                            c = slice(h * P, (h + 1) * P)
                            ins = mm(bank[:, c], TTm[:, g, c], dec[:, g % 4, c], start=True, stop=True)
                        A.done(("dt", g, lv), ins)
                    bank = A.take(pe, ("dtt", g, lv))
                    for h in range(4):
                        c = slice(h * P, (h + 1) * P)
                        ins = mm(bank[:, c], dec[:, g % 4, c], TTm[:, g, c], start=True, stop=True)
                    A.done(("dtt", g, lv), ins)

            def advance(s):
                for d in range(2):
                    g = 2 * s + d
                    pe.wait_ge(ttb_ready, g + 1)
                    pe.wait_ge(kb_ready, g + 1)
                    if s:
                        bank = A.take(pe, ("nw", g))
                        for h in range(4):
                            c = slice(h * P, (h + 1) * P)
                            ins = mm(bank[:, c], kbe[:, d, c], TTm[:, g, c], start=True, stop=True)
                        A.done(("nw", g), ins)
                for d in range(2):
                    g, tt = 2 * s + d, TILE[d][s]
                    if s:
                        A.moved(pe, ("nw", g))
                        A.moved(pe, ("st", g - 2))
                    bank = B.take(pe, ("vn", g))
                    for h in range(4):
                        c = slice(h * P, (h + 1) * P)
                        ins = mm(bank[:, c], TTm[:, g, c], v_tm[:, tt, h, :], start=True, stop=s == 0)
                        if s:
                            ins = mm(bank[:, c], nwT[:, d, c], S[:, d, c], start=False, stop=True)
                    B.done(("vn", g), ins)
                for d in range(2):
                    g, tt = 2 * s + d, TILE[d][s]
                    B.moved(pe, ("vn", g))
                    if tt < 2:
                        pe.wait_ge(qdec_ready, g - 3)
                        B.moved(pe, ("kq", g))
                        bank = B.take(pe, ("og", g))
                        for h in range(4):
                            c = slice(h * P, (h + 1) * P)
                            mm(bank[:, c], S[:, d, c], qdec[:, g % 4, c], start=True, stop=False)
                            ins = mm(bank[:, c], vnew[:, d, c], ATm[:, g % 4, c], start=False, stop=True)
                        B.done(("og", g), ins)
                    if s < 3:
                        bank = A.take(pe, ("st", g))
                        for h in range(4):
                            c = slice(h * P, (h + 1) * P)
                            ins = mm(bank[:, c], kdec[:, d, c], vnew[:, d, c], start=True, stop=True)
                        A.done(("st", g), ins)

            for what, *args in DELTA:
                dict(prepare=prepare, level=level, advance=advance,
                     fill=lambda n: n and fill_sum(C, 0, 7 + n))[what](*args)

            def head_norm_sum(j):
                pe.wait_ge(hn_sq, j + 1)
                for i in range(2):
                    bank = A.take(pe, ("hn", j, i))
                    ins = mm(bank[:, :], ones, sq[:, i * 512:(i + 1) * 512], start=True, stop=True)
                    A.done(("hn", j, i), ins)
            head_norm_sum(0)

            def project_out(tag, names, mix, ready):
                for s_, n_ in ready:
                    pe.wait_ge(s_, n_)
                for u in range(4):
                    w = unit(names + (u,)).rearrange("p (k n) -> p k n", k=KT)
                    for j in range(2):
                        proj((tag, 2 * u + j), w, j, mix, T)
                    owe()

            project_out("xo1", ("out1",), mixT, [(hn_out, 4), (norm_out, norms[2]["out"])])

            def ffn(tag, h, part):
                accs = []

                def up(f):
                    c, j = f // 2, f % 2
                    bank = A.take(pe, (tag, "gu", f))
                    for i, m in enumerate("gu"):
                        w = unit((tag, m, c)).rearrange("p (k n) -> p k n", k=KT)
                        for k in range(KT):
                            ins = mm(bank[:, i * T:(i + 1) * T], w[:, k, j * P:(j + 1) * P], h[:, k, :],
                                     start=k == 0, stop=k == KT - 1)
                            if k == 0:
                                pay(ins)
                        if j == 1 and i == 0:
                            ins.then_inc(unit_used, 1)
                    if j == 1:
                        owe()
                    A.done((tag, "gu", f), ins)

                def down(f):
                    if f == 0:
                        accs.extend(B.take(pe, (tag, "acc", i)) for i in range(3))
                        accs.append(C.take(pe, (tag, "acc", 3)))
                    w = unit((tag, "d", f // 2)).rearrange("p (r n) -> p r n", r=2)
                    if tag == "ffn1":
                        pe.wait_ge(gT_ready, f + 1)
                    else:
                        A.moved(pe, (tag, "gu", f))
                    for dt in range(KT):
                        ins = mm(accs[dt // 2][:, (dt % 2) * T:(dt % 2 + 1) * T], w[:, f % 2, dt * P:(dt + 1) * P],
                                 gT[:, f % 4, :], start=f == 0 and dt % 2 == 0, stop=f == FT - 1,
                                 skip_group_check=True)
                        if dt == 0:
                            pay(ins)
                        if f == FT - 1 and dt % 2 == 1:
                            rg = B if dt < 6 else C
                            rg.done((tag, "acc", dt // 2), ins)
                    if f == FT - 1:
                        owe()
                    elif f % 2:
                        ins.then_inc(unit_used, 1)

                for f in range(FT + 3):
                    if f < FT:
                        up(f)
                    if f:
                        fill_sum(A, part, f - 1)
                    if f % 2 and 3 <= f < FT + 2:
                        down(f - 3)
                        down(f - 2)

            norm_sum(3)
            pe.wait_ge(norm_out, norms[3]["out"])
            ffn("ffn1", hF, 1)
            norm_sum(4)

            for l in range(2):
                n0 = 5 + 3 * l
                norm_sum(n0)
                pe.wait_ge(norm_out, norms[n0]["out"])
                w_in = lambda u: unit(("in2", l, u)).rearrange("p (k n) -> p k n", k=KT)

                def features(kind, u0, i):
                    proj((l, kind, i), w_in(u0 + i // 2), i % 2, h2, T)
                    if i % 2:
                        owe()

                def tokens(kind, u0, half):
                    w = w_in(u0 + half)
                    bank = A.take(pe, (l, kind, half))
                    for tt in range(TT):
                        for k in range(KT):
                            ins = mm(bank[:, tt * UW:(tt + 1) * UW], h2[:, k, tt * P:(tt + 1) * P], w[:, k, :],
                                     start=k == 0, stop=k == KT - 1)
                            if tt == 0 and k == 0:
                                pay(ins)
                    owe()
                    A.done((l, kind, half), ins)

                def turn_rotary(j):
                    for i in range(2):
                        A.moved(pe, (l, "qr" if j < 2 else "kr", 2 * (j % 2) + i))
                    bank = A.take(pe, (l, "rr", j))
                    src = (qR if j < 2 else kR)[:, 2 * (j % 2):2 * (j % 2) + 2, :].rearrange("p a b -> p (a b)")
                    ins = mm(bank[:, :], c_two("rot128"), src, start=True, stop=True)
                    A.done((l, "rr", j), ins)

                def s2(u):
                    h, qt = u // 2, u % 2
                    r0 = HD * (h % 2)
                    return qA2[r0:r0 + HD, h // 2, qt * P:(qt + 1) * P], kA2[r0:r0 + HD, h // 2, 0:(qt + 1) * P], (qt + 1) * P
                stage = attention(("a2", l), 16 * (l + 1), s2,
                                  lambda u, k: vA2[:, k, HD * (u // 2):HD * (u // 2) + HD], prob2, probT2)
                for i in range(4):
                    features("qa", 0, i)
                for i in range(4):
                    features("ka", 2, i)
                for i in range(2):
                    tokens("va", 4, i)
                pe.wait_ge(con2_landed, 16)
                for i, (kind, u0, j) in enumerate(SLOTS2):
                    dict(qr=features, kr=features, gr=features, vr=tokens,
                         rr=lambda kind, u0, j: turn_rotary(j))[kind](kind, u0, j)
                    if i == 0:
                        for n in [(l, "qa", i) for i in range(4)] + [(l, "ka", i) for i in range(4)] + [(l, "va", 0), (l, "va", 1)]:
                            A.moved(pe, n)
                    stage(i)
                stage(2 * HQ + 2)
                norm_sum(n0 + 1)
                pe.wait_ge(rrope, 4 * (l + 1))
                A.moved(pe, (l, "vr", 0))
                A.moved(pe, (l, "vr", 1))

                def ret_scores(h):
                    bank = B.take(pe, (l, "rs", h))
                    mm(bank[:, 0:256], kR[:, h, 0:P], qR[:, h, :], start=True, stop=True)
                    ins = mm(bank[:, 256:384], kR[:, h, P:T], qR[:, h, P:T], start=True, stop=True)
                    B.done((l, "rs", h), ins)
                ret_scores(0)
                for h in range(4):
                    if h < 3:
                        ret_scores(h + 1)
                    B.moved(pe, (l, "rs", h))
                    bank = A.take(pe, (l, "ro", h))
                    a = AR[:, h % 2, :]
                    mm(bank[:, 0:P], vR[:, 0, h * P:(h + 1) * P], a[:, 0:P], start=True, stop=True)
                    mm(bank[:, P:T], vR[:, 0, h * P:(h + 1) * P], a[:, P:T], start=True, stop=False)
                    ins = mm(bank[:, P:T], vR[:, 1, h * P:(h + 1) * P], a[:, 256:384], start=False, stop=True)
                    A.done((l, "ro", h), ins)
                head_norm_sum(1 + l)
                project_out(("xo2", l), ("out2", l), mix2, [(hn_out, 4 * (l + 2)), (norm_out, norms[n0 + 1]["out"])])
                norm_sum(n0 + 2)
                pe.wait_ge(norm_out, norms[n0 + 2]["out"])
                if l == 0:
                    ffn("ffn2", hF, 2)

            pe.wait_ge(wrt_landed, 16)
            bank = A.take(pe, "logits")
            for tt in range(TT):
                for k in range(KT):
                    ins = mm(bank[:, tt * NE:(tt + 1) * NE], hF[:, k, tt * P:(tt + 1) * P], wrt[:, k, :],
                             start=k == 0, stop=k == KT - 1)
            A.done("logits", ins)
            for tt in range(TT):
                for kg in range(2):
                    bank = A.take(pe, ("htm", tt, kg))
                    for k in range(4):
                        ins = nc.tensor.transpose(bank[:, k * P:(k + 1) * P],
                                                  hF[:, 4 * kg + k, tt * P:(tt + 1) * P], ident)
                    A.done(("htm", tt, kg), ins)
            pe.wait_ge(sel_ready, 1)
            bank = A.take(pe, "pos")
            sel = [rout[:, 4 + tt, :] for tt in range(2)]
            mm(bank[:, 0:8], c_all("ustrict"), sel[0], start=True, stop=True)
            mm(bank[:, 8:16], ones, sel[0], start=True, stop=False)
            mm(bank[:, 8:16], c_all("ustrict"), sel[1], start=False, stop=True)
            mm(bank[:, 16:24], ones, sel[0], start=True, stop=False)
            ins = mm(bank[:, 16:24], ones, sel[1], start=False, stop=True)
            A.done("pos", ins)
            for e in range(NE):
                pe.wait_ge(pw_ready, e + 1)
                bank = A.take(pe, ("pwT", e))
                for s in range(2):
                    for tt in range(TT):
                        ins = nc.tensor.transpose(bank[:, s * T + tt * P:s * T + (tt + 1) * P],
                                                  Pw[:, e % 2, tt * 256 + s * P:tt * 256 + (s + 1) * P], ident)
                A.done(("pwT", e), ins)
            for rg in (A, B, C):
                rg.all_free(pe)

            def expert(e, ns):
                st = ns // P

                def eunit(name):
                    k = U0 + e_order[name]
                    pe.wait_ge(landed[slot[k]], e * (16 * EU // RING) + 16 * turn[k])
                    return ring[:, slot[k], :]

                for j in range(KT):
                    pe.wait_ge(moved, e * 16 + (j + 1))
                    bank = banks[2 + j % 2]
                    for tt in range(TT):
                        ins = mm(bank[:, 0:ns], h_tm[:, tt, j * P:(j + 1) * P], Pg[:, tt, e, 0:ns],
                                 start=tt == 0, stop=tt == TT - 1)
                    ins.then_inc(xj_full, 1)
                pe.wait_ge(moved, e * 16 + (KT + 2))

                def up(f):
                    c, j = f // 2, f % 2
                    pe.wait_ge(gated, e * FT + (f + 1))
                    bank = banks[f % 2]
                    for i, m in enumerate("gu"):
                        w = eunit((m, c)).rearrange("p (k n) -> p k n", k=KT)
                        for k in range(KT):
                            ins = mm(bank[:, i * ns:(i + 1) * ns], w[:, k, j * P:(j + 1) * P], xg[:, k, 0:ns],
                                     start=k == 0, stop=k == KT - 1)
                            if k == 0:
                                pay(ins)
                        if j == 1 and i == 0:
                            ins.then_inc(unit_used, 1)
                    if j == 1:
                        owe()
                    ins.then_inc(gu_full, 1)

                def down(f):
                    w = eunit(("d", f // 2)).rearrange("p (r n) -> p r n", r=2)
                    pe.wait_ge(gated, e * FT + (f + 3))
                    for s in range(st):
                        for half in range(2):
                            ins = mm(banks[4 + 2 * s + half][:, :], gTe[:, f % 4, s * P:(s + 1) * P],
                                     w[:, f % 2, half * 512:(half + 1) * 512], start=f == 0, stop=f == FT - 1,
                                     skip_group_check=True)
                            if s == 0 and half == 0:
                                pay(ins)
                    if f % 2:
                        ins.then_inc(unit_used, 1)

                for f in range(FT + 2):
                    if f < FT:
                        up(f)
                    if f >= 2 and f % 2 == 1:
                        down(f - 3)
                        down(f - 2)
                pe.wait_ge(ye_ready, e + 1)
                for j in range(KT):
                    pe.wait_ge(moved, e * 16 + (8 + j + 1))
                    bank = banks[2 + j % 2]
                    for s in range(st):
                        ins = mm(bank[:, 0:T], ye[:, s, j * P:(j + 1) * P], PwT[:, s, e, :],
                                 start=s == 0, stop=s == st - 1)
                    ins.then_inc(xj_full, 1)

            with pe.Fori(0, NE) as e:
                count = pe.value_load(cnt_i[0:1, bass.ts(e, 1)], min_val=0, max_val=T)
                with pe.If(count > NARROW):
                    expert(e, T)
                with pe.Else():
                    expert(e, NARROW)
                pe.nop()

            pe.wait_ge(sq_ready, 12)
            for k in range(KT):
                ins = mm(banks[0][:, 0:T], ones, sq[:, k * T:(k + 1) * T], start=k == 0, stop=k == KT - 1)
            ins.then_inc(fin_ready, 1)
            pe.wait_ge(norm_out, norms[11]["out"])
            for tt in range(TT):
                for kg in range(2):
                    for k in range(4):
                        ins = nc.tensor.transpose(banks[4 + 2 * tt + kg][:, k * P:(k + 1) * P],
                                                  xT[:, 4 * kg + k, tt * P:(tt + 1) * P], ident)
                    ins.then_inc(fin_ready, 1)

        @block.scalar
        def _(act):
            steps = [0]

            def step(ins):
                steps[0] += 1
                ins.then_inc(act_step, 1)
                act.wait_ge(act_step, steps[0])
            F = nc.scalar.activation

            rows = vrows

            def vrow(table, row, ap):
                n = ap.shape[0]
                act.dma_start(rows[row:row + n, table * P:(table + 1) * P], ap).then_inc(v_landed, 16)

            def tiles(ap):
                return ap.rearrange("(a p) -> a p", p=P)
            vrow(0, V_C, tiles(t["c"][0]))
            vrow(0, V_CCTX, tiles(t["c_ctx"]))
            vrow(0, V_BMOD, tiles(t["b_mod"][0]))
            vrow(0, V_N1, tiles(t["norm1_g"][0]))
            vrow(0, V_ATTG, tiles(t["attn_out_g"][0]))
            vrow(0, V_GDNG, t["gdn_norm_g"])
            vrow(0, V_N2, tiles(t["norm2_g"][0]))
            vrow(0, V_CONV, t["conv_qkv_w"][0].rearrange("k (a p) -> (k a) p", p=P))
            for row, name in ((V_QG, "q_norm_g"), (V_KG, "k_norm_g")):
                for half in range(2):
                    act.dma_start(rows[row:row + 1, half * HD:(half + 1) * HD], t[name]).then_inc(v_landed, 16)
            cw = t["ffn_conv_w"][0].rearrange("k (a p) -> k a p", p=P)
            vrow(1, V_FW01, cw[0])
            vrow(1, V_FW01 + 44, cw[1])
            vrow(1, V_C2, tiles(t["c_2"][0]))
            vrow(1, V_NMIX, t["norm_mix_g_2"].rearrange("l (a p) -> (l a) p", p=P))
            vrow(1, V_NFFN, t["norm_ffn_g_2"].rearrange("l (a p) -> (l a) p", p=P))
            vrow(2, V_FW2, cw[2])
            vrow(2, V_FB, tiles(t["ffn_conv_b"][0]))
            vrow(2, V_FIN1, tiles(t["final_norm_g"]))
            vrow(2, V_FIN2, tiles(t["final_norm_g_2"]))
            vrow(3, V_BADA, t["ada_b_2"][0:1].rearrange("l (a p) -> (l a) p", p=P))
            vrow(3, V_BADA + 48, t["ada_b_2"][1:2].rearrange("l (a p) -> (l a) p", p=P))
            vrow(3, V_ATTG2, t["att_out_g_2"][0:1].rearrange("l (a p) -> (l a) p", p=P))
            vrow(3, V_ATTG2 + 4, t["att_out_g_2"][1:2].rearrange("l (a p) -> (l a) p", p=P))
            vrow(3, V_RETG, t["ret_out_g_2"].rearrange("l (a p) -> (l a) p", p=P))
            act.dma_start(con2[:, :], t["constants"][:, C_ALL_W:C_ALL_W + C_ONE_W]).then_inc(con1_landed, 16)
            for i, (f, b) in enumerate((("a_log_f", "a_log_b"), ("dt_bias_f", "dt_bias_b"))):
                for j, name in enumerate((f, b)):
                    act.dma_start(gconst[:, i, 4 * j:4 * j + 4], t[name].to_broadcast([P, 4])).then_inc(gc_landed, 16)
            with nc.allow_non_contiguous_dma(reason="small"):
                act.dma_start(wab[:, :, :], t["w_in"][0][:, 11 * UW:].rearrange("(k p) n -> p k n", p=P)).then_inc(wab_landed, 16)
                act.dma_start(wrt[:, :, :], t["router_w_2"][0].rearrange("(k p) n -> p k n", p=P)).then_inc(wrt_landed, 16)

            for s in range(2):
                dst = (xT, ctxT)[s]
                for tt in range(TT):
                    for kg in range(2):
                        n = ("xt", s, tt, kg)
                        bank = A.full(act, n)
                        ins = F(dst[:, 4 * kg:4 * kg + 4, tt * P:(tt + 1) * P],
                                bank[:, :].rearrange("p (a b) -> p a b", a=4), ACT.Copy)
                        A.free(n, ins)

            def norm(n):
                N = norms[n]
                N["wait"](act)
                w = N["nt"] * T
                F(sq[:, 0:w].rearrange("p (a b) -> p a b", b=T), N["src"], ACT.Square).then_inc(sq_ready, 1)
                if n == 11:
                    act.wait_ge(fin_ready, 1)
                    bank = banks[0]
                else:
                    bank = A.full(act, ("ss", n))
                if n > 1:
                    act.wait_ge(norm_out, norms[n - 1]["out"])
                ins = F(root(n), bank[:, 0:T], ACT.Sqrt, bias=EPS, scale=1.0 / (N["nt"] * P))
                if n == 11:
                    ins.then_inc(root_ready, 1)
                else:
                    A.free(("ss", n), ins)
            A.moved(act, "vec")
            F(cs[:, :, 0], v(0, V_C, 8), ACT.Silu)
            F(cs[:, :, 1], v(0, V_CCTX, 8), ACT.Silu)
            F(cs2[:, :], v(1, V_C2, 8), ACT.Silu).then_inc(cs_ready, 1)
            norm(0)
            norm(1)
            for u in range(8):
                n = ("ada", 0, u)
                A.free(n, F(sq[0:2, u * UW:(u + 1) * UW], A.full(act, n)[0:2, 0:UW], ACT.Copy))

            for i in range(4):
                ins = F(qA[:, i, :], A.full(act, ("q", i))[:, 0:T], ACT.Copy)
                A.free(("q", i), ins)
            ins = F(kA[:, :], A.full(act, "k")[:, :], ACT.Copy)
            A.free("k", ins)
            ins = F(vA[:, :, :].rearrange("p a b -> p (a b)"), A.full(act, "v")[:, :], ACT.Copy)
            A.free("v", ins)

            def attention(tag, base, keys, scaled, pbuf, ptbuf, o):
                def expo(u):
                    n = keys(u)
                    act.wait_ge(max_ready, base + u + 1)
                    st = stat[:, u % 4, :]
                    if scaled:
                        F(pbuf[:, u % 3, 0:n], pbuf[:, u % 3, 0:n], ACT.Exp, bias=st[:, 1:2],
                          accum_out=st[:, 2:3]).then_inc(exp_done, 1)
                    else:
                        bank = B.full(act, (tag, "s", u))
                        if u >= 3:
                            A.full(act, (tag, "pt", u - 3))
                        ins = F(pbuf[:, u % 3, 0:n], bank[:, 0:n], ACT.Exp, bias=st[:, 1:2], scale=HD ** -0.5,
                                accum_out=st[:, 2:3])
                        B.free((tag, "s", u), ins)

                def turned(u):
                    n = keys(u)
                    name = (tag, "pt", u)
                    A.free(name, F(ptbuf[:, u % 2, 0:n], A.full(act, name)[:, 0:n], ACT.Copy))

                def output(j):
                    name = (tag, "o", j)
                    C.free(name, F(o[:, j, :], C.full(act, name)[:, 0:T], ACT.Copy))

                def stage(i):
                    if i >= 7 and i % 4 == 3:
                        output((i - 7) // 4)
                    if i < 2 * HQ:
                        expo(i)
                    if 2 <= i < 2 * HQ + 2:
                        turned(i - 2)
                return stage

            for n in [("q", i) for i in range(4)] + ["k"]:
                A.moved(act, n)
            F(sq[:, 0:1024], qA[:, :, :].rearrange("p a b -> p (a b)"), ACT.Square)
            F(sq[:, 1024:1536], kA[:, :], ACT.Square).then_inc(ansq, 1)

            def conv_place(i):
                return qF[:, i, :] if i < 4 else kF[:, i - 4, :] if i < 8 else ybuf[:, i - 8, :]
            stage = attention("a1", 0, lambda u: 512, False, prob, probT, oA)
            for i in range(2 * HQ):
                if i < 12:
                    wd = T if i < 4 else 512
                    F(conv_place(i), A.full(act, ("d", i))[:, 0:wd], ACT.Copy, scale=v(0, V_CONV + 12 + i)).then_inc(centre_ready, 1)
                else:
                    n = ("z", i - 12)
                    A.free(n, F(zs[:, i - 12, :], A.full(act, n)[:, 0:T], ACT.Copy))
                if i == 0:
                    for j in range(3):
                        n = ("an", j)
                        B.free(n, F(hroot[:, j, :] if j < 2 else kroot, B.full(act, n)[:, :], ACT.Sqrt, bias=EPS,
                                    scale=1.0 / HD))
                elif i == 2:
                    for kv in range(2):
                        n = ("dup", kv)
                        B.free(n, F(kdup[:, kv, :], B.full(act, n)[:, :], ACT.Copy))
                elif i > 2:
                    stage(i - 3)
            for i in range(2 * HQ - 3, 2 * HQ + 4):
                stage(i)
            act.wait_ge(sp_abs, 1)
            step(F(gates[:, G_T1, :], gates[:, G_T1, :], ACT.Exp, scale=-1.0))
            act.wait_ge(gc_landed, 64)
            F(gates[:, G_EA, 0:8], gconst[:, 0, :], ACT.Exp)
            F(gates[:, G_T1, :], gates[:, G_T1, :], ACT.Ln, bias=1.0).then_inc(sp_ln, 1)
            ins = F(gates[:, G_BETA, :].rearrange("p (d t h) -> p t d h", d=2, t=4),
                    A.full(act, "ab")[:, 0:64].rearrange("p (t x d h) -> p t x d h", t=4, x=2, d=2)[:, :, 1, :, :], ACT.Sigmoid)
            A.free("ab", ins)
            for n in range(8, 20):
                i = n % 12
                A.moved(act, ("d", i))
                y = conv_place(i)
                F(y, y, ACT.Silu).then_inc(d_ready, 1)
            for i in range(4):
                A.moved(act, ("z", i))
                step(F(zs[:, i, :], zs[:, i, :], ACT.Silu))
            for h in range(4):
                n = ("vtm", h)
                A.free(n, F(v_tm[:, :, h, :], A.full(act, n)[:, :].rearrange("p (a b) -> p a b", a=4), ACT.Copy))
            def l2_root(i):
                wd = T if i < 4 else 512
                bank = A.full(act, ("l2", i))
                if i >= 2:
                    act.wait_ge(l2_ready, i - 1)
                c = float(P) if i < 4 else 1.0
                ins = F(hroot[:, i % 2, 0:wd], bank[:, 0:wd], ACT.Sqrt, bias=EPS * c, scale=c)
                A.free(("l2", i), ins)
            act.wait_ge(d_ready, 12)
            for i in range(9):
                if i < 8:
                    wd = T if i < 4 else 512
                    if i >= 4:
                        A.full(act, ("l2", i - 4))
                    F(sq[:, (i % 4) * 512:(i % 4) * 512 + wd], qF[:, i, :] if i < 4 else kF[:, i - 4, :],
                      ACT.Square).then_inc(sqd_ready, 1)
                if i:
                    l2_root(i - 1)
            for h in range(4):
                n = ("ktm", h)
                ins = F(k_tm[:, :, h, :], A.full(act, n)[:, :].rearrange("p (a b) -> p a b", a=4), ACT.Copy)
                A.free(n, ins)
            norm(2)

            act.wait_ge(tmg_ready, 1)
            F(gates[:, G_EG, :], gates[:, G_CUM, :], ACT.Exp)
            F(gates[:, G_KD, :], gates[:, G_T0, :], ACT.Exp)
            F(gates[:, G_DL, :], gates[:, G_TOT, :], ACT.Exp).then_inc(gate_ready, 1)

            def head_norm(j, src, wait):
                wait()
                F(sq[:, 0:1024], src.rearrange("p a b -> p (a b)"), ACT.Square).then_inc(hn_sq, 1)
                if j == 0:
                    act.wait_ge(l2_ready, 8)
                else:
                    act.wait_ge(hn_out, 4 * j)
                for i in range(2):
                    n = ("hn", j, i)
                    ins = F(hroot[:, i, :], A.full(act, n)[:, :], ACT.Sqrt, bias=EPS, scale=1.0 / P)
                    A.free(n, ins)

            def prepare(half):
                for s, d in GROUPS[half]:
                    g, tt = 2 * s + d, TILE[d][s]
                    if tt < 2:
                        A.moved(act, ("gb", g), 1)
                        A.free(("gb", g), F(egb[:, g % 4, :], A.full(act, ("gb", g))[:, :], ACT.Exp))
                    A.moved(act, ("gb", g))
                    for h in range(4):
                        c = slice(h * P, (h + 1) * P)
                        ins = F(dec[:, g % 4, c], dec[:, g % 4, c], ACT.Exp, bias=gcol(G_CUM, d, tt, h))
                    ins.then_inc(dec_ready, 1)
                    if tt < 2:
                        for h in range(4):
                            c = slice(h * P, (h + 1) * P)
                            ins = F(ATm[:, g % 4, c], ATm[:, g % 4, c], ACT.Exp, bias=gcol(G_NCUM, d, tt, h))
                        ins.then_inc(att_ready, 1)
                for s, d in GROUPS[half]:
                    n = ("lt", 2 * s + d)
                    A.free(n, F(LTm[:, n[1] % 4, :], A.full(act, n)[:, :], ACT.Copy))

            def advance(s):
                if s:
                    for d in range(2):
                        n = ("nw", 2 * s + d)
                        A.free(n, F(nwT[:, d, :], A.full(act, n)[:, :], ACT.Copy))
                for d in range(2):
                    n = ("vn", 2 * s + d)
                    B.free(n, F(vnew[:, d, :], B.full(act, n)[:, :], ACT.Copy))
            for what, *args in DELTA:
                if what == "prepare":
                    prepare(*args)
                elif what == "advance":
                    advance(*args)

            def last_og():
                B.moved(act, ("og", 7))
                B.moved(act, ("og", 6))
            head_norm(0, oG, last_og)
            norm(3)
            act.dma_start(con2[:, 0:C_TWO_W], t["constants"][:, C_ALL_W + C_ONE_W:]).then_inc(con2_landed, 16)

            for f in range(FT + 1):
                if f < FT:
                    bank = A.full(act, ("ffn1", "gu", f))
                    if f >= 3:
                        act.wait_ge(gT_ready, f - 2)
                    F(yc[:, f % 3, 0:T], bank[:, 0:T], ACT.Identity, scale=v(1, V_FW01 + 44 + f), bias=v(2, V_FB + f))
                    F(yc[:, f % 3, T:512], bank[:, T:512], ACT.Identity, scale=v(1, V_FW01 + 44 + FT + f),
                      bias=v(2, V_FB + FT + f)).then_inc(centre_ready, 1)
                if f:
                    A.moved(act, ("ffn1", "gu", f - 1))
                    y = yc[:, (f - 1) % 3, 0:T]
                    F(y, y, ACT.Silu).then_inc(silu_ready, 1)
            norm(4)

            for l in range(2):
                n0 = 5 + 3 * l
                norm(n0)
                place = dict(qa=qA2, ka=kA2, qr=qR, kr=kR, gr=sgr, va=vA2, vr=vR)

                def copy_out(kind, i):
                    n = (l, kind, i)
                    bank = A.full(act, n)
                    if kind[0] == "v":
                        ins = F(place[kind][:, :, i * UW:(i + 1) * UW], bank[:, :].rearrange("p (a b) -> p a b", a=2), ACT.Copy)
                    else:
                        ins = F(place[kind][:, i, :], bank[:, 0:T], ACT.Copy)
                    A.free(n, ins)
                for kind, m in (("qa", 4), ("ka", 4), ("va", 2)):
                    for i in range(m):
                        copy_out(kind, i)
                stage = attention(("a2", l), 16 * (l + 1), lambda u: (u % 2 + 1) * P, True, prob2, probT2, oA2)
                for i, (kind, _, j) in enumerate(SLOTS2):
                    if kind != "rr":
                        copy_out(kind, j)
                    stage(i)
                stage(2 * HQ + 2)
                stage(2 * HQ + 3)
                for i in range(4):
                    A.moved(act, (l, "gr", i))
                F(sgr[:, :, :], sgr[:, :, :], ACT.Silu).then_inc(sg_ready, 1)
                norm(n0 + 1)
                for h in range(4):
                    n = (l, "ro", h)
                    A.free(n, F(oR[:, h, :], A.full(act, n)[:, 0:T], ACT.Copy))

                def last_ro():
                    for h in range(4):
                        A.moved(act, (l, "ro", h))
                head_norm(1 + l, oR, last_ro)
                norm(n0 + 2)
                if l == 0:
                    for f in range(FT):
                        bank = A.full(act, ("ffn2", "gu", f))
                        if f >= 3:
                            A.moved(act, ("ffn2", "gu", f - 3))
                        F(yc[:, f % 3, 0:T], bank[:, 0:T], ACT.Silu).then_inc(silu_ready, 1)

            for tt in range(TT):
                for kg in range(2):
                    n = ("htm", tt, kg)
                    A.free(n, F(h_tm[:, tt, kg * 512:(kg + 1) * 512], A.full(act, n)[:, :], ACT.Copy))
            act.wait_ge(top_ready, 1)
            for tt in range(TT):
                F(rout[:, 14 + tt, 0:1], rout[:, 12 + tt, 0:1], ACT.Sigmoid)
                ins = F(rout[:, 14 + tt, 1:2], rout[:, 12 + tt, 0:1], ACT.Sigmoid, scale=-1.0)
            ins.then_inc(wt_ready, 1)
            for e in range(NE):
                n = ("pwT", e)
                A.free(n, F(PwT[:, :, e, :], A.full(act, n)[:, :].rearrange("p (a b) -> p a b", a=2), ACT.Copy))
            A.moved(act, "pos")

            def expert(e, ns):
                for f in range(FT):
                    act.wait_ge(gu_full, e * FT + (f + 1))
                    act.wait_ge(gated, e * FT + (f + 1))
                    F(sge[:, f % 2, 0:ns], banks[f % 2][:, 0:ns], ACT.Silu).then_inc(sge_ready, 1)
                act.wait_ge(unit_used, e * EU + (U0 + EU))
                for i in range(2 * ns // P):
                    ins = F(ye[:, i // 2, (i % 2) * 512:(i % 2 + 1) * 512], banks[4 + i][:, :], ACT.Copy)
                ins.then_inc(ye_ready, 1)

            with act.Fori(0, NE) as e:
                count = act.value_load(cnt_i[0:1, bass.ts(e, 1)], min_val=0, max_val=T)
                with act.If(count > NARROW):
                    expert(e, T)
                with act.Else():
                    expert(e, NARROW)
                act.nop()
            norm(11)

        @block.vector
        def _(dve):
            steps = [0]
            V = nc.vector

            def step(ins):
                steps[0] += 1
                ins.then_inc(dve_step, 1)
                dve.wait_ge(dve_step, steps[0])

            n = "vec"
            bank = A.full(dve, n)
            for i, rows in enumerate((V0_ROWS, V1_ROWS, V2_ROWS, V3_ROWS)):
                ins = V.tensor_copy(vec[:, i, 0:rows], bank[:, i * P:i * P + rows])
            A.free(n, ins)
            A.moved(dve, n)

            def norm(n, gains=None):
                N = norms[n]
                nt = N["nt"]
                if n == 11:
                    dve.wait_ge(root_ready, 1)
                else:
                    A.moved(dve, ("ss", n))
                step(V.reciprocal(root(n), root(n)))
                step(V.tensor_tensor(N["dst"], N["src"], over(root(n), nt), ALU.mult))
                for k in range(nt):
                    y = N["dst"][:, k, :]
                    if N["shift"] is None:
                        ins = V.tensor_scalar(y, y, N["gain"][:, k:k + 1], None, ALU.mult)
                    else:
                        ins = V.tensor_scalar(y, y, N["gain"][:, k:k + 1], N["shift"][:, k:k + 1], ALU.mult, ALU.add)
                    ins.then_inc(norm_out, 1)

            fills = [0]

            def fill(part, u):
                n = fills[0]
                fills[0] += 1
                k = order["mod", part, u]
                if n >= 2:
                    rg, name = filled[n - 2]
                    rg.full(dve, name)
                dve.wait_ge(landed[slot[k]], 16 * turn[k])
                w = ring[:, slot[k], :].rearrange("p (k n) -> p k n", k=KT)
                for i in range(KT):
                    acc = facc2[:, n % 2, i % 2, :]
                    c = cs[:, i, 0:1] if part == 0 else cs2[:, i:i + 1]
                    if i < 2:
                        ins = V.tensor_scalar(acc, w[:, i, :], c, None, ALU.mult)
                    else:
                        dve.wait_ge(dve_step, steps[0] - 1)
                        ins = V.scalar_tensor_tensor(out=acc, in0=w[:, i, :], scalar=c, in1=acc, op0=ALU.mult, op1=ALU.add)
                    steps[0] += 1
                    ins.then_inc(dve_step, 1)
                dve.wait_ge(dve_step, steps[0])
                V.tensor_tensor(facc2[:, n % 2, 0, :], facc2[:, n % 2, 0, :], facc2[:, n % 2, 1, :],
                                ALU.add).then_inc(fill_ready, 1)
                filled.append((C if part == 0 else A, ("ada", part, u)))
            filled = []

            def ada(part, u):
                n = ("ada", part, u)
                rg = C if part == 0 else A
                bank = rg.full(dve, n)
                c = slice(2 * u, 2 * u + 2)
                if part == 0:
                    ins = V.tensor_tensor(m1[:, c, 0], bank[:, 0:2], v(0, V_BMOD + 2 * u, 2), ALU.add)
                else:
                    ins = V.tensor_tensor(m2[:, part - 1, c], bank[:, 0:2], v(3, V_BADA + 48 * (part - 1) + 2 * u, 2), ALU.add)
                rg.free(n, ins)

            def gain(i, scale, g):
                return V.scalar_tensor_tensor(out=amul[:, i, :], in0=scale, scalar=1.0, in1=g, op0=ALU.add, op1=ALU.mult)

            dve.wait_ge(con_landed, 16)
            bias = v(0, V_BMOD, 16).rearrange("p (a b) -> p a b", b=1).to_broadcast([P, 16, 2])
            ins = V.tensor_tensor(m1[:, 0:16, :], A.full(dve, "adat")[:, 0:32].rearrange("p (a b) -> p a b", a=16), bias, ALU.add)
            A.free("adat", ins)
            A.moved(dve, "adat")
            gain(0, m1[:, 8:16, 0], v(0, V_N1, 8))
            step(gain(1, m1[:, 8:16, 1], v(0, V_N1, 8)))
            norm(0)
            norm(1)

            def side_taps(y, p, w0, w2, last):
                for i, (yy, pp) in enumerate(zip(y, p)):
                    ins = V.scalar_tensor_tensor(out=yy[..., 1:T], in0=pp[..., 0:T - 1], scalar=w0[i], in1=yy[..., 1:T],
                                                 op0=ALU.mult, op1=ALU.add)
                step(ins)
                for i, (yy, pp) in enumerate(zip(y, p)):
                    ins = V.scalar_tensor_tensor(out=yy[..., 0:T - 1], in0=pp[..., 1:T], scalar=w2[i], in1=yy[..., 0:T - 1],
                                                 op0=ALU.mult, op1=ALU.add)
                last(ins)

            def conv_sides(i):
                nseg = 1 if i < 4 else 2
                n = ("d", i)
                y = (qF[:, i, :] if i < 4 else kF[:, i - 4, :] if i < 8 else ybuf[:, i - 8, :]).rearrange("p (a b) -> p a b", a=nseg)
                dve.wait_ge(centre_ready, i + 1)
                bank = A.full(dve, n)
                side_taps([y], [bank[:, 0:nseg * T].rearrange("p (a b) -> p a b", a=nseg)],
                          [v(0, V_CONV + i)], [v(0, V_CONV + 24 + i)], lambda ins: A.free(n, ins))

            pair = lambda ap: ap.rearrange("p a b -> p (a b)")
            def qk_norm():
                for j in range(3):
                    B.moved(dve, ("an", j))
                    r = hroot[:, j, :] if j < 2 else kroot
                    step(V.reciprocal(r, r))
                    x = pair(qA[:, 2 * j:2 * j + 2, :]) if j < 2 else kA[:, :]
                    V.scalar_tensor_tensor(out=x, in0=x, scalar=v(0, V_QG if j < 2 else V_KG), in1=r,
                                           op0=ALU.mult, op1=ALU.mult).then_inc(qk_normed, 1)

            def rotary(rg, n, x, cos, sin, tmp, signal):
                m = x.shape[1]
                bank = rg.full(dve, n)
                rg.free(n, V.tensor_tensor(tmp, bank[:, 0:m * T].rearrange("p (a b) -> p a b", a=m), over(sin, m), ALU.mult))
                step(V.tensor_tensor(x, x, over(cos, m), ALU.mult))
                V.tensor_tensor(x, x, tmp, ALU.add).then_inc(signal, 1)
            dve.wait_ge(con1_landed, 16)

            def qk_rotary():
                for j in range(3):
                    x = qA[:, 2 * j:2 * j + 2, :] if j < 2 else kA[:, 0:T].rearrange("p (a b) -> p a b", a=1)
                    m = x.shape[1]
                    tmp = atmp[:, j % 2, 0:m * T].rearrange("p (a b) -> p a b", a=m)
                    rotary(B, ("rot", j), x, c_one("cos", T), c_one("sin", T), tmp, rope_done)

            def attention(tag, base, keys, scaled, pbuf, mask=None):
                def maxima(u):
                    n = keys(u)
                    st = stat[:, u % 4, :]
                    name = (tag, "s", u)
                    bank = B.full(dve, name)
                    if scaled:
                        p = pbuf[:, u % 3, :]
                        if u >= 3:
                            A.full(dve, (tag, "pt", u - 3))
                        if n > P:
                            V.tensor_scalar(p[:, 0:n - P], bank[:, 0:n - P], HD ** -0.5, None, ALU.mult)
                        ins = V.scalar_tensor_tensor(out=p[:, n - P:n], in0=bank[:, n - P:n], scalar=HD ** -0.5,
                                                     in1=mask, op0=ALU.mult, op1=ALU.add)
                        B.free(name, ins)
                        B.moved(dve, name)
                        step(V.tensor_reduce(st[:, 0:1], p[:, 0:n], AX_X, ALU.max))
                        V.tensor_scalar(st[:, 1:2], st[:, 0:1], -1.0, None, ALU.mult).then_inc(max_ready, 1)
                    else:
                        step(V.tensor_reduce(st[:, 0:1], bank[:, 0:n], AX_X, ALU.max))
                        V.tensor_scalar(st[:, 1:2], st[:, 0:1], -HD ** -0.5, None, ALU.mult).then_inc(max_ready, 1)

                def divide(u):
                    n = keys(u)
                    st = stat[:, u % 4, :]
                    if scaled:
                        dve.wait_ge(exp_done, base + u + 1)
                    else:
                        B.moved(dve, (tag, "s", u))
                    step(V.reciprocal(st[:, 3:4], st[:, 2:3]))
                    p = pbuf[:, u % 3, 0:n]
                    V.tensor_scalar(p, p, st[:, 3:4], None, ALU.mult).then_inc(prob_ready, 1)

                def stage(i):
                    if i < 2 * HQ:
                        maxima(i)
                    if 1 <= i <= 2 * HQ:
                        divide(i - 1)
                return stage
            stage = attention("a1", 0, lambda u: 512, False, prob)
            for i in range(2 * HQ):
                if i < 12:
                    conv_sides(i)
                if i == 0:
                    qk_norm()
                elif i == 1:
                    qk_rotary()
                elif i > 2:
                    stage(i - 3)
            for i in range(2 * HQ - 3, 2 * HQ + 1):
                stage(i)

            bank = A.full(dve, "ab")
            dve.wait_ge(gc_landed, 64)
            bias = gconst[:, 1, :].rearrange("p (a d h) -> p a d h", a=1, d=2).to_broadcast([P, 4, 2, 4])
            ins = V.tensor_tensor(gates[:, G_T0, :].rearrange("p (d t h) -> p t d h", d=2, t=4),
                                  bank[:, 0:64].rearrange("p (t x d h) -> p t x d h", t=4, x=2, d=2)[:, :, 0, :, :],
                                  bias, ALU.add)
            A.free("ab", ins)
            A.moved(dve, "ab", 1)
            V.scalar_tensor_tensor(out=gates[:, G_T1, :], in0=gates[:, G_T0, :], scalar=-1.0, in1=gates[:, G_T0, :],
                                   op0=ALU.mult, op1=ALU.max).then_inc(sp_abs, 1)
            dve.wait_ge(sp_ln, 1)
            V.tensor_scalar(gates[:, G_EA, 0:8], gates[:, G_EA, 0:8], -1.0, None, ALU.mult)
            step(V.scalar_tensor_tensor(out=gates[:, G_T0, :], in0=gates[:, G_T0, :], scalar=0.0, in1=gates[:, G_T1, :],
                                        op0=ALU.max, op1=ALU.add))
            ea = gates[:, G_EA, 0:8].rearrange("p (d a h) -> p d a h", d=2, a=1).to_broadcast([P, 2, 4, 4])
            V.tensor_tensor(gates[:, G_G, :].rearrange("p (d t h) -> p d t h", d=2, t=4),
                            gates[:, G_T0, :].rearrange("p (d t h) -> p d t h", d=2, t=4), ea, ALU.mult).then_inc(g_ready, 1)

            for i in range(8):
                wd = T if i < 4 else 512
                r = hroot[:, i % 2, 0:wd]
                A.moved(dve, ("l2", i))
                step(V.reciprocal(r, r))
                x = qF[:, i, :] if i < 4 else kF[:, i - 4, :]
                V.tensor_tensor(x, x, r, ALU.mult).then_inc(l2_ready, 1)

            norm(2)

            bank = A.full(dve, "gc")
            V.tensor_copy(gates[:, G_CUM, :], bank[:, 0:32])
            V.tensor_scalar(gates[:, G_NCUM, :], bank[:, 0:32], -1.0, None, ALU.mult)
            A.free("gc", V.tensor_copy(gates[:, G_TOT, :], bank[:, 32:64]))
            A.moved(dve, "gc")
            V.tensor_tensor(gates[:, G_T0, :], gates[:, G_TOT, :], gates[:, G_CUM, :], ALU.subtract).then_inc(tmg_ready, 1)
            dve.wait_ge(gate_ready, 1)
            V.tensor_scalar(gates[:, G_NEG, :], gates[:, G_EG, :], -1.0, None, ALU.mult).then_inc(ngl_ready, 1)

            heads = lambda ap: ap.rearrange("p (a b) -> p a b", a=4)

            def prepare(half):
                for s, d in GROUPS[half]:
                    g, tt = 2 * s + d, TILE[d][s]
                    way = ("fwd", "bwd")[d]
                    bank = A.full(dve, ("gb", g))
                    ins = V.scalar_tensor_tensor(out=heads(dec[:, g % 4, :]), in0=heads(bank[:, :]), scalar=-1.0,
                                                 in1=over(c_one("strict_" + way), 4), op0=ALU.mult, op1=ALU.add)
                    if tt < 2:
                        ins = V.tensor_tensor(heads(ATm[:, g % 4, :]), heads(bank[:, :]), over(c_one("incl_" + way), 4), ALU.add)
                    A.free(("gb", g), ins)
                    if g % 4:
                        lower(g - 1)
                lower(g)

            def lower(g):
                s, d = g // 2, g % 2
                tt = TILE[d][s]
                dve.wait_ge(dec_ready, g + 1)
                bank = A.full(dve, ("kk", g))
                for h in range(4):
                    c = slice(h * P, (h + 1) * P)
                    ins = V.scalar_tensor_tensor(out=dec[:, g % 4, c], in0=bank[:, c], scalar=gcol(G_BETA, d, tt, h),
                                                 in1=dec[:, g % 4, c], op0=ALU.mult, op1=ALU.mult)
                A.free(("kk", g), ins)
                if tt < 2:
                    dve.wait_ge(att_ready, g - 3)
                    n = ("kq", g)
                    B.free(n, V.tensor_tensor(ATm[:, g % 4, :], B.full(dve, n)[:, :], ATm[:, g % 4, :], ALU.mult))

            def level(half, lv):
                for s, d in GROUPS[half]:
                    n = ("m1", 2 * s + d, lv)
                    A.free(n, V.tensor_tensor(heads(dec[:, n[1] % 4, :]), heads(A.full(dve, n)[:, :]),
                                              over(c_one("level", P, lv), 4), ALU.mult))
                for s, d in GROUPS[half]:
                    g, tt = 2 * s + d, TILE[d][s]
                    if lv < 6:
                        n = ("dt", g, lv)
                        A.free(n, V.tensor_tensor(Tm[:, g % 4, :], Tm[:, g % 4, :], A.full(dve, n)[:, :], ALU.subtract))
                    n = ("dtt", g, lv)
                    A.free(n, V.tensor_tensor(TTm[:, g, :], TTm[:, g, :], A.full(dve, n)[:, :], ALU.subtract))
                    if lv == 6:
                        A.moved(dve, n)
                        for h in range(4):
                            c = slice(h * P, (h + 1) * P)
                            ins = V.tensor_scalar(TTm[:, g, c], TTm[:, g, c], gcol(G_BETA, d, tt, h), None, ALU.mult)
                        ins.then_inc(ttb_ready, 1)

            def advance(s):
                for d in range(2):
                    g, tt = 2 * s + d, TILE[d][s]
                    if tt < 2:
                        n = ("og", g)
                        bank = B.full(dve, n)
                        o = oG[:, :, tt * P:(tt + 1) * P]
                        if s == 2:
                            ins = V.tensor_copy(o, heads(bank[:, :]))
                        else:
                            B.moved(dve, ("og", 5 - d))
                            ins = V.tensor_tensor(o, heads(bank[:, :]), o, ALU.add)
                        B.free(n, ins)
                    if s < 3:
                        n = ("st", g)
                        bank = A.full(dve, n)
                        if s == 0:
                            ins = V.tensor_copy(S[:, d, :], bank[:, :])
                        else:
                            A.moved(dve, ("st", g - 2))
                            for h in range(4):
                                c = slice(h * P, (h + 1) * P)
                                ins = V.scalar_tensor_tensor(out=S[:, d, c], in0=S[:, d, c], scalar=gcol(G_DL, d, tt, h),
                                                             in1=bank[:, c], op0=ALU.mult, op1=ALU.add)
                        A.free(n, ins)

            def fill_place(n):
                if n < 16:
                    fill(0, 8 + n)
                if n >= 1:
                    ada(0, 7 + n)
            for what, *args in DELTA:
                dict(prepare=prepare, level=level, advance=advance, fill=fill_place)[what](*args)
            C.moved(dve, ("ada", 0, 23))
            step(gain(2, m1[:, 32:40, 0], v(0, V_N2, 8)))

            def gains2(l):
                A.moved(dve, ("ada", 1 + l, 23))
                gain(3 + 2 * l, m2[:, l, 8:16], v(1, V_NMIX + 8 * l, 8))
                step(gain(4 + 2 * l, m2[:, l, 32:40], v(1, V_NFFN + 8 * l, 8)))

            def head_norm(j, o, gains, gate, dst):
                for i in range(2):
                    A.moved(dve, ("hn", j, i))
                    step(V.reciprocal(hroot[:, i, :], hroot[:, i, :]))
                    for h in (2 * i, 2 * i + 1):
                        ins = V.scalar_tensor_tensor(out=o[:, h, :], in0=o[:, h, :], scalar=gains(h),
                                                     in1=hroot[:, i, (h % 2) * T:(h % 2 + 1) * T], op0=ALU.mult, op1=ALU.mult)
                    step(ins)
                    for h in (2 * i, 2 * i + 1):
                        V.tensor_tensor(dst[:, 4 + h, :], o[:, h, :], gate[:, h, :], ALU.mult).then_inc(hn_out, 1)
            dve.wait_ge(hn_sq, 1)
            head_norm(0, oG, lambda h: v(0, V_GDNG), zs, mixT)

            def residual(jobs, gate):
                for dt, (rg, name, part) in enumerate(jobs):
                    bank = rg.full(dve, name)
                    ins = V.scalar_tensor_tensor(out=xT[:, dt, :], in0=bank[:, part * T:(part + 1) * T],
                                                 scalar=gate[:, dt:dt + 1], in1=xT[:, dt, :], op0=ALU.mult, op1=ALU.add)
                    if dt == KT - 1 or jobs[dt + 1][1] != name:
                        rg.free(name, ins)

            def acc_jobs(tag):
                return [(B if dt < 6 else C, (tag, "acc", dt // 2), dt % 2) for dt in range(KT)]
            residual([(A, ("xo1", dt), 0) for dt in range(KT)], m1[:, 16:24, 0])
            norm(3)
            for f in range(FT + 3):
                if f < FT:
                    n = ("ffn1", "gu", f)
                    bank = A.full(dve, n)
                    dve.wait_ge(centre_ready, 12 + f + 1)
                    y = yc[:, f % 3, :]
                    side_taps([y[:, 0:T], y[:, T:512]], [bank[:, 0:T], bank[:, T:512]],
                              [v(1, V_FW01 + f), v(1, V_FW01 + FT + f)], [v(2, V_FW2 + f), v(2, V_FW2 + FT + f)],
                              lambda ins: A.free(n, ins))
                if 1 <= f <= FT:
                    y = yc[:, (f - 1) % 3, :]
                    dve.wait_ge(silu_ready, f)
                    V.tensor_tensor(gT[:, (f - 1) % 4, :], y[:, 0:T], y[:, T:512], ALU.mult).then_inc(gT_ready, 1)
                if f < 24:
                    fill(1, f)
                if f:
                    ada(1, f - 1)
            residual(acc_jobs("ffn1"), m1[:, 40:48, 0])
            gains2(0)
            norm(4)

            dve.wait_ge(con2_landed, 16)
            for l in range(2):
                n0 = 5 + 3 * l
                norm(n0)
                stage = attention(("a2", l), 16 * l, lambda u: (u % 2 + 1) * P, True, prob2, c_two("causal"))
                for i, (kind, _, j) in enumerate(SLOTS2):
                    if kind == "rr":
                        x = (qR if j < 2 else kR)[:, 2 * (j % 2):2 * (j % 2) + 2, :]
                        rotary(A, (l, "rr", j), x, c_two("cos", T), c_two("sin", T),
                               rtmp[:, j % 2, :].rearrange("p (a b) -> p a b", a=2), rrope)
                    stage(i)
                norm(n0 + 1)
                for h in range(4):
                    n = (l, "rs", h)
                    B.free(n, V.tensor_tensor(AR[:, h % 2, 0:384], B.full(dve, n)[:, 0:384],
                                              c_two("ret", 384, h * 384), ALU.mult))
                dve.wait_ge(sg_ready, l + 1)
                head_norm(1 + l, oR, lambda h: v(3, V_RETG + 4 * l + h), sgr, mix2)
                residual([(A, (("xo2", l), dt), 0) for dt in range(KT)], m2[:, l, 16:24])
                norm(n0 + 2)
                if l == 0:
                    for f in range(FT + 3):
                        if f < FT:
                            n = ("ffn2", "gu", f)
                            bank = A.full(dve, n)
                            dve.wait_ge(silu_ready, FT + f + 1)
                            A.free(n, V.tensor_tensor(gT[:, f % 4, :], yc[:, f % 3, 0:T], bank[:, T:512], ALU.mult))
                        if f < 24:
                            fill(2, f)
                        if f:
                            ada(2, f - 1)
                    residual(acc_jobs("ffn2"), m2[:, 0, 40:48])
                    gains2(1)

            bank = A.full(dve, "logits")
            A.free("logits", V.tensor_copy(rout[:, 0:2, :], bank[:, 0:16].rearrange("p (a b) -> p a b", a=2)))
            A.moved(dve, "logits")
            R = lambda i, tt, a=0, b=8: rout[:, i + tt, a:b]
            both = range(TT)
            for tt in both:
                ins = V.max(R(2, tt), R(0, tt))
            step(ins)
            for tt in both:
                V.max_index(idx_u[:, tt, :], R(2, tt), R(0, tt))
                ins = V.tensor_tensor(R(12, tt, 0, 1), R(2, tt, 0, 1), R(2, tt, 1, 2), ALU.subtract)
            ins.then_inc(top_ready, 1)
            dve.wait_ge(top_ready, 1)
            for tt in both:
                ins = V.tensor_copy(R(6, tt), idx_u[:, tt, :])
            step(ins)
            for tt in both:
                V.tensor_scalar(R(8, tt), c_all("iota", 8), R(6, tt, 0, 1), None, ALU.is_equal)
                ins = V.tensor_scalar(R(10, tt), c_all("iota", 8), R(6, tt, 1, 2), None, ALU.is_equal)
            step(ins)
            for tt in both:
                ins = V.tensor_tensor(R(4, tt), R(8, tt), R(10, tt), ALU.add)
            ins.then_inc(sel_ready, 1)
            dve.wait_ge(wt_ready, 1)
            for tt in both:
                ins = V.tensor_scalar(R(16, tt), R(8, tt), R(14, tt, 0, 1), None, ALU.mult)
            step(ins)
            for tt in both:
                ins = V.scalar_tensor_tensor(out=R(16, tt), in0=R(10, tt), scalar=R(14, tt, 1, 2), in1=R(16, tt),
                                             op0=ALU.mult, op1=ALU.add)
            step(ins)
            dve.wait_ge(sel_ready, 1)
            bank = A.full(dve, "pos")
            for tt in both:
                V.scalar_tensor_tensor(out=R(18, tt), in0=bank[:, tt * 8:(tt + 1) * 8], scalar=1.0, in1=R(4, tt),
                                       op0=ALU.add, op1=ALU.mult)
            A.free("pos", V.tensor_copy(cnt_i[:, :], bank[:, 16:24]))
            A.moved(dve, "pos")
            for tt in both:
                ins = V.tensor_scalar(R(18, tt), R(18, tt), -1.0, None, ALU.add)
            step(ins)
            for e in range(NE):
                for tt in both:
                    V.tensor_scalar(Pg[:, tt, e, :], c_all("iota", 256), R(18, tt, e, e + 1), None, ALU.is_equal)
                if e >= 2:
                    A.full(dve, ("pwT", e - 2))
                for tt in both:
                    ins = V.tensor_scalar(Pw[:, e % 2, tt * 256:(tt + 1) * 256], c_all("iota", 256), R(18, tt, e, e + 1),
                                          R(16, tt, e, e + 1), ALU.is_equal, ALU.mult)
                ins.then_inc(pw_ready, 1)
            V.memset(facc, 0.0).then_inc(moved, 2)
            V.memset(stat[:, 0, 0:1], 0.0).then_inc(gated, 2)

            def expert(e, ns):
                for j in range(KT):
                    dve.wait_ge(xj_full, e * 16 + (j + 1))
                    V.tensor_copy(xg[:, j, 0:ns], banks[2 + j % 2][:, 0:ns]).then_inc(moved, 1)
                for f in range(FT):
                    dve.wait_ge(sge_ready, e * FT + (f + 1))
                    V.tensor_tensor(gTe[:, f % 4, 0:ns], sge[:, f % 2, 0:ns], banks[f % 2][:, ns:2 * ns],
                                    ALU.mult).then_inc(gated, 1)
                for j in range(KT):
                    dve.wait_ge(xj_full, e * 16 + (KT + j + 1))
                    V.tensor_tensor(facc[:, j, :], banks[2 + j % 2][:, 0:T], facc[:, j, :], ALU.add).then_inc(moved, 1)

            with dve.Fori(0, NE) as e:
                count = dve.value_load(cnt_i[0:1, bass.ts(e, 1)], min_val=0, max_val=T)
                with dve.If(count > NARROW):
                    expert(e, T)
                with dve.Else():
                    expert(e, NARROW)
                dve.nop()
            dve.wait_ge(moved, 16 * NE + 2)
            for dt in range(KT):
                V.scalar_tensor_tensor(out=xT[:, dt, :], in0=facc[:, dt, :], scalar=m2[:, 1, 40 + dt:41 + dt],
                                       in1=xT[:, dt, :], op0=ALU.mult, op1=ALU.add).then_inc(x_updated, 1)
            norm(11)
            for i in range(4):
                dve.wait_ge(fin_ready, i + 2)
                V.tensor_copy(outT[:, i // 2, (i % 2) * 512:(i % 2 + 1) * 512], banks[4 + i][:, :]).then_inc(out_ready, 1)

        @block.gpsimd
        def _(pool):
            steps = [0]
            G = nc.gpsimd

            def step(ins):
                steps[0] += 1
                ins.then_inc(pool_step, 1)
                pool.wait_ge(pool_step, steps[0])
            heads = lambda ap: ap.rearrange("p (a b) -> p a b", a=4)
            pool.wait_ge(con_landed, 16)
            pool.wait_ge(con1_landed, 16)
            pool.wait_ge(ngl_ready, 1)
            for h in range(4):
                A.moved(pool, ("ktm", h))

            def seeds(half):
                for s, d in GROUPS[half]:
                    g = 2 * s + d
                    nb, eye = over(c_one("level"), 4), over(ident, 4)
                    A.moved(pool, ("kk", g))
                    G.tensor_tensor(heads(Tm[:, g % 4, :]), heads(dec[:, g % 4, :]), nb, ALU.mult)
                    A.moved(pool, ("lt", g))
                    step(G.tensor_tensor(heads(TTm[:, g, :]), heads(LTm[:, g % 4, :]), nb, ALU.mult))
                    G.tensor_tensor(heads(Tm[:, g % 4, :]), heads(Tm[:, g % 4, :]), eye, ALU.add)
                    G.tensor_tensor(heads(TTm[:, g, :]), heads(TTm[:, g, :]), eye, ALU.add).then_inc(seed_ready, 1)

            def keys(s):
                for d in range(2):
                    g, tt = 2 * s + d, TILE[d][s]
                    if s:
                        A.full(pool, ("st", g - 2))
                    for h in range(4):
                        c = slice(h * P, (h + 1) * P)
                        G.tensor_scalar(kbe[:, d, c], k_tm[:, tt, h, :], gcol(G_NEG, d, tt, h), None, ALU.mult)
                        ins = G.tensor_scalar(kdec[:, d, c], k_tm[:, tt, h, :], gcol(G_KD, d, tt, h), None, ALU.mult)
                    ins.then_inc(kb_ready, 1)
            seeds(0)
            keys(0)
            seeds(1)
            for g in range(4, 8):
                tt = TILE[g % 2][g // 2]
                A.moved(pool, ("gb", g))
                G.tensor_tensor(heads(qdec[:, g % 4, :]), qF[:, :, tt * P:(tt + 1) * P], heads(egb[:, g % 4, :]),
                                ALU.mult).then_inc(qdec_ready, 1)
            for s in range(1, 4):
                keys(s)

        @block.sync
        def _(sp):
            sp.dma_start(con[:, :], t["constants"][:, 0:C_ALL_W]).then_inc(con_landed, 16)
            sp.dma_start(xraw[:, 0:2, :], t["x"][0].rearrange("(a p) n -> p a n", p=P)).then_inc(x_landed, 16)
            sp.dma_start(xraw[:, 2:4, :], t["ctx"][0].rearrange("(a p) n -> p a n", p=P)).then_inc(x_landed, 16)
            for k, (name, ap) in enumerate(units):
                if need[k]:
                    sp.wait_ge(unit_used, need[k])
                n = ap.shape[1]
                sp.dma_start(ring[:, slot[k], :].rearrange("p (a b) -> p a b", a=n), ap).then_inc(landed[slot[k]], 16)
            src = dict(g=t["moe_w_gate_2"], u=t["moe_w_up_2"], d=t["moe_w_down_2"])
            with sp.Fori(0, NE) as e:
                for (m, c), j in e_order.items():
                    k = U0 + j
                    w = src[m][0][e, :, :]
                    ap = w_rows(w, c) if m == "d" else w_cols(w, c)
                    sp.wait_ge(unit_used, e * EU + (k - RING + 1))
                    sp.dma_start(ring[:, slot[k], :].rearrange("p (a b) -> p a b", a=ap.shape[1]), ap).then_inc(landed[slot[k]], 16)
            for tt in range(TT):
                sp.wait_ge(out_ready, 2 * tt + 2)
                sp.dma_start(out[0, tt * P:(tt + 1) * P, :], outT[:, tt, :]).then_inc(out_landed, 16)
            sp.wait_ge(out_landed, 16 * TT)


_INS = ["x", "c", "ctx", "c_ctx", "w_mod", "b_mod", "norm1_g", "w_in", "q_norm_g", "k_norm_g", "attn_out_g",
        "conv_qkv_w", "a_log_f", "a_log_b", "dt_bias_f", "dt_bias_b", "gdn_norm_g", "w_out", "norm2_g", "w_up",
        "ffn_conv_w", "ffn_conv_b", "w_down", "final_norm_g", "c_2", "norm_mix_g_2", "norm_ffn_g_2", "ada_w_2",
        "ada_b_2", "w_in_2", "w_out_2", "att_out_g_2", "ret_out_g_2", "ffn_w_gate_2", "ffn_w_up_2",
        "ffn_w_down_2", "router_w_2", "moe_w_gate_2", "moe_w_up_2", "moe_w_down_2", "final_norm_g_2"]


def kernel(**inputs):
    import concourse.bacc as _bacc
    from concourse.bass_utils import run_bass_kernel_spmd as _run

    nc = _bacc.Bacc("TRN2", target_bir_lowering=False, num_devices=1, dynamic_dma_scratch_size=1024)
    arrays, t = {}, {}
    for name in _INS + ["constants"]:
        a = shape_constants() if name == "constants" else np.ascontiguousarray(inputs[name])
        arrays[f"in_{name}_dram"] = a
        t[name] = nc.dram_tensor(f"in_{name}_dram", a.shape, mybir.dt.from_np(a.dtype), kind="ExternalInput").ap()
    out = nc.dram_tensor("out_0_dram", (1, T, D), F32, kind="ExternalOutput").ap()
    build(nc, t, out)
    r = _run(nc, [arrays], core_ids=[0])
    return r.results[0]["out_0_dram"]
```

```python
from contextlib import ExitStack

import numpy as np

import concourse.bass as bass
from concourse import mybir

ALU = mybir.AluOpType
ACT = mybir.ActivationFunctionType
F32 = mybir.dt.float32
F32R = mybir.dt.float32r
I32 = mybir.dt.int32
U32 = mybir.dt.uint32
AX_X = mybir.AxisListType.X

P = 128
D = 1024
KT = D // P
T = 256
TT = T // P
EPS = 1e-6
NEG = -1e30

HD = 64
GH = 4
MIX_T = 4
GRID_W = 64
FF = 2816
UW = 256
FC = FF // UW
FT = FF // P
NE = 8
RING = 11
RING1 = 8
HALVES = 11
HW = KT * UW // 2
NARROW = 128

C_ALL = dict(ident=0, ones=128, ustrict=256, iota=384)
C_ALL_W = 640
C_ONE = dict(ones64=0, rot64=128, sel=256, u_fwd=512, u_bwd=640, strict_fwd=768, strict_bwd=896,
             incl_fwd=1024, incl_bwd=1152, level=1280, cos=2176, sin=2432)
C_ONE_W = 2688
C_TWO = dict(rot128=0, cos=128, sin=384, ret=640, causal=2176)
C_TWO_W = 2304

V_C, V_CCTX, V_BMOD, V_N1, V_ATTG, V_GDNG, V_N2, V_CONV, V_QG, V_KG = 0, 8, 16, 64, 72, 76, 77, 85, 121, 122
V0_ROWS = 123
V_FW01, V_C2, V_NMIX, V_NFFN = 0, 88, 96, 112
V1_ROWS = 128
V_FW2, V_FB, V_FIN1, V_FIN2 = 0, 44, 88, 96
V2_ROWS = 104
V_BADA, V_ATTG2, V_RETG = 0, 96, 104
V3_ROWS = 112
V_LOADS = 14


def shape_constants():
    i = np.arange(P)
    row, col = i[:, None], i[None, :]
    f = np.float32
    allc = np.zeros((P, C_ALL_W), f)
    allc[:, 0:128] = np.eye(P)
    allc[:, 128:256] = 1.0
    allc[:, 256:384] = row < col
    allc[:, 384:640] = np.arange(256)[None, :]

    def rotation(hd):
        r = np.zeros((P, P), f)
        for m in range(P):
            if m % hd < hd // 2:
                r[m + hd // 2, m] = -1.0
            else:
                r[m - hd // 2, m] = 1.0
        return r

    one = np.zeros((P, C_ONE_W), f)
    c = C_ONE
    one[:, c["ones64"]:c["ones64"] + P] = (row // HD) == (col // HD)
    one[:, c["rot64"]:c["rot64"] + P] = rotation(HD)
    for kv in range(2):
        one[:, c["sel"] + kv * P:c["sel"] + (kv + 1) * P] = row == (HD * kv + col % HD)
    one[:, c["u_fwd"]:c["u_fwd"] + P] = row <= col
    one[:, c["u_bwd"]:c["u_bwd"] + P] = row >= col
    one[:, c["strict_fwd"]:c["strict_fwd"] + P] = np.where(row > col, 0, NEG)
    one[:, c["strict_bwd"]:c["strict_bwd"] + P] = np.where(row < col, 0, NEG)
    one[:, c["incl_fwd"]:c["incl_fwd"] + P] = np.where(row <= col, 0, NEG)
    one[:, c["incl_bwd"]:c["incl_bwd"] + P] = np.where(row >= col, 0, NEG)
    for lv in range(7):
        s = 1 << lv
        pair = (row // (2 * s) == col // (2 * s)) & (row // s != col // s)
        one[:, c["level"] + lv * P:c["level"] + (lv + 1) * P] = pair * (-1.0 if lv == 0 else 1.0)
    t = np.arange(T)
    quarter = HD // 4
    inv = 10000.0 ** (-np.arange(quarter, dtype=f) / f(quarter))
    inv = inv.astype(f)
    ang = np.concatenate([(t // GRID_W).astype(f)[:, None] * inv, (t % GRID_W).astype(f)[:, None] * inv], 1)
    lane = (i % HD) % (HD // 2)
    one[:, c["cos"]:c["cos"] + T] = np.cos(ang).T[lane]
    one[:, c["sin"]:c["sin"] + T] = np.sin(ang).T[lane]

    two = np.zeros((P, C_TWO_W), f)
    c = C_TWO
    two[:, 0:P] = rotation(P)
    half = P // 2
    inv = (10000.0 ** (-np.arange(half, dtype=f) / f(half))).astype(f)
    ang = t.astype(f)[:, None] * inv[None, :]
    two[:, c["cos"]:c["cos"] + T] = np.cos(ang).T[i % half]
    two[:, c["sin"]:c["sin"] + T] = np.sin(ang).T[i % half]
    for h in range(GH):
        lg = np.log(1.0 - 2.0 ** (-5.0 - h))
        for b, (j0, i0, n) in enumerate(((0, 0, 256), (128, 128, 128))):
            dist = (i0 + np.arange(n))[None, :] - (j0 + i)[:, None]
            m = np.where(dist >= 0, np.exp(np.maximum(dist, 0) * lg), 0.0) * P ** -0.5
            at = c["ret"] + h * 384 + b * 256
            two[:, at:at + n] = m
    two[:, c["causal"]:c["causal"] + P] = np.where(col <= row, 0, NEG)
    return np.concatenate([allc, one, two], 1)


class BankRing:

    def __init__(self, banks, full, free):
        self.banks, self.sem_full, self.sem_free = banks, full, free
        self.taken = 0
        self.uses = [0] * len(banks)
        self.frees = [0] * len(banks)
        self.where = {}

    def take(self, pe, name, readers=1):
        b = self.taken % len(self.banks)
        if self.frees[b]:
            pe.wait_ge(self.sem_free[b], self.frees[b])
        self.taken += 1
        self.uses[b] += 1
        self.frees[b] += readers
        self.where[name] = (b, self.uses[b], self.frees[b])
        return self.banks[b]

    def done(self, name, ins):
        ins.then_inc(self.sem_full[self.where[name][0]], 1)

    def full(self, eng, name):
        b, n, _ = self.where[name]
        eng.wait_ge(self.sem_full[b], n)
        return self.banks[b]

    def free(self, name, ins):
        ins.then_inc(self.sem_free[self.where[name][0]], 1)

    def moved(self, eng, name, but=0):
        b, _, n = self.where[name]
        eng.wait_ge(self.sem_free[b], n - but)

    def all_free(self, pe):
        for b, n in enumerate(self.frees):
            if n:
                pe.wait_ge(self.sem_free[b], n)


def build(nc, t, out):
    ctx = ExitStack()
    with ctx:
        def sb(name, shape, dt=F32):
            return ctx.enter_context(nc.sbuf_tensor(name, shape, dt))

        def sem(name):
            return ctx.enter_context(nc.semaphore(name))

        banks = [ctx.enter_context(nc.psum_tensor(f"bank{b}", [P, 512], F32)) for b in range(8)]

        con = sb("con", [P, C_ALL_W])
        con2 = sb("con2", [P, C_ONE_W])
        vec = sb("vec", [P, 4, P])
        xT = sb("xT", [P, KT, T])[:, :, :]
        sq = sb("sq", [P, 2048])
        rstd = sb("rstd", [P, T])
        hroot = sb("hroot", [P, 2, 512])
        m1 = sb("m1", [P, 48, 2])
        m2 = sb("m2", [P, 2, 48])
        amul = sb("amul", [P, 7, 8])
        cs = sb("cs", [P, 8, 2])
        cs2 = sb("cs2", [P, 8])
        wab = sb("wab", [P, KT, 16])
        wrt = sb("wrt", [P, KT, NE])
        gconst = sb("gconst", [P, 2, 8])
        gates = sb("gates", [P, 12, 32])
        stat = sb("stat", [P, 4, 4])
        facc2 = sb("facc2", [P, 2, 2, UW])
        cnt_i = sb("cnt_i", [P, 8], I32)
        idx_u = sb("idx_u", [P, 2, 8], U32)
        ARENA = 23296
        XG_AT, G_AT = 12288, 18432
        with nc.sbuf_tensor("ring", [P, RING, KT * UW], F32) as ring, nc.sbuf_tensor("arena", [P, ARENA], F32) as arena:
            pass
        ring_parts = sb("ring_parts", [P, RING, KT * UW], F32R)
        sb("before_xg", [P, XG_AT])
        xg_parts = sb("xg_parts", [P, 2, KT, 256], F32R)
        sb("before_g", [P, G_AT - XG_AT - 2 * KT * 256])
        g_parts = sb("g_parts", [P, 2, 2, 512], F32R)

        def at(a, *shape):
            n = int(np.prod(shape))
            assert a + n <= ARENA, (a, n)
            v = arena[:, a:a + n]
            if len(shape) == 2:
                return v.rearrange("p (a b) -> p a b", a=shape[0])
            if len(shape) == 3:
                return v.rearrange("p (a b c) -> p a b c", a=shape[0], b=shape[1])
            return v

        def c_all(name, w=P):
            return con[:, C_ALL[name]:C_ALL[name] + w]

        def c_one(name, w=P, i=0):
            a = C_ONE[name] + i * P
            return con2[:, a:a + w]

        def c_two(name, w=P, i=0):
            a = C_TWO[name] + i
            return con2[:, a:a + w]

        ident, ones = c_all("ident"), c_all("ones")

        def over(ap, n):
            w = ap.shape[-1]
            return ap.rearrange("p (a w) -> p a w", a=1).to_broadcast([ap.shape[0], n, w])

        mixT = at(0, 8, T)
        zs = at(2048, 4, T)
        qF = at(3072, 4, T)
        kF = at(4096, 4, 512)
        k_tm = at(6144, 4, 4, P)
        v_tm = at(8192, 4, 4, P)
        G0 = 10240
        hT = at(G0, KT, 512)
        xraw = at(G0 + 4096, 4, D)
        ctxT = at(G0 + 8192, KT, T)
        vrows = at(G0 + 10240, 512)
        ybuf = at(G0 + 10240, 4, 512)
        qA = at(G0 + 4096, 4, T)
        kA = at(G0 + 7168, 512)
        vA = at(G0 + 6656, 4, P)
        extra = ring[:, RING1:RING, :].rearrange("p a b -> p (a b)")

        def ex(a, n, w):
            return extra[:, a:a + n * w].rearrange("p (a b) -> p a b", a=n)
        kdup = ex(0, 2, 512)
        prob = ex(1024, 3, 512)
        probT = ex(2560, 2, 512)
        oA = ex(3584, 4, T)
        atmp = ex(4608, 2, 512)
        kroot = extra[:, 5632:6144]
        TTm = at(G0 + 0, 8, 512)
        Tm = at(G0 + 4096, 4, 512)
        LTm = at(G0 + 6144, 4, 512)
        dec = at(G0 + 8192, 4, 512)
        kbe = at(G0 + 10240, 2, 512)
        kdec = at(G0 + 11264, 2, 512)
        S = hroot[:, :, :]
        ATm = ex(0, 4, 512)
        qdec = ex(2048, 4, 512)
        nwT = ex(4096, 2, 512)
        vnew = ex(5120, 2, 512)
        egb = sq[:, :].rearrange("p (a b) -> p a b", a=4)
        oG = mixT[:, 4:8, :]
        hF = at(0, KT, T)
        gT = at(2048, 4, T)
        yc = at(3072, 3, 512)
        h2 = at(0, KT, T)
        mix2 = at(2048, 8, T)
        qA2 = at(4096, 4, T)
        kA2 = at(5120, 4, T)
        vA2 = at(6144, 2, 512)
        qR = at(7168, 4, T)
        kR = at(8192, 4, T)
        vR = at(9216, 2, 512)
        sgr = at(10240, 4, T)
        prob2 = at(11264, 3, 512)
        probT2 = at(12800, 2, 512)
        oA2 = at(13824, 4, T)
        rtmp = at(14848, 2, 512)
        AR = at(15872, 2, 512)
        oR = at(16896, 4, T)
        facc = at(0, KT, T)
        Pg = at(2048, 2, NE, 256)
        PwT = at(6144, 2, NE, 256)
        h_tm = at(10240, 2, D)
        xgH, xgL = xg_parts[:, 0, :, :], xg_parts[:, 1, :, :]
        ye = at(16384, 2, D)
        gH, gL = g_parts[:, 0, :, :], g_parts[:, 1, :, :]
        sge = at(20480, 2, 512)
        Pw = at(20480, 2, 512)
        hid = at(21504, 2, 512)
        rout = at(22528, 24, 8)
        outT = at(16384, 2, D)

        full = [sem(f"full{b}") for b in range(8)]
        free = [sem(f"free{b}") for b in range(8)]
        landed = [sem(f"landed{s}") for s in range(RING)]
        unit_used = sem("unit_used")
        x_landed, v0_landed, v_landed = sem("x_landed"), sem("v0_landed"), sem("v_landed")
        con_landed, con1_landed, con2_landed = sem("con_landed"), sem("con1_landed"), sem("con2_landed")
        gc_landed, wab_landed, wrt_landed = sem("gc_landed"), sem("wab_landed"), sem("wrt_landed")
        out_landed = sem("out_landed")
        dve_step, act_step, pool_step = sem("dve_step"), sem("act_step"), sem("pool_step")
        fill_ready = sem("fill_ready")
        cs_ready, sq_ready, root_ready, norm_out = sem("cs_ready"), sem("sq_ready"), sem("root_ready"), sem("norm_out")
        scaled = sem("scaled")
        x_updated = sem("x_updated")
        centre_ready, d_ready = sem("centre_ready"), sem("d_ready")
        sqd_ready, l2_ready = sem("sqd_ready"), sem("l2_ready")
        ansq, qk_normed, rope_done = sem("ansq"), sem("qk_normed"), sem("rope_done")
        max_ready, exp_done, prob_ready = sem("max_ready"), sem("exp_done"), sem("prob_ready")
        sp_abs, sp_ln, g_ready, tmg_ready, gate_ready, ngl_ready = (
            sem("sp_abs"), sem("sp_ln"), sem("g_ready"), sem("tmg_ready"), sem("gate_ready"), sem("ngl_ready"))
        dec_ready, att_ready, kb_ready, seed_ready, ttb_ready, qdec_ready = (
            sem("dec_ready"), sem("att_ready"), sem("kb_ready"), sem("seed_ready"),
            sem("ttb_ready"), sem("qdec_ready"))
        hn_sq, hn_out = sem("hn_sq"), sem("hn_out")
        silu_ready, gT_ready = sem("silu_ready"), sem("gT_ready")
        rrope, sg_ready = sem("rrope"), sem("sg_ready")
        top_ready, wt_ready, sel_ready, pw_ready = sem("top_ready"), sem("wt_ready"), sem("sel_ready"), sem("pw_ready")
        xj_full, moved, gu_full, gated = sem("xj_full"), sem("moved"), sem("gu_full"), sem("gated")
        sge_ready, xh_ready = sem("sge_ready"), sem("xh_ready")
        ye_ready = [sem("ye_left_ready"), sem("ye_right_ready")]
        turned_h, gh_ready, gl_ready = sem("turned_h"), sem("gh_ready"), sem("gl_ready")
        raw_landed = [sem(f"raw_landed{i}") for i in range(HALVES)]
        wh_ready, split_ready, pair_used = sem("wh_ready"), sem("split_ready"), sem("pair_used")
        out_ready = sem("out_ready")
        fin_ready = sem("fin_ready")

        A = BankRing(banks[0:4], full[0:4], free[0:4])
        B = BankRing(banks[4:7], full[4:7], free[4:7])
        C = BankRing(banks[7:8], full[7:8], free[7:8])

        w_cols = lambda w, u: w[:, u * UW:(u + 1) * UW].rearrange("(k p) n -> p k n", p=P)
        w_rows = lambda w, c: w[c * UW:(c + 1) * UW, :].rearrange("(k p) n -> p k n", p=P)
        units = []

        def add(name, ap):
            units.append((name, ap))

        def add_ffn(tag, gate, up, down, fill=None):
            for f in range(FT + 3):
                if f % 2 and f < FT:
                    add((tag, "g", f // 2), gate(f // 2))
                    add((tag, "u", f // 2), up(f // 2))
                if f and fill:
                    add(*fill(f - 1))
                if f % 2 and 3 <= f < FT + 2:
                    add((tag, "d", (f - 3) // 2), down((f - 3) // 2))

        for u in range(8):
            add(("mod", 0, u), w_cols(t["w_mod"][0], u))
        for u in range(11):
            add(("in1", u), w_cols(t["w_in"][0], u))
        for u in range(8, 24):
            add(("mod", 0, u), w_cols(t["w_mod"][0], u))
        for u in range(4):
            add(("out1", u), w_cols(t["w_out"][0], u))
        K1 = len(units)
        ada2 = lambda l: lambda u: (("mod", 1 + l, u), w_cols(t["ada_w_2"][l], u))
        add_ffn("ffn1", lambda c: w_cols(t["w_up"][0], c), lambda c: w_cols(t["w_up"][0], FC + c),
                lambda c: w_rows(t["w_down"][0], c), ada2(0))
        for l in range(2):
            for u in range(14):
                add(("in2", l, u), w_cols(t["w_in_2"][l], u))
            for u in range(4):
                add(("out2", l, u), w_cols(t["w_out_2"][l], u))
            if l == 0:
                add_ffn("ffn2", lambda c: w_cols(t["ffn_w_gate_2"][0], c), lambda c: w_cols(t["ffn_w_up_2"][0], c),
                        lambda c: w_rows(t["ffn_w_down_2"][0], c), ada2(1))
        U0 = len(units)
        order = {name: k for k, (name, _) in enumerate(units)}
        EU = 3 * FC
        e_order, e_steps = {}, []
        for i in range(FC + 2):
            if i < FC:
                e_steps += [("g", i), ("u", i)]
            if 1 <= i <= FC:
                e_steps.append(("turn", i - 1))
            if i >= 2:
                e_steps.append(("d", i - 2))
        for what in e_steps:
            if what[0] != "turn":
                e_order[what] = len(e_order)

        slot, turn, need, last = [], [], [], {}
        for k in range(U0):
            sl = k % RING1 if k < K1 else (k - K1) % RING
            before = last.get(sl)
            slot.append(sl)
            turn.append(1 if before is None else turn[before] + 1)
            need.append(before + 1 if before is not None else order["out1", 0] + 1 if k >= K1 else 0)
            last[sl] = k
        base = (U0 - K1) % RING
        assert all(slot[U0 - RING + i] == (base + i) % RING for i in range(RING))
        raw = [ring[:, (base + i // 2) % RING, (i % 2) * HW:(i % 2 + 1) * HW] for i in range(HALVES - 1)]
        raw.append(hroot[:, :, :].rearrange("p a b -> p (a b)"))
        pair_at = lambda s: ring_parts[:, s % RING, :]
        wH = [pair_at(base + 5 + 2 * i) for i in range(3)]
        wL = [pair_at(base + 6 + 2 * i) for i in range(3)]
        gather_bank = lambda j: banks[(6, 7, 1)[j % 3]]
        half_of = lambda w, i: w[:, (i % 2) * HW:(i % 2 + 1) * HW]
        assert EU % 3 == 0 and 2 * EU % HALVES == 0

        def v(i, r, n=1):
            return vec[:, i, r:r + n]

        def last_of(*name):
            return lambda eng, k: A.moved(eng, name) if k == 0 else None

        def tile_of(tag):
            return lambda eng, k: A.moved(eng, (tag, k))

        def pair_of(tag):
            return lambda eng, k: (B if k < 6 else C).moved(eng, (tag, "acc", k // 2)) if k % 2 == 0 else None

        norms = [
            dict(src=xT, nt=8, wait=last_of("xt", 0, 1, 1), gain=amul[:, 0, :], shift=m1[:, 0:8, 0], dst=hT[:, :, 0:T]),
            dict(src=ctxT, nt=8, wait=last_of("xt", 1, 1, 1), gain=amul[:, 1, :], shift=m1[:, 0:8, 1], dst=hT[:, :, T:512]),
            dict(src=oA, nt=4, wait=lambda eng, k: C.moved(eng, ("a1", "o", k)), gain=v(0, V_ATTG, 4), shift=None, dst=mixT[:, 0:4, :]),
            dict(src=xT, nt=8, wait=tile_of("xo1"), gain=amul[:, 2, :], shift=m1[:, 24:32, 0], dst=hF),
            dict(src=xT, nt=8, wait=pair_of("ffn1"), gain=v(2, V_FIN1, 8), shift=None, dst=xT),
        ]
        for l in range(2):
            norms += [
                dict(src=xT, nt=8, wait=(lambda eng, k: eng.wait_ge(norm_out, 28 + k + 1)) if l == 0 else pair_of("ffn2"),
                     gain=amul[:, 3 + 2 * l, :], shift=m2[:, l, 0:8], dst=h2),
                dict(src=oA2, nt=4, wait=(lambda l: lambda eng, k: C.moved(eng, (("a2", l), "o", k)))(l), gain=v(3, V_ATTG2 + 4 * l, 4), shift=None,
                     dst=mix2[:, 0:4, :]),
                dict(src=xT, nt=8, wait=tile_of(("xo2", l)), gain=amul[:, 4 + 2 * l, :], shift=m2[:, l, 24:32], dst=hF),
            ]
        norms.append(dict(src=xT, nt=8, wait=lambda eng, k: eng.wait_ge(x_updated, k + 1), gain=v(2, V_FIN2, 8), shift=None, dst=xT))
        total = 0
        for n in norms:
            total += n["nt"]
            n["out"] = total
            n["first"] = total - n["nt"]
        assert norms[4]["out"] == 36

        def root(n):
            return hroot[:, 0, 0:T] if n == 1 else rstd[:, 0:T]

        TILE = [[2, 3, 0, 1], [3, 2, 1, 0]]

        def gcol(buf, d, tt, h=0, n=1):
            a = (d * 4 + tt) * 4 + h
            return gates[:, buf, a:a + n]
        G_G, G_BETA, G_CUM, G_NCUM, G_TOT, G_EG, G_NEG, G_KD, G_DL, G_T0, G_T1, G_EA = range(12)

        HQ = 8
        GROUPS = [[(s, d) for s in (2 * half, 2 * half + 1) for d in range(2)] for half in range(2)]
        DELTA = [("prepare", 0)]
        for lv in range(1, 7):
            DELTA += [("level", 0, lv), ("fill", lv - 1)]
        DELTA += [("prepare", 1)]
        for lv in range(1, 7):
            DELTA += [("level", 1, lv), ("fill", 5 + lv)]
            if lv in (2, 4):
                DELTA += [("advance", lv // 2 - 1)]
        DELTA += [("fill", 12), ("fill", 13), ("advance", 2), ("fill", 14), ("fill", 15), ("advance", 3), ("fill", 16)]
        SLOTS2 = [("qr", 6, i) for i in range(4)] + [("kr", 8, i) for i in range(4)] + \
                 [("vr", 10, i) for i in range(2)] + [("gr", 12, i) for i in range(4)] + [("rr", 0, i) for i in range(4)]
        block = ctx.enter_context(nc.Block())

        @block.tensor
        def _(pe):
            mm = nc.tensor.matmul
            owed = [0]

            def owe():
                owed[0] += 1

            def pay(ins, used=unit_used):
                if owed[0]:
                    ins.then_inc(used, owed[0])
                    owed[0] = 0

            def unit(name):
                k = order[name]
                pe.wait_ge(landed[slot[k]], 16 * turn[k])
                return ring[:, slot[k], :]

            def ada_rows(u):
                w = unit(("mod", 0, u)).rearrange("p (k n) -> p k n", k=KT)
                bank = A.take(pe, ("ada", 0, u))
                for k in range(KT):
                    ins = mm(bank[0:2, 0:UW], cs[:, k, 0:2], w[:, k, :], start=k == 0, stop=k == KT - 1)
                    if k == 0:
                        pay(ins)
                owe()
                A.done(("ada", 0, u), ins)

            fills = [0]

            def fill_sum(rg, part, u):
                pe.wait_ge(fill_ready, fills[0] + 1)
                acc = facc2[:, fills[0] % 2, 0, :]
                fills[0] += 1
                bank = rg.take(pe, ("ada", part, u))
                for j in range(2):
                    ins = mm(bank[:, j:j + 1], acc[:, j * P:(j + 1) * P], ones[:, 0:1], start=True, stop=True)
                    if j == 0:
                        pay(ins)
                owe()
                rg.done(("ada", part, u), ins)

            new = []

            def new_tile(k):
                if new:
                    pe.wait_ge(norm_out, norms[new[0]]["first"] + k + 1)
                    if k == KT - 1:
                        new.pop()

            def norm_sum(n):
                N = norms[n]
                bank = A.take(pe, ("ss", n))
                for k in range(N["nt"]):
                    pe.wait_ge(sq_ready, N["first"] + k + 1)
                    ins = mm(bank[:, 0:T], ones, sq[:, k * T:(k + 1) * T], start=k == 0, stop=k == N["nt"] - 1)
                    if k == 0:
                        pay(ins)
                A.done(("ss", n), ins)

            def proj(name, w, j, h, width):
                bank = A.take(pe, name)
                for k in range(KT):
                    new_tile(k)
                    ins = mm(bank[:, 0:width], w[:, k, j * P:(j + 1) * P], h[:, k, 0:width],
                             start=k == 0, stop=k == KT - 1)
                    if k == 0:
                        pay(ins)
                A.done(name, ins)

            pe.wait_ge(con_landed, 16)
            pe.wait_ge(x_landed, 32)
            for s in range(2):
                for tt in range(TT):
                    for kg in range(2):
                        bank = A.take(pe, ("xt", s, tt, kg))
                        for k in range(4):
                            ins = nc.tensor.transpose(bank[:, k * P:(k + 1) * P],
                                                      xraw[:, 2 * s + tt, (4 * kg + k) * P:(4 * kg + k + 1) * P], ident)
                        A.done(("xt", s, tt, kg), ins)
            def turn_vectors(name, tables):
                bank = A.take(pe, name)
                for i in tables:
                    n = (V0_ROWS, V1_ROWS, V2_ROWS, V3_ROWS)[i]
                    ins = nc.tensor.transpose(bank[:, i * P:i * P + n], vrows[0:n, i * P:(i + 1) * P], ident[0:n, 0:n])
                A.done(name, ins)
            pe.wait_ge(v0_landed, 16 * 12)
            turn_vectors("vec0", (0,))
            norm_sum(0)
            norm_sum(1)
            pe.wait_ge(cs_ready, 1)
            for u in range(8):
                ada_rows(u)
            pe.wait_ge(v_landed, 16 * V_LOADS)
            turn_vectors("vec", (1, 2, 3))
            A.moved(pe, ("ada", 0, 7))
            bank = A.take(pe, "adat")
            for j in range(16):
                ins = nc.tensor.transpose(bank[:, 2 * j:2 * j + 2], sq[0:2, j * P:(j + 1) * P], ident[0:2, 0:2])
            A.done("adat", ins)

            def attention(tag, base, scores, values, pbuf, ptbuf):
                def score(u):
                    bank = B.take(pe, (tag, "s", u))
                    l, r, n = scores(u)
                    ins = mm(bank[:, 0:n], l, r, start=True, stop=True)
                    B.done((tag, "s", u), ins)

                def turn(u):
                    nk = scores(u)[2] // P
                    pe.wait_ge(prob_ready, base + u + 1)
                    bank = A.take(pe, (tag, "pt", u))
                    for k in range(nk):
                        ins = nc.tensor.transpose(bank[:, k * P:(k + 1) * P], pbuf[:, u % 3, k * P:(k + 1) * P], ident)
                    A.done((tag, "pt", u), ins)

                def weigh(u):
                    nk = scores(u)[2] // P
                    h, qt = u // 2, u % 2
                    r0 = HD * (h % 2)
                    bank = C.take(pe, (tag, "o", h // 2)) if u % 4 == 0 else C.banks[0]
                    A.moved(pe, (tag, "pt", u))
                    for k in range(nk):
                        ins = mm(bank[r0:r0 + HD, qt * P:(qt + 1) * P], values(u, k), ptbuf[:, u % 2, k * P:(k + 1) * P],
                                 start=k == 0, stop=k == nk - 1)
                    if u % 4 == 3:
                        C.done((tag, "o", h // 2), ins)

                def stage(i):
                    if i < 2 * HQ:
                        score(i)
                    if 2 <= i < 2 * HQ + 2:
                        turn(i - 2)
                    if 3 <= i < 2 * HQ + 3:
                        weigh(i - 3)
                return stage

            def s1(u):
                h, qt = u // 2, u % 2
                r0 = HD * (h % 2)
                return qA[r0:r0 + HD, h // 2, qt * P:(qt + 1) * P], kdup[r0:r0 + HD, h // 4, :], 512

            new.append(0)
            w_in = lambda u: unit(("in1", u)).rearrange("p (k n) -> p k n", k=KT)
            for u in range(2):
                for j in range(2):
                    proj(("q", 2 * u + j), w_in(u), j, hT, T)
                owe()
            w = w_in(2)
            pe.wait_ge(norm_out, norms[1]["out"])
            proj("k", w, 0, hT, 512)
            bank = A.take(pe, "v")
            for tt in range(4):
                for k in range(KT):
                    ins = mm(bank[:, tt * P:(tt + 1) * P], hT[:, k, tt * P:(tt + 1) * P], w[:, k, P:2 * P],
                             start=k == 0, stop=k == KT - 1)
            A.done("v", ins)
            owe()
            stage = attention("a1", 0, s1, lambda u, k: vA[:, k, HD * (u // 8):HD * (u // 8) + HD], prob, probT)
            for i in range(2 * HQ):
                w = w_in(3 + i // 2)
                if i < 12:
                    proj(("d", i), w, i % 2, hT, T if i < 4 else 512)
                else:
                    proj(("z", i - 12), w, i % 2, hT, T)
                if i % 2:
                    owe()
                if i == 0:
                    pe.wait_ge(con1_landed, 16)
                    pe.wait_ge(ansq, 1)
                    for j in range(3):
                        bank = B.take(pe, ("an", j))
                        ins = mm(bank[:, :], c_one("ones64"), sq[:, j * 512:(j + 1) * 512], start=True, stop=True)
                        B.done(("an", j), ins)
                elif i == 1:
                    for j in range(3):
                        pe.wait_ge(qk_normed, j + 1)
                        bank = B.take(pe, ("rot", j))
                        if j < 2:
                            src = qA[:, 2 * j:2 * j + 2, :].rearrange("p a b -> p (a b)")
                            ins = mm(bank[:, :], c_one("rot64"), src, start=True, stop=True)
                        else:
                            ins = mm(bank[:, 0:T], c_one("rot64"), kA[:, 0:T], start=True, stop=True)
                        B.done(("rot", j), ins)
                elif i == 2:
                    pe.wait_ge(rope_done, 3)
                    for kv in range(2):
                        bank = B.take(pe, ("dup", kv))
                        ins = mm(bank[:, :], c_one("sel", P, kv), kA[:, :], start=True, stop=True)
                        B.done(("dup", kv), ins)
                    A.moved(pe, "v")
                    B.moved(pe, ("dup", 0))
                    B.moved(pe, ("dup", 1))
                else:
                    stage(i - 3)
            for i in range(2 * HQ - 3, 2 * HQ + 3):
                stage(i)
            pe.wait_ge(wab_landed, 16)
            bank = A.take(pe, "ab", readers=2)
            for tt in range(4):
                for k in range(KT):
                    ins = mm(bank[:, tt * 16:(tt + 1) * 16], hT[:, k, tt * P:(tt + 1) * P], wab[:, k, :],
                             start=k == 0, stop=k == KT - 1)
                    if tt == 0 and k == 0:
                        pay(ins)
            A.done("ab", ins)
            for h in range(4):
                pe.wait_ge(d_ready, 1 + h)
                bank = A.take(pe, ("vtm", h))
                for tt in range(4):
                    ins = nc.tensor.transpose(bank[:, tt * P:(tt + 1) * P], ybuf[:, h, tt * P:(tt + 1) * P], ident)
                A.done(("vtm", h), ins)
            for i in range(8):
                wd = T if i < 4 else 512
                pe.wait_ge(sqd_ready, i + 1)
                bank = A.take(pe, ("l2", i))
                ins = mm(bank[:, 0:wd], ones, sq[:, (i % 4) * 512:(i % 4) * 512 + wd], start=True, stop=True)
                A.done(("l2", i), ins)
            for h in range(4):
                pe.wait_ge(l2_ready, 5 + h)
                bank = A.take(pe, ("ktm", h))
                for tt in range(4):
                    ins = nc.tensor.transpose(bank[:, tt * P:(tt + 1) * P], kF[:, h, tt * P:(tt + 1) * P], ident)
                A.done(("ktm", h), ins)
            norm_sum(2)

            pe.wait_ge(g_ready, 1)
            bank = A.take(pe, "gc")
            for d, um in enumerate(("u_fwd", "u_bwd")):
                mm(bank[:, d * 16:(d + 1) * 16], c_one(um), gates[:, G_G, d * 16:(d + 1) * 16], start=True, stop=True)
            ins = mm(bank[:, 32:64], ones, gates[:, G_G, :], start=True, stop=True)
            A.done("gc", ins)
            for h in range(4):
                A.moved(pe, ("ktm", h))
                A.moved(pe, ("vtm", h))

            def prepare(half):
                for s, d in GROUPS[half]:
                    g, tt = 2 * s + d, TILE[d][s]
                    lat = tt < 2
                    bank = A.take(pe, ("gb", g), readers=2 if lat else 1)
                    for h in range(4):
                        ins = mm(bank[:, h * P:(h + 1) * P], gcol(G_G, d, tt, h).to_broadcast([P, P]),
                                 c_one(("u_fwd", "u_bwd")[d]), start=True, stop=True)
                    A.done(("gb", g), ins)
                    bank = A.take(pe, ("kk", g))
                    for h in range(4):
                        k = kF[:, h, tt * P:(tt + 1) * P]
                        ins = mm(bank[:, h * P:(h + 1) * P], k, k, start=True, stop=True)
                    A.done(("kk", g), ins)
                    if lat:
                        bank = B.take(pe, ("kq", g))
                        for h in range(4):
                            ins = mm(bank[:, h * P:(h + 1) * P], kF[:, h, tt * P:(tt + 1) * P],
                                     qF[:, h, tt * P:(tt + 1) * P], start=True, stop=True)
                        B.done(("kq", g), ins)
                for s, d in GROUPS[half]:
                    g = 2 * s + d
                    A.moved(pe, ("kk", g))
                    bank = A.take(pe, ("lt", g))
                    for h in range(4):
                        ins = nc.tensor.transpose(bank[:, h * P:(h + 1) * P], dec[:, g % 4, h * P:(h + 1) * P], ident)
                    A.done(("lt", g), ins)

            def level(half, lv):
                for s, d in GROUPS[half]:
                    g = 2 * s + d
                    if lv == 1:
                        pe.wait_ge(seed_ready, g + 1)
                    else:
                        A.moved(pe, ("dt", g, lv - 1))
                    bank = A.take(pe, ("m1", g, lv))
                    for h in range(4):
                        c = slice(h * P, (h + 1) * P)
                        ins = mm(bank[:, c], LTm[:, g % 4, c], Tm[:, g % 4, c], start=True, stop=True)
                    A.done(("m1", g, lv), ins)
                for s, d in GROUPS[half]:
                    g = 2 * s + d
                    A.moved(pe, ("m1", g, lv))
                    if lv > 1:
                        A.moved(pe, ("dtt", g, lv - 1))
                    if lv < 6:
                        bank = A.take(pe, ("dt", g, lv))
                        for h in range(4):
                            c = slice(h * P, (h + 1) * P)
                            ins = mm(bank[:, c], TTm[:, g, c], dec[:, g % 4, c], start=True, stop=True)
                        A.done(("dt", g, lv), ins)
                    bank = A.take(pe, ("dtt", g, lv))
                    for h in range(4):
                        c = slice(h * P, (h + 1) * P)
                        ins = mm(bank[:, c], dec[:, g % 4, c], TTm[:, g, c], start=True, stop=True)
                    A.done(("dtt", g, lv), ins)

            def advance(s):
                for d in range(2):
                    g = 2 * s + d
                    pe.wait_ge(ttb_ready, g + 1)
                    pe.wait_ge(kb_ready, g + 1)
                    if s:
                        bank = A.take(pe, ("nw", g))
                        for h in range(4):
                            c = slice(h * P, (h + 1) * P)
                            ins = mm(bank[:, c], kbe[:, d, c], TTm[:, g, c], start=True, stop=True)
                        A.done(("nw", g), ins)
                for d in range(2):
                    g, tt = 2 * s + d, TILE[d][s]
                    if s:
                        A.moved(pe, ("nw", g))
                        A.moved(pe, ("st", g - 2))
                    bank = B.take(pe, ("vn", g))
                    for h in range(4):
                        c = slice(h * P, (h + 1) * P)
                        ins = mm(bank[:, c], TTm[:, g, c], v_tm[:, tt, h, :], start=True, stop=s == 0)
                        if s:
                            ins = mm(bank[:, c], nwT[:, d, c], S[:, d, c], start=False, stop=True)
                    B.done(("vn", g), ins)
                for d in range(2):
                    g, tt = 2 * s + d, TILE[d][s]
                    B.moved(pe, ("vn", g))
                    if tt < 2:
                        pe.wait_ge(qdec_ready, g - 3)
                        B.moved(pe, ("kq", g))
                        bank = B.take(pe, ("og", g))
                        for h in range(4):
                            c = slice(h * P, (h + 1) * P)
                            mm(bank[:, c], S[:, d, c], qdec[:, g % 4, c], start=True, stop=False)
                            ins = mm(bank[:, c], vnew[:, d, c], ATm[:, g % 4, c], start=False, stop=True)
                        B.done(("og", g), ins)
                    if s < 3:
                        bank = A.take(pe, ("st", g))
                        for h in range(4):
                            c = slice(h * P, (h + 1) * P)
                            ins = mm(bank[:, c], kdec[:, d, c], vnew[:, d, c], start=True, stop=True)
                        A.done(("st", g), ins)

            for what, *args in DELTA:
                dict(prepare=prepare, level=level, advance=advance,
                     fill=lambda n: n and fill_sum(C, 0, 7 + n))[what](*args)

            def head_norm_sum(j):
                pe.wait_ge(hn_sq, j + 1)
                for i in range(2):
                    bank = A.take(pe, ("hn", j, i))
                    ins = mm(bank[:, :], ones, sq[:, i * 512:(i + 1) * 512], start=True, stop=True)
                    A.done(("hn", j, i), ins)
            head_norm_sum(0)

            def project_out(tag, names, mix, ready):
                for s_, n_ in ready:
                    pe.wait_ge(s_, n_)
                for u in range(4):
                    w = unit(names + (u,)).rearrange("p (k n) -> p k n", k=KT)
                    for j in range(2):
                        proj((tag, 2 * u + j), w, j, mix, T)
                    owe()

            project_out("xo1", ("out1",), mixT, [(hn_out, 4), (norm_out, norms[2]["out"])])

            def ffn(tag, h, part):
                accs = []

                def up(f):
                    c, j = f // 2, f % 2
                    bank = A.take(pe, (tag, "gu", f))
                    for i, m in enumerate("gu"):
                        w = unit((tag, m, c)).rearrange("p (k n) -> p k n", k=KT)
                        for k in range(KT):
                            new_tile(k)
                            ins = mm(bank[:, i * T:(i + 1) * T], w[:, k, j * P:(j + 1) * P], h[:, k, :],
                                     start=k == 0, stop=k == KT - 1)
                            if k == 0:
                                pay(ins)
                        if j == 1 and i == 0:
                            ins.then_inc(unit_used, 1)
                    if j == 1:
                        owe()
                    A.done((tag, "gu", f), ins)

                def down(f):
                    if f == 0:
                        accs.extend(B.take(pe, (tag, "acc", i)) for i in range(3))
                        accs.append(C.take(pe, (tag, "acc", 3)))
                    w = unit((tag, "d", f // 2)).rearrange("p (r n) -> p r n", r=2)
                    if tag == "ffn1":
                        pe.wait_ge(gT_ready, f + 1)
                    else:
                        A.moved(pe, (tag, "gu", f))
                    for dt in range(KT):
                        ins = mm(accs[dt // 2][:, (dt % 2) * T:(dt % 2 + 1) * T], w[:, f % 2, dt * P:(dt + 1) * P],
                                 gT[:, f % 4, :], start=f == 0 and dt % 2 == 0, stop=f == FT - 1,
                                 skip_group_check=True)
                        if dt == 0:
                            pay(ins)
                        if f == FT - 1 and dt % 2 == 1:
                            rg = B if dt < 6 else C
                            rg.done((tag, "acc", dt // 2), ins)
                    if f == FT - 1:
                        owe()
                    elif f % 2:
                        ins.then_inc(unit_used, 1)

                for f in range(FT + 3):
                    if f < FT:
                        up(f)
                    if f:
                        fill_sum(A, part, f - 1)
                    if f % 2 and 3 <= f < FT + 2:
                        down(f - 3)
                        down(f - 2)

            norm_sum(3)
            new.append(3)
            ffn("ffn1", hF, 1)
            norm_sum(4)

            for l in range(2):
                n0 = 5 + 3 * l
                norm_sum(n0)
                new.append(n0)
                w_in = lambda u: unit(("in2", l, u)).rearrange("p (k n) -> p k n", k=KT)

                def features(kind, u0, i):
                    proj((l, kind, i), w_in(u0 + i // 2), i % 2, h2, T)
                    if i % 2:
                        owe()

                def tokens(kind, u0, half):
                    w = w_in(u0 + half)
                    bank = A.take(pe, (l, kind, half))
                    for tt in range(TT):
                        for k in range(KT):
                            ins = mm(bank[:, tt * UW:(tt + 1) * UW], h2[:, k, tt * P:(tt + 1) * P], w[:, k, :],
                                     start=k == 0, stop=k == KT - 1)
                            if tt == 0 and k == 0:
                                pay(ins)
                    owe()
                    A.done((l, kind, half), ins)

                def turn_rotary(j):
                    for i in range(2):
                        A.moved(pe, (l, "qr" if j < 2 else "kr", 2 * (j % 2) + i))
                    bank = A.take(pe, (l, "rr", j))
                    src = (qR if j < 2 else kR)[:, 2 * (j % 2):2 * (j % 2) + 2, :].rearrange("p a b -> p (a b)")
                    ins = mm(bank[:, :], c_two("rot128"), src, start=True, stop=True)
                    A.done((l, "rr", j), ins)

                def s2(u):
                    h, qt = u // 2, u % 2
                    r0 = HD * (h % 2)
                    return qA2[r0:r0 + HD, h // 2, qt * P:(qt + 1) * P], kA2[r0:r0 + HD, h // 2, 0:(qt + 1) * P], (qt + 1) * P
                stage = attention(("a2", l), 16 * (l + 1), s2,
                                  lambda u, k: vA2[:, k, HD * (u // 2):HD * (u // 2) + HD], prob2, probT2)
                for i in range(4):
                    features("qa", 0, i)
                for i in range(4):
                    features("ka", 2, i)
                for i in range(2):
                    tokens("va", 4, i)
                pe.wait_ge(con2_landed, 16)
                for i, (kind, u0, j) in enumerate(SLOTS2):
                    dict(qr=features, kr=features, gr=features, vr=tokens,
                         rr=lambda kind, u0, j: turn_rotary(j))[kind](kind, u0, j)
                    if i == 0:
                        for n in [(l, "qa", i) for i in range(4)] + [(l, "ka", i) for i in range(4)] + [(l, "va", 0), (l, "va", 1)]:
                            A.moved(pe, n)
                    stage(i)
                stage(2 * HQ + 2)
                norm_sum(n0 + 1)
                pe.wait_ge(rrope, 4 * (l + 1))
                A.moved(pe, (l, "vr", 0))
                A.moved(pe, (l, "vr", 1))

                def ret_scores(h):
                    bank = B.take(pe, (l, "rs", h))
                    mm(bank[:, 0:256], kR[:, h, 0:P], qR[:, h, :], start=True, stop=True)
                    ins = mm(bank[:, 256:384], kR[:, h, P:T], qR[:, h, P:T], start=True, stop=True)
                    B.done((l, "rs", h), ins)
                ret_scores(0)
                for h in range(4):
                    if h < 3:
                        ret_scores(h + 1)
                    B.moved(pe, (l, "rs", h))
                    bank = A.take(pe, (l, "ro", h))
                    a = AR[:, h % 2, :]
                    mm(bank[:, 0:P], vR[:, 0, h * P:(h + 1) * P], a[:, 0:P], start=True, stop=True)
                    mm(bank[:, P:T], vR[:, 0, h * P:(h + 1) * P], a[:, P:T], start=True, stop=False)
                    ins = mm(bank[:, P:T], vR[:, 1, h * P:(h + 1) * P], a[:, 256:384], start=False, stop=True)
                    A.done((l, "ro", h), ins)
                head_norm_sum(1 + l)
                project_out(("xo2", l), ("out2", l), mix2, [(hn_out, 4 * (l + 2)), (norm_out, norms[n0 + 1]["out"])])
                norm_sum(n0 + 2)
                if l == 1:
                    pe.wait_ge(norm_out, norms[n0 + 2]["out"])
                else:
                    new.append(n0 + 2)
                    ffn("ffn2", hF, 2)

            pe.wait_ge(wrt_landed, 16)
            bank = A.take(pe, "logits")
            for tt in range(TT):
                for k in range(KT):
                    ins = mm(bank[:, tt * NE:(tt + 1) * NE], hF[:, k, tt * P:(tt + 1) * P], wrt[:, k, :],
                             start=k == 0, stop=k == KT - 1)
            A.done("logits", ins)
            for tt in range(TT):
                for kg in range(2):
                    bank = A.take(pe, ("htm", tt, kg))
                    for k in range(4):
                        ins = nc.tensor.transpose(bank[:, k * P:(k + 1) * P],
                                                  hF[:, 4 * kg + k, tt * P:(tt + 1) * P], ident)
                    A.done(("htm", tt, kg), ins)
            pe.wait_ge(sel_ready, 1)
            bank = A.take(pe, "pos")
            sel = [rout[:, 4 + tt, :] for tt in range(2)]
            mm(bank[:, 0:8], c_all("ustrict"), sel[0], start=True, stop=True)
            mm(bank[:, 8:16], ones, sel[0], start=True, stop=False)
            mm(bank[:, 8:16], c_all("ustrict"), sel[1], start=False, stop=True)
            mm(bank[:, 16:24], ones, sel[0], start=True, stop=False)
            ins = mm(bank[:, 16:24], ones, sel[1], start=False, stop=True)
            A.done("pos", ins)
            for e in range(NE):
                pe.wait_ge(pw_ready, e + 1)
                bank = A.take(pe, ("pwT", e))
                for s in range(2):
                    for tt in range(TT):
                        ins = nc.tensor.transpose(bank[:, s * T + tt * P:s * T + (tt + 1) * P],
                                                  Pw[:, e % 2, tt * 256 + s * P:tt * 256 + (s + 1) * P], ident)
                A.done(("pwT", e), ins)
            for rg in (A, B, C):
                rg.all_free(pe)

            def product(bank, left, right, start, stop):
                (lh, ll), (rh, rl) = left, right
                first = mm(bank, lh, rh, start=start, stop=False, skip_group_check=True)
                mm(bank, lh, rl, start=False, stop=False, skip_group_check=True)
                return first, mm(bank, ll, rh, start=False, stop=stop, skip_group_check=True)

            def expert(e, ns):
                st = ns // P
                wide = st == 2

                def eunit(name):
                    n = e_order[name]
                    return wH[n % 3], wL[n % 3]

                def parts_ready(name, i):
                    pe.wait_ge(split_ready, e * (2 * EU) + (2 * e_order[name] + i + 1 + HALVES))

                pe.wait_ge(gated, e * FC + 2)
                for j in range(KT):
                    if j >= 3:
                        pe.wait_ge(moved, e * 16 + j)
                    bank = gather_bank(j)
                    for tt in range(TT):
                        ins = mm(bank[:, 0:ns], h_tm[:, tt, j * P:(j + 1) * P], Pg[:, tt, e, 0:ns],
                                 start=tt == 0, stop=tt == TT - 1)
                    ins.then_inc(xj_full, 1)

                def up(m, c):
                    if m == "g":
                        pe.wait_ge(gated, e * FC + (c + 1 + wide))
                    w = [x.rearrange("p (k n) -> p k n", k=KT) for x in eunit((m, c))]
                    if wide:
                        bank = banks["gu".index(m)]
                        for j in range(2):
                            for k in range(KT):
                                if j == 0 and k % (KT // 2) == 0:
                                    parts_ready((m, c), k // (KT // 2))
                                if m == "g" and c == 0 and j == 0:
                                    pe.wait_ge(moved, e * 16 + (k + 3))
                                first, ins = product(bank[:, j * T:(j + 1) * T], [x[:, k, j * P:(j + 1) * P] for x in w],
                                                     (xgH[:, k, :], xgL[:, k, :]), k == 0, k == KT - 1)
                                if k == 0:
                                    pay(first, pair_used)
                            if m == "u" and j == 0 and c >= 1:
                                ins.then_inc(turned_h, 1)
                    else:
                        bank = banks[c % 2]
                        o = T * "gu".index(m)
                        for k in range(KT):
                            if k % (KT // 2) == 0:
                                parts_ready((m, c), k // (KT // 2))
                            if m == "g" and c == 0:
                                pe.wait_ge(moved, e * 16 + (k + 3))
                            first, ins = product(bank[:, o:o + T], (xgH[:, k, 0:P], xgL[:, k, 0:P]),
                                                 [x[:, k, :] for x in w], k == 0, k == KT - 1)
                            if k == 0:
                                pay(first, pair_used)
                    if m == "g":
                        ins.then_inc(pair_used, 1)
                    else:
                        owe()
                        ins.then_inc(gu_full, 1)

                def turn(c):
                    if wide:
                        return
                    pe.wait_ge(gated, e * FC + (c + 3))
                    if c >= 2:
                        pe.wait_ge(gl_ready, e * FC + (c - 1))
                    for f in range(2):
                        ins = nc.tensor.transpose(banks[2 + c % 2][:, f * P:(f + 1) * P],
                                                  hid[:, c % 2, f * P:(f + 1) * P], ident)
                        if f == 0:
                            pay(ins, pair_used)
                    ins.then_inc(turned_h, 1)

                def down(c):
                    pe.wait_ge(gl_ready, e * FC + (c + 1))
                    w = [x.rearrange("p (r n) -> p r n", r=2) for x in eunit(("d", c))]
                    for f in range(2):
                        parts_ready(("d", c), f)
                        for s in range(st):
                            a = f * ns + s * P
                            for half in range(2):
                                first, ins = product(banks[4 + 2 * s + half][:, :], (gH[:, c % 2, a:a + P], gL[:, c % 2, a:a + P]),
                                                     [x[:, f, half * 512:(half + 1) * 512] for x in w],
                                                     c == 0 and f == 0, c == FC - 1 and f == 1)
                                if f == 0 and s == 0 and half == 0:
                                    pay(first, pair_used)
                                    if wide and c == FC - 2:
                                        ins.then_inc(turned_h, 1)
                    ins.then_inc(pair_used, 1)

                for what, c in e_steps:
                    if what in ("g", "u"):
                        up(what, c)
                    else:
                        dict(turn=turn, d=down)[what](c)
                for j in range(KT):
                    if j % 4 == 0:
                        pe.wait_ge(ye_ready[j // 4], e + 1)
                    pe.wait_ge(moved, e * 16 + (8 + j + 1))
                    bank = banks[2 + j % 2]
                    for s in range(st):
                        ins = mm(bank[:, 0:T], ye[:, s, j * P:(j + 1) * P], PwT[:, s, e, :],
                                 start=s == 0, stop=s == st - 1)
                    ins.then_inc(xj_full, 1)

            with pe.Fori(0, NE) as e:
                count = pe.value_load(cnt_i[0:1, bass.ts(e, 1)], min_val=0, max_val=T)
                with pe.If(count > NARROW):
                    expert(e, T)
                with pe.Else():
                    expert(e, NARROW)
                pe.nop()

            for k in range(KT):
                pe.wait_ge(sq_ready, norms[11]["first"] + k + 1)
                ins = mm(banks[0][:, 0:T], ones, sq[:, k * T:(k + 1) * T], start=k == 0, stop=k == KT - 1)
            ins.then_inc(fin_ready, 1)
            pe.wait_ge(norm_out, norms[11]["out"])
            for tt in range(TT):
                for kg in range(2):
                    for k in range(4):
                        ins = nc.tensor.transpose(banks[4 + 2 * tt + kg][:, k * P:(k + 1) * P],
                                                  xT[:, 4 * kg + k, tt * P:(tt + 1) * P], ident)
                    ins.then_inc(fin_ready, 1)

        @block.scalar
        def _(act):
            steps = [0]

            def step(ins):
                steps[0] += 1
                ins.then_inc(act_step, 1)
                act.wait_ge(act_step, steps[0])
            F = nc.scalar.activation

            rows = vrows

            def vrow(table, row, ap):
                n = ap.shape[0]
                act.dma_start(rows[row:row + n, table * P:(table + 1) * P], ap).then_inc(v_landed if table else v0_landed, 16)

            def tiles(ap):
                return ap.rearrange("(a p) -> a p", p=P)
            vrow(0, V_C, tiles(t["c"][0]))
            vrow(0, V_CCTX, tiles(t["c_ctx"]))
            vrow(0, V_BMOD, tiles(t["b_mod"][0]))
            vrow(0, V_N1, tiles(t["norm1_g"][0]))
            vrow(0, V_ATTG, tiles(t["attn_out_g"][0]))
            vrow(0, V_GDNG, t["gdn_norm_g"])
            vrow(0, V_N2, tiles(t["norm2_g"][0]))
            vrow(0, V_CONV, t["conv_qkv_w"][0].rearrange("k (a p) -> (k a) p", p=P))
            for row, name in ((V_QG, "q_norm_g"), (V_KG, "k_norm_g")):
                for half in range(2):
                    act.dma_start(rows[row:row + 1, half * HD:(half + 1) * HD], t[name]).then_inc(v0_landed, 16)
            for s in range(2):
                dst = (xT, ctxT)[s]
                for tt in range(TT):
                    for kg in range(2):
                        n = ("xt", s, tt, kg)
                        bank = A.full(act, n)
                        ins = F(dst[:, 4 * kg:4 * kg + 4, tt * P:(tt + 1) * P],
                                bank[:, :].rearrange("p (a b) -> p a b", a=4), ACT.Copy)
                        A.free(n, ins)

            def norm(n):
                N = norms[n]
                for k in range(N["nt"]):
                    N["wait"](act, k)
                    F(sq[:, k * T:(k + 1) * T], N["src"][:, k, :], ACT.Square).then_inc(sq_ready, 1)
                if n == 11:
                    act.wait_ge(fin_ready, 1)
                    bank = banks[0]
                else:
                    bank = A.full(act, ("ss", n))
                if n > 1:
                    act.wait_ge(norm_out, norms[n - 1]["out"])
                ins = F(root(n), bank[:, 0:T], ACT.Sqrt, bias=EPS, scale=1.0 / (N["nt"] * P))
                if n == 11:
                    ins.then_inc(root_ready, 1)
                else:
                    A.free(("ss", n), ins)
                if n > 1:
                    shift(n)

            shifted = [0]

            def shift(n):
                N = norms[n]
                if N["shift"] is not None:
                    for k in range(N["nt"]):
                        shifted[0] += 1
                        act.wait_ge(scaled, shifted[0])
                        y = N["dst"][:, k, :]
                        F(y, y, ACT.Identity, bias=N["shift"][:, k:k + 1]).then_inc(norm_out, 1)
            A.moved(act, "vec0")
            F(cs[:, :, 0], v(0, V_C, 8), ACT.Silu)
            F(cs[:, :, 1], v(0, V_CCTX, 8), ACT.Silu).then_inc(cs_ready, 1)
            norm(0)
            norm(1)

            cw = t["ffn_conv_w"][0].rearrange("k (a p) -> k a p", p=P)
            vrow(1, V_FW01, cw[0])
            vrow(1, V_FW01 + 44, cw[1])
            vrow(1, V_C2, tiles(t["c_2"][0]))
            vrow(1, V_NMIX, t["norm_mix_g_2"].rearrange("l (a p) -> (l a) p", p=P))
            vrow(1, V_NFFN, t["norm_ffn_g_2"].rearrange("l (a p) -> (l a) p", p=P))
            vrow(2, V_FW2, cw[2])
            vrow(2, V_FB, tiles(t["ffn_conv_b"][0]))
            vrow(2, V_FIN1, tiles(t["final_norm_g"]))
            vrow(2, V_FIN2, tiles(t["final_norm_g_2"]))
            vrow(3, V_BADA, t["ada_b_2"][0:1].rearrange("l (a p) -> (l a) p", p=P))
            vrow(3, V_BADA + 48, t["ada_b_2"][1:2].rearrange("l (a p) -> (l a) p", p=P))
            vrow(3, V_ATTG2, t["att_out_g_2"][0:1].rearrange("l (a p) -> (l a) p", p=P))
            vrow(3, V_ATTG2 + 4, t["att_out_g_2"][1:2].rearrange("l (a p) -> (l a) p", p=P))
            vrow(3, V_RETG, t["ret_out_g_2"].rearrange("l (a p) -> (l a) p", p=P))
            act.dma_start(con2[:, :], t["constants"][:, C_ALL_W:C_ALL_W + C_ONE_W]).then_inc(con1_landed, 16)
            for i, (f, b) in enumerate((("a_log_f", "a_log_b"), ("dt_bias_f", "dt_bias_b"))):
                for j, name in enumerate((f, b)):
                    act.dma_start(gconst[:, i, 4 * j:4 * j + 4], t[name].to_broadcast([P, 4])).then_inc(gc_landed, 16)
            with nc.allow_non_contiguous_dma(reason="small"):
                act.dma_start(wab[:, :, :], t["w_in"][0][:, 11 * UW:].rearrange("(k p) n -> p k n", p=P)).then_inc(wab_landed, 16)
                act.dma_start(wrt[:, :, :], t["router_w_2"][0].rearrange("(k p) n -> p k n", p=P)).then_inc(wrt_landed, 16)

            for u in range(8):
                n = ("ada", 0, u)
                A.free(n, F(sq[0:2, u * UW:(u + 1) * UW], A.full(act, n)[0:2, 0:UW], ACT.Copy))
            A.moved(act, "vec")
            F(cs2[:, :], v(1, V_C2, 8), ACT.Silu).then_inc(cs_ready, 1)
            shift(0)
            shift(1)

            for i in range(4):
                ins = F(qA[:, i, :], A.full(act, ("q", i))[:, 0:T], ACT.Copy)
                A.free(("q", i), ins)
            ins = F(kA[:, :], A.full(act, "k")[:, :], ACT.Copy)
            A.free("k", ins)
            ins = F(vA[:, :, :].rearrange("p a b -> p (a b)"), A.full(act, "v")[:, :], ACT.Copy)
            A.free("v", ins)

            def attention(tag, base, keys, scaled, pbuf, ptbuf, o):
                def expo(u):
                    n = keys(u)
                    act.wait_ge(max_ready, base + u + 1)
                    st = stat[:, u % 4, :]
                    if scaled:
                        F(pbuf[:, u % 3, 0:n], pbuf[:, u % 3, 0:n], ACT.Exp, bias=st[:, 1:2],
                          accum_out=st[:, 2:3]).then_inc(exp_done, 1)
                    else:
                        bank = B.full(act, (tag, "s", u))
                        if u >= 3:
                            A.full(act, (tag, "pt", u - 3))
                        ins = F(pbuf[:, u % 3, 0:n], bank[:, 0:n], ACT.Exp, bias=st[:, 1:2], scale=HD ** -0.5,
                                accum_out=st[:, 2:3])
                        B.free((tag, "s", u), ins)

                def turned(u):
                    n = keys(u)
                    name = (tag, "pt", u)
                    A.free(name, F(ptbuf[:, u % 2, 0:n], A.full(act, name)[:, 0:n], ACT.Copy))

                def output(j):
                    name = (tag, "o", j)
                    C.free(name, F(o[:, j, :], C.full(act, name)[:, 0:T], ACT.Copy))

                def stage(i):
                    if i >= 7 and i % 4 == 3:
                        output((i - 7) // 4)
                    if i < 2 * HQ:
                        expo(i)
                    if 2 <= i < 2 * HQ + 2:
                        turned(i - 2)
                return stage

            for n in [("q", i) for i in range(4)] + ["k"]:
                A.moved(act, n)
            F(sq[:, 0:1024], qA[:, :, :].rearrange("p a b -> p (a b)"), ACT.Square)
            F(sq[:, 1024:1536], kA[:, :], ACT.Square).then_inc(ansq, 1)

            def conv_place(i):
                return qF[:, i, :] if i < 4 else kF[:, i - 4, :] if i < 8 else ybuf[:, i - 8, :]
            stage = attention("a1", 0, lambda u: 512, False, prob, probT, oA)
            for i in range(2 * HQ):
                if i < 12:
                    wd = T if i < 4 else 512
                    F(conv_place(i), A.full(act, ("d", i))[:, 0:wd], ACT.Copy, scale=v(0, V_CONV + 12 + i)).then_inc(centre_ready, 1)
                else:
                    n = ("z", i - 12)
                    A.free(n, F(zs[:, i - 12, :], A.full(act, n)[:, 0:T], ACT.Copy))
                if i == 0:
                    for j in range(3):
                        n = ("an", j)
                        B.free(n, F(hroot[:, j, :] if j < 2 else kroot, B.full(act, n)[:, :], ACT.Sqrt, bias=EPS,
                                    scale=1.0 / HD))
                elif i == 2:
                    for kv in range(2):
                        n = ("dup", kv)
                        B.free(n, F(kdup[:, kv, :], B.full(act, n)[:, :], ACT.Copy))
                elif i > 2:
                    stage(i - 3)
            for i in range(2 * HQ - 3, 2 * HQ + 4):
                stage(i)
            act.wait_ge(sp_abs, 1)
            step(F(gates[:, G_T1, :], gates[:, G_T1, :], ACT.Exp, scale=-1.0))
            act.wait_ge(gc_landed, 64)
            F(gates[:, G_EA, 0:8], gconst[:, 0, :], ACT.Exp)
            F(gates[:, G_T1, :], gates[:, G_T1, :], ACT.Ln, bias=1.0).then_inc(sp_ln, 1)
            ins = F(gates[:, G_BETA, :].rearrange("p (d t h) -> p t d h", d=2, t=4),
                    A.full(act, "ab")[:, 0:64].rearrange("p (t x d h) -> p t x d h", t=4, x=2, d=2)[:, :, 1, :, :], ACT.Sigmoid)
            A.free("ab", ins)
            for n in range(8, 20):
                i = n % 12
                A.moved(act, ("d", i))
                y = conv_place(i)
                F(y, y, ACT.Silu).then_inc(d_ready, 1)
            for i in range(4):
                A.moved(act, ("z", i))
                step(F(zs[:, i, :], zs[:, i, :], ACT.Silu))
            for h in range(4):
                n = ("vtm", h)
                A.free(n, F(v_tm[:, :, h, :], A.full(act, n)[:, :].rearrange("p (a b) -> p a b", a=4), ACT.Copy))
            def l2_root(i):
                wd = T if i < 4 else 512
                bank = A.full(act, ("l2", i))
                if i >= 2:
                    act.wait_ge(l2_ready, i - 1)
                c = float(P) if i < 4 else 1.0
                ins = F(hroot[:, i % 2, 0:wd], bank[:, 0:wd], ACT.Sqrt, bias=EPS * c, scale=c)
                A.free(("l2", i), ins)
            act.wait_ge(d_ready, 12)
            for i in range(9):
                if i < 8:
                    wd = T if i < 4 else 512
                    if i >= 4:
                        A.full(act, ("l2", i - 4))
                    F(sq[:, (i % 4) * 512:(i % 4) * 512 + wd], qF[:, i, :] if i < 4 else kF[:, i - 4, :],
                      ACT.Square).then_inc(sqd_ready, 1)
                if i:
                    l2_root(i - 1)
            for h in range(4):
                n = ("ktm", h)
                ins = F(k_tm[:, :, h, :], A.full(act, n)[:, :].rearrange("p (a b) -> p a b", a=4), ACT.Copy)
                A.free(n, ins)
            norm(2)

            act.wait_ge(tmg_ready, 1)
            F(gates[:, G_EG, :], gates[:, G_CUM, :], ACT.Exp)
            F(gates[:, G_KD, :], gates[:, G_T0, :], ACT.Exp)
            F(gates[:, G_DL, :], gates[:, G_TOT, :], ACT.Exp).then_inc(gate_ready, 1)

            def head_norm(j, src, wait):
                wait()
                F(sq[:, 0:1024], src.rearrange("p a b -> p (a b)"), ACT.Square).then_inc(hn_sq, 1)
                if j == 0:
                    act.wait_ge(l2_ready, 8)
                else:
                    act.wait_ge(hn_out, 4 * j)
                for i in range(2):
                    n = ("hn", j, i)
                    ins = F(hroot[:, i, :], A.full(act, n)[:, :], ACT.Sqrt, bias=EPS, scale=1.0 / P)
                    A.free(n, ins)

            def prepare(half):
                for s, d in GROUPS[half]:
                    g, tt = 2 * s + d, TILE[d][s]
                    if tt < 2:
                        A.moved(act, ("gb", g), 1)
                        A.free(("gb", g), F(egb[:, g % 4, :], A.full(act, ("gb", g))[:, :], ACT.Exp))
                    A.moved(act, ("gb", g))
                    for h in range(4):
                        c = slice(h * P, (h + 1) * P)
                        ins = F(dec[:, g % 4, c], dec[:, g % 4, c], ACT.Exp, bias=gcol(G_CUM, d, tt, h))
                    ins.then_inc(dec_ready, 1)
                    if tt < 2:
                        for h in range(4):
                            c = slice(h * P, (h + 1) * P)
                            ins = F(ATm[:, g % 4, c], ATm[:, g % 4, c], ACT.Exp, bias=gcol(G_NCUM, d, tt, h))
                        ins.then_inc(att_ready, 1)
                for s, d in GROUPS[half]:
                    n = ("lt", 2 * s + d)
                    A.free(n, F(LTm[:, n[1] % 4, :], A.full(act, n)[:, :], ACT.Copy))

            def advance(s):
                if s:
                    for d in range(2):
                        n = ("nw", 2 * s + d)
                        A.free(n, F(nwT[:, d, :], A.full(act, n)[:, :], ACT.Copy))
                for d in range(2):
                    n = ("vn", 2 * s + d)
                    B.free(n, F(vnew[:, d, :], B.full(act, n)[:, :], ACT.Copy))
            for what, *args in DELTA:
                if what == "prepare":
                    prepare(*args)
                elif what == "advance":
                    advance(*args)

            def last_og():
                B.moved(act, ("og", 7))
                B.moved(act, ("og", 6))
            head_norm(0, oG, last_og)
            norm(3)
            act.dma_start(con2[:, 0:C_TWO_W], t["constants"][:, C_ALL_W + C_ONE_W:]).then_inc(con2_landed, 16)

            for f in range(FT + 1):
                if f < FT:
                    bank = A.full(act, ("ffn1", "gu", f))
                    if f >= 3:
                        act.wait_ge(gT_ready, f - 2)
                    F(yc[:, f % 3, 0:T], bank[:, 0:T], ACT.Identity, scale=v(1, V_FW01 + 44 + f), bias=v(2, V_FB + f))
                    F(yc[:, f % 3, T:512], bank[:, T:512], ACT.Identity, scale=v(1, V_FW01 + 44 + FT + f),
                      bias=v(2, V_FB + FT + f)).then_inc(centre_ready, 1)
                if f:
                    A.moved(act, ("ffn1", "gu", f - 1))
                    y = yc[:, (f - 1) % 3, 0:T]
                    F(y, y, ACT.Silu).then_inc(silu_ready, 1)
            norm(4)

            for l in range(2):
                n0 = 5 + 3 * l
                norm(n0)
                place = dict(qa=qA2, ka=kA2, qr=qR, kr=kR, gr=sgr, va=vA2, vr=vR)

                def copy_out(kind, i):
                    n = (l, kind, i)
                    bank = A.full(act, n)
                    if kind[0] == "v":
                        ins = F(place[kind][:, :, i * UW:(i + 1) * UW], bank[:, :].rearrange("p (a b) -> p a b", a=2), ACT.Copy)
                    else:
                        ins = F(place[kind][:, i, :], bank[:, 0:T], ACT.Copy)
                    A.free(n, ins)
                for kind, m in (("qa", 4), ("ka", 4), ("va", 2)):
                    for i in range(m):
                        copy_out(kind, i)
                stage = attention(("a2", l), 16 * (l + 1), lambda u: (u % 2 + 1) * P, True, prob2, probT2, oA2)
                for i, (kind, _, j) in enumerate(SLOTS2):
                    if kind != "rr":
                        copy_out(kind, j)
                    stage(i)
                stage(2 * HQ + 2)
                stage(2 * HQ + 3)
                for i in range(4):
                    A.moved(act, (l, "gr", i))
                F(sgr[:, :, :], sgr[:, :, :], ACT.Silu).then_inc(sg_ready, 1)
                norm(n0 + 1)
                for h in range(4):
                    n = (l, "ro", h)
                    A.free(n, F(oR[:, h, :], A.full(act, n)[:, 0:T], ACT.Copy))

                def last_ro():
                    for h in range(4):
                        A.moved(act, (l, "ro", h))
                head_norm(1 + l, oR, last_ro)
                norm(n0 + 2)
                if l == 0:
                    for f in range(FT):
                        bank = A.full(act, ("ffn2", "gu", f))
                        if f >= 3:
                            A.moved(act, ("ffn2", "gu", f - 3))
                        F(yc[:, f % 3, 0:T], bank[:, 0:T], ACT.Silu).then_inc(silu_ready, 1)

            for tt in range(TT):
                for kg in range(2):
                    n = ("htm", tt, kg)
                    A.free(n, F(h_tm[:, tt, kg * 512:(kg + 1) * 512], A.full(act, n)[:, :], ACT.Copy))
            act.wait_ge(top_ready, 1)
            for tt in range(TT):
                F(rout[:, 14 + tt, 0:1], rout[:, 12 + tt, 0:1], ACT.Sigmoid)
                ins = F(rout[:, 14 + tt, 1:2], rout[:, 12 + tt, 0:1], ACT.Sigmoid, scale=-1.0)
            ins.then_inc(wt_ready, 1)
            for e in range(NE):
                n = ("pwT", e)
                A.free(n, F(PwT[:, :, e, :], A.full(act, n)[:, :].rearrange("p (a b) -> p a b", a=2), ACT.Copy))
            A.moved(act, "pos")

            act.wait_ge(unit_used, U0)

            def split(e, n):
                act.wait_ge(pair_used, e * EU + (n + 1))
                for i in (2 * n, 2 * n + 1):
                    act.wait_ge(raw_landed[i % HALVES], e * (16 * 2 * EU // HALVES) + 16 * (i // HALVES + 1))
                    F(half_of(wH[n % 3], i), raw[i % HALVES], ACT.Copy).then_inc(wh_ready, 1)
            split(0, 0)
            split(0, 1)

            def expert(e, ns):
                wide = ns == T

                for j in range(KT):
                    act.wait_ge(xj_full, e * 16 + (j + 1))
                    F(xgH[:, j, 0:ns], gather_bank(j)[:, 0:ns], ACT.Copy).then_inc(xh_ready, 1)
                split(e, 2)
                for what, c in e_steps:
                    if what == "turn":
                        act.wait_ge(turned_h, e * FC + (c + 1))
                        if wide:
                            act.wait_ge(gated, e * FC + (c + 3))
                        F(gH[:, c % 2, 0:2 * ns], hid[:, c % 2, :] if wide else banks[2 + c % 2][:, 0:T],
                          ACT.Copy).then_inc(gh_ready, 1)
                        continue
                    if what == "u":
                        act.wait_ge(gu_full, e * FC + (c + 1))
                        act.wait_ge(gated, e * FC + (c + 1))
                        F(sge[:, c % 2, 0:2 * ns], banks[0 if wide else c % 2][:, 0:2 * ns], ACT.Silu).then_inc(sge_ready, 1)
                    n = e_order[what, c]
                    if n + 3 < EU:
                        split(e, n + 3)
                with act.If(e < NE - 1):
                    split(e, EU)
                    split(e, EU + 1)
                act.wait_ge(pair_used, e * EU + (EU + 3))
                for i in range(ns // P):
                    ins = F(ye[:, i, 0:512], banks[4 + 2 * i][:, :], ACT.Copy)
                ins.then_inc(ye_ready[0], 1)

            with act.Fori(0, NE) as e:
                count = act.value_load(cnt_i[0:1, bass.ts(e, 1)], min_val=0, max_val=T)
                with act.If(count > NARROW):
                    expert(e, T)
                with act.Else():
                    expert(e, NARROW)
                act.nop()
            norm(11)

        @block.vector
        def _(dve):
            steps = [0]
            V = nc.vector

            def step(ins):
                steps[0] += 1
                ins.then_inc(dve_step, 1)
                dve.wait_ge(dve_step, steps[0])

            V.memset(stat[:, 0, 0:1], 0.0).then_inc(split_ready, HALVES)
            def turned_vectors(n, tables):
                bank = A.full(dve, n)
                for i in tables:
                    rows = (V0_ROWS, V1_ROWS, V2_ROWS, V3_ROWS)[i]
                    ins = V.tensor_copy(vec[:, i, 0:rows], bank[:, i * P:i * P + rows])
                A.free(n, ins)
                A.moved(dve, n)
            turned_vectors("vec0", (0,))

            def norm(n):
                N = norms[n]
                nt = N["nt"]
                if n == 11:
                    dve.wait_ge(root_ready, 1)
                else:
                    A.moved(dve, ("ss", n))
                step(V.reciprocal(root(n), root(n)))
                for k in range(nt):
                    V.scalar_tensor_tensor(out=N["dst"][:, k, :], in0=N["src"][:, k, :], scalar=N["gain"][:, k:k + 1],
                                           in1=root(n), op0=ALU.mult, op1=ALU.mult).then_inc(norm_out if N["shift"] is None else scaled, 1)

            fills = [0]

            def fill(part, u):
                n = fills[0]
                fills[0] += 1
                k = order["mod", part, u]
                if n >= 2:
                    rg, name = filled[n - 2]
                    rg.full(dve, name)
                dve.wait_ge(landed[slot[k]], 16 * turn[k])
                dve.wait_ge(cs_ready, 2 if part else 1)
                w = ring[:, slot[k], :].rearrange("p (k n) -> p k n", k=KT)
                for i in range(KT):
                    acc = facc2[:, n % 2, i % 2, :]
                    c = cs[:, i, 0:1] if part == 0 else cs2[:, i:i + 1]
                    if i < 2:
                        ins = V.tensor_scalar(acc, w[:, i, :], c, None, ALU.mult)
                    else:
                        dve.wait_ge(dve_step, steps[0] - 1)
                        ins = V.scalar_tensor_tensor(out=acc, in0=w[:, i, :], scalar=c, in1=acc, op0=ALU.mult, op1=ALU.add)
                    steps[0] += 1
                    ins.then_inc(dve_step, 1)
                dve.wait_ge(dve_step, steps[0])
                V.tensor_tensor(facc2[:, n % 2, 0, :], facc2[:, n % 2, 0, :], facc2[:, n % 2, 1, :],
                                ALU.add).then_inc(fill_ready, 1)
                filled.append((C if part == 0 else A, ("ada", part, u)))
            filled = []

            def ada(part, u):
                n = ("ada", part, u)
                rg = C if part == 0 else A
                bank = rg.full(dve, n)
                c = slice(2 * u, 2 * u + 2)
                if part == 0:
                    ins = V.tensor_tensor(m1[:, c, 0], bank[:, 0:2], v(0, V_BMOD + 2 * u, 2), ALU.add)
                else:
                    ins = V.tensor_tensor(m2[:, part - 1, c], bank[:, 0:2], v(3, V_BADA + 48 * (part - 1) + 2 * u, 2), ALU.add)
                rg.free(n, ins)

            def gain(i, scale, g):
                return V.scalar_tensor_tensor(out=amul[:, i, :], in0=scale, scalar=1.0, in1=g, op0=ALU.add, op1=ALU.mult)

            dve.wait_ge(con_landed, 16)
            turned_vectors("vec", (1, 2, 3))
            bias = v(0, V_BMOD, 16).rearrange("p (a b) -> p a b", b=1).to_broadcast([P, 16, 2])
            ins = V.tensor_tensor(m1[:, 0:16, :], A.full(dve, "adat")[:, 0:32].rearrange("p (a b) -> p a b", a=16), bias, ALU.add)
            A.free("adat", ins)
            A.moved(dve, "adat")
            gain(0, m1[:, 8:16, 0], v(0, V_N1, 8))
            step(gain(1, m1[:, 8:16, 1], v(0, V_N1, 8)))
            norm(0)
            norm(1)

            def side_taps(y, p, w0, w2, last):
                for i, (yy, pp) in enumerate(zip(y, p)):
                    ins = V.scalar_tensor_tensor(out=yy[..., 1:T], in0=pp[..., 0:T - 1], scalar=w0[i], in1=yy[..., 1:T],
                                                 op0=ALU.mult, op1=ALU.add)
                step(ins)
                for i, (yy, pp) in enumerate(zip(y, p)):
                    ins = V.scalar_tensor_tensor(out=yy[..., 0:T - 1], in0=pp[..., 1:T], scalar=w2[i], in1=yy[..., 0:T - 1],
                                                 op0=ALU.mult, op1=ALU.add)
                last(ins)

            def conv_sides(i):
                nseg = 1 if i < 4 else 2
                n = ("d", i)
                y = (qF[:, i, :] if i < 4 else kF[:, i - 4, :] if i < 8 else ybuf[:, i - 8, :]).rearrange("p (a b) -> p a b", a=nseg)
                dve.wait_ge(centre_ready, i + 1)
                bank = A.full(dve, n)
                side_taps([y], [bank[:, 0:nseg * T].rearrange("p (a b) -> p a b", a=nseg)],
                          [v(0, V_CONV + i)], [v(0, V_CONV + 24 + i)], lambda ins: A.free(n, ins))

            pair = lambda ap: ap.rearrange("p a b -> p (a b)")
            def qk_norm():
                for j in range(3):
                    B.moved(dve, ("an", j))
                    r = hroot[:, j, :] if j < 2 else kroot
                    step(V.reciprocal(r, r))
                    x = pair(qA[:, 2 * j:2 * j + 2, :]) if j < 2 else kA[:, :]
                    V.scalar_tensor_tensor(out=x, in0=x, scalar=v(0, V_QG if j < 2 else V_KG), in1=r,
                                           op0=ALU.mult, op1=ALU.mult).then_inc(qk_normed, 1)

            def rotary(rg, n, x, cos, sin, tmp, signal):
                m = x.shape[1]
                bank = rg.full(dve, n)
                rg.free(n, V.tensor_tensor(tmp, bank[:, 0:m * T].rearrange("p (a b) -> p a b", a=m), over(sin, m), ALU.mult))
                step(V.tensor_tensor(x, x, over(cos, m), ALU.mult))
                V.tensor_tensor(x, x, tmp, ALU.add).then_inc(signal, 1)
            dve.wait_ge(con1_landed, 16)

            def qk_rotary():
                for j in range(3):
                    x = qA[:, 2 * j:2 * j + 2, :] if j < 2 else kA[:, 0:T].rearrange("p (a b) -> p a b", a=1)
                    m = x.shape[1]
                    tmp = atmp[:, j % 2, 0:m * T].rearrange("p (a b) -> p a b", a=m)
                    rotary(B, ("rot", j), x, c_one("cos", T), c_one("sin", T), tmp, rope_done)

            def attention(tag, base, keys, scaled, pbuf, mask=None):
                def maxima(u):
                    n = keys(u)
                    st = stat[:, u % 4, :]
                    name = (tag, "s", u)
                    bank = B.full(dve, name)
                    if scaled:
                        p = pbuf[:, u % 3, :]
                        if u >= 3:
                            A.full(dve, (tag, "pt", u - 3))
                        if n > P:
                            V.tensor_scalar(p[:, 0:n - P], bank[:, 0:n - P], HD ** -0.5, None, ALU.mult)
                        ins = V.scalar_tensor_tensor(out=p[:, n - P:n], in0=bank[:, n - P:n], scalar=HD ** -0.5,
                                                     in1=mask, op0=ALU.mult, op1=ALU.add)
                        B.free(name, ins)
                        B.moved(dve, name)
                        step(V.tensor_reduce(st[:, 0:1], p[:, 0:n], AX_X, ALU.max))
                        V.tensor_scalar(st[:, 1:2], st[:, 0:1], -1.0, None, ALU.mult).then_inc(max_ready, 1)
                    else:
                        step(V.tensor_reduce(st[:, 0:1], bank[:, 0:n], AX_X, ALU.max))
                        V.tensor_scalar(st[:, 1:2], st[:, 0:1], -HD ** -0.5, None, ALU.mult).then_inc(max_ready, 1)

                def divide(u):
                    n = keys(u)
                    st = stat[:, u % 4, :]
                    if scaled:
                        dve.wait_ge(exp_done, base + u + 1)
                    else:
                        B.moved(dve, (tag, "s", u))
                    step(V.reciprocal(st[:, 3:4], st[:, 2:3]))
                    p = pbuf[:, u % 3, 0:n]
                    V.tensor_scalar(p, p, st[:, 3:4], None, ALU.mult).then_inc(prob_ready, 1)

                def stage(i):
                    if i < 2 * HQ:
                        maxima(i)
                    if 1 <= i <= 2 * HQ:
                        divide(i - 1)
                return stage
            stage = attention("a1", 0, lambda u: 512, False, prob)
            for i in range(2 * HQ):
                if i < 12:
                    conv_sides(i)
                if i == 0:
                    qk_norm()
                elif i == 1:
                    qk_rotary()
                elif i > 2:
                    stage(i - 3)
            for i in range(2 * HQ - 3, 2 * HQ + 1):
                stage(i)

            bank = A.full(dve, "ab")
            dve.wait_ge(gc_landed, 64)
            bias = gconst[:, 1, :].rearrange("p (a d h) -> p a d h", a=1, d=2).to_broadcast([P, 4, 2, 4])
            ins = V.tensor_tensor(gates[:, G_T0, :].rearrange("p (d t h) -> p t d h", d=2, t=4),
                                  bank[:, 0:64].rearrange("p (t x d h) -> p t x d h", t=4, x=2, d=2)[:, :, 0, :, :],
                                  bias, ALU.add)
            A.free("ab", ins)
            A.moved(dve, "ab", 1)
            V.scalar_tensor_tensor(out=gates[:, G_T1, :], in0=gates[:, G_T0, :], scalar=-1.0, in1=gates[:, G_T0, :],
                                   op0=ALU.mult, op1=ALU.max).then_inc(sp_abs, 1)
            dve.wait_ge(sp_ln, 1)
            V.tensor_scalar(gates[:, G_EA, 0:8], gates[:, G_EA, 0:8], -1.0, None, ALU.mult)
            step(V.scalar_tensor_tensor(out=gates[:, G_T0, :], in0=gates[:, G_T0, :], scalar=0.0, in1=gates[:, G_T1, :],
                                        op0=ALU.max, op1=ALU.add))
            ea = gates[:, G_EA, 0:8].rearrange("p (d a h) -> p d a h", d=2, a=1).to_broadcast([P, 2, 4, 4])
            V.tensor_tensor(gates[:, G_G, :].rearrange("p (d t h) -> p d t h", d=2, t=4),
                            gates[:, G_T0, :].rearrange("p (d t h) -> p d t h", d=2, t=4), ea, ALU.mult).then_inc(g_ready, 1)

            for i in range(8):
                wd = T if i < 4 else 512
                r = hroot[:, i % 2, 0:wd]
                A.moved(dve, ("l2", i))
                step(V.reciprocal(r, r))
                x = qF[:, i, :] if i < 4 else kF[:, i - 4, :]
                V.tensor_tensor(x, x, r, ALU.mult).then_inc(l2_ready, 1)

            norm(2)

            bank = A.full(dve, "gc")
            V.tensor_copy(gates[:, G_CUM, :], bank[:, 0:32])
            V.tensor_scalar(gates[:, G_NCUM, :], bank[:, 0:32], -1.0, None, ALU.mult)
            A.free("gc", V.tensor_copy(gates[:, G_TOT, :], bank[:, 32:64]))
            A.moved(dve, "gc")
            V.tensor_tensor(gates[:, G_T0, :], gates[:, G_TOT, :], gates[:, G_CUM, :], ALU.subtract).then_inc(tmg_ready, 1)
            dve.wait_ge(gate_ready, 1)
            V.tensor_scalar(gates[:, G_NEG, :], gates[:, G_EG, :], -1.0, None, ALU.mult).then_inc(ngl_ready, 1)

            heads = lambda ap: ap.rearrange("p (a b) -> p a b", a=4)

            def prepare(half):
                for s, d in GROUPS[half]:
                    g, tt = 2 * s + d, TILE[d][s]
                    way = ("fwd", "bwd")[d]
                    bank = A.full(dve, ("gb", g))
                    ins = V.scalar_tensor_tensor(out=heads(dec[:, g % 4, :]), in0=heads(bank[:, :]), scalar=-1.0,
                                                 in1=over(c_one("strict_" + way), 4), op0=ALU.mult, op1=ALU.add)
                    if tt < 2:
                        ins = V.tensor_tensor(heads(ATm[:, g % 4, :]), heads(bank[:, :]), over(c_one("incl_" + way), 4), ALU.add)
                    A.free(("gb", g), ins)
                    if g % 4:
                        lower(g - 1)
                lower(g)

            def lower(g):
                s, d = g // 2, g % 2
                tt = TILE[d][s]
                dve.wait_ge(dec_ready, g + 1)
                bank = A.full(dve, ("kk", g))
                for h in range(4):
                    c = slice(h * P, (h + 1) * P)
                    ins = V.scalar_tensor_tensor(out=dec[:, g % 4, c], in0=bank[:, c], scalar=gcol(G_BETA, d, tt, h),
                                                 in1=dec[:, g % 4, c], op0=ALU.mult, op1=ALU.mult)
                A.free(("kk", g), ins)
                if tt < 2:
                    dve.wait_ge(att_ready, g - 3)
                    n = ("kq", g)
                    B.free(n, V.tensor_tensor(ATm[:, g % 4, :], B.full(dve, n)[:, :], ATm[:, g % 4, :], ALU.mult))

            def level(half, lv):
                for s, d in GROUPS[half]:
                    n = ("m1", 2 * s + d, lv)
                    A.free(n, V.tensor_tensor(heads(dec[:, n[1] % 4, :]), heads(A.full(dve, n)[:, :]),
                                              over(c_one("level", P, lv), 4), ALU.mult))
                for s, d in GROUPS[half]:
                    g, tt = 2 * s + d, TILE[d][s]
                    if lv < 6:
                        n = ("dt", g, lv)
                        A.free(n, V.tensor_tensor(Tm[:, g % 4, :], Tm[:, g % 4, :], A.full(dve, n)[:, :], ALU.subtract))
                    n = ("dtt", g, lv)
                    A.free(n, V.tensor_tensor(TTm[:, g, :], TTm[:, g, :], A.full(dve, n)[:, :], ALU.subtract))
                    if lv == 6:
                        A.moved(dve, n)
                        for h in range(4):
                            c = slice(h * P, (h + 1) * P)
                            ins = V.tensor_scalar(TTm[:, g, c], TTm[:, g, c], gcol(G_BETA, d, tt, h), None, ALU.mult)
                        ins.then_inc(ttb_ready, 1)

            def advance(s):
                for d in range(2):
                    g, tt = 2 * s + d, TILE[d][s]
                    if tt < 2:
                        n = ("og", g)
                        bank = B.full(dve, n)
                        o = oG[:, :, tt * P:(tt + 1) * P]
                        if s == 2:
                            ins = V.tensor_copy(o, heads(bank[:, :]))
                        else:
                            B.moved(dve, ("og", 5 - d))
                            ins = V.tensor_tensor(o, heads(bank[:, :]), o, ALU.add)
                        B.free(n, ins)
                    if s < 3:
                        n = ("st", g)
                        bank = A.full(dve, n)
                        if s == 0:
                            ins = V.tensor_copy(S[:, d, :], bank[:, :])
                        else:
                            A.moved(dve, ("st", g - 2))
                            for h in range(4):
                                c = slice(h * P, (h + 1) * P)
                                ins = V.scalar_tensor_tensor(out=S[:, d, c], in0=S[:, d, c], scalar=gcol(G_DL, d, tt, h),
                                                             in1=bank[:, c], op0=ALU.mult, op1=ALU.add)
                        A.free(n, ins)

            def fill_place(n):
                if n < 16:
                    fill(0, 8 + n)
                if n >= 1:
                    ada(0, 7 + n)
            for what, *args in DELTA:
                dict(prepare=prepare, level=level, advance=advance, fill=fill_place)[what](*args)
            C.moved(dve, ("ada", 0, 23))
            step(gain(2, m1[:, 32:40, 0], v(0, V_N2, 8)))

            def gains2(l):
                A.moved(dve, ("ada", 1 + l, 23))
                gain(3 + 2 * l, m2[:, l, 8:16], v(1, V_NMIX + 8 * l, 8))
                step(gain(4 + 2 * l, m2[:, l, 32:40], v(1, V_NFFN + 8 * l, 8)))

            def head_norm(j, o, gains, gate, dst):
                for i in range(2):
                    A.moved(dve, ("hn", j, i))
                    step(V.reciprocal(hroot[:, i, :], hroot[:, i, :]))
                    for h in (2 * i, 2 * i + 1):
                        ins = V.scalar_tensor_tensor(out=o[:, h, :], in0=o[:, h, :], scalar=gains(h),
                                                     in1=hroot[:, i, (h % 2) * T:(h % 2 + 1) * T], op0=ALU.mult, op1=ALU.mult)
                    step(ins)
                    for h in (2 * i, 2 * i + 1):
                        V.tensor_tensor(dst[:, 4 + h, :], o[:, h, :], gate[:, h, :], ALU.mult).then_inc(hn_out, 1)
            dve.wait_ge(hn_sq, 1)
            head_norm(0, oG, lambda h: v(0, V_GDNG), zs, mixT)

            def residual(jobs, gate):
                for dt, (rg, name, part) in enumerate(jobs):
                    bank = rg.full(dve, name)
                    ins = V.scalar_tensor_tensor(out=xT[:, dt, :], in0=bank[:, part * T:(part + 1) * T],
                                                 scalar=gate[:, dt:dt + 1], in1=xT[:, dt, :], op0=ALU.mult, op1=ALU.add)
                    if dt == KT - 1 or jobs[dt + 1][1] != name:
                        rg.free(name, ins)

            def acc_jobs(tag):
                return [(B if dt < 6 else C, (tag, "acc", dt // 2), dt % 2) for dt in range(KT)]
            residual([(A, ("xo1", dt), 0) for dt in range(KT)], m1[:, 16:24, 0])
            norm(3)
            for f in range(FT + 3):
                if f < FT:
                    n = ("ffn1", "gu", f)
                    bank = A.full(dve, n)
                    dve.wait_ge(centre_ready, 12 + f + 1)
                    y = yc[:, f % 3, :]
                    side_taps([y[:, 0:T], y[:, T:512]], [bank[:, 0:T], bank[:, T:512]],
                              [v(1, V_FW01 + f), v(1, V_FW01 + FT + f)], [v(2, V_FW2 + f), v(2, V_FW2 + FT + f)],
                              lambda ins: A.free(n, ins))
                if 1 <= f <= FT:
                    y = yc[:, (f - 1) % 3, :]
                    dve.wait_ge(silu_ready, f)
                    V.tensor_tensor(gT[:, (f - 1) % 4, :], y[:, 0:T], y[:, T:512], ALU.mult).then_inc(gT_ready, 1)
                if f < 24:
                    fill(1, f)
                if f:
                    ada(1, f - 1)
            residual(acc_jobs("ffn1"), m1[:, 40:48, 0])
            gains2(0)
            norm(4)

            dve.wait_ge(con2_landed, 16)
            for l in range(2):
                n0 = 5 + 3 * l
                norm(n0)
                stage = attention(("a2", l), 16 * l, lambda u: (u % 2 + 1) * P, True, prob2, c_two("causal"))
                for i, (kind, _, j) in enumerate(SLOTS2):
                    if kind == "rr":
                        x = (qR if j < 2 else kR)[:, 2 * (j % 2):2 * (j % 2) + 2, :]
                        rotary(A, (l, "rr", j), x, c_two("cos", T), c_two("sin", T),
                               rtmp[:, j % 2, :].rearrange("p (a b) -> p a b", a=2), rrope)
                    stage(i)
                norm(n0 + 1)
                for h in range(4):
                    n = (l, "rs", h)
                    B.free(n, V.tensor_tensor(AR[:, h % 2, 0:384], B.full(dve, n)[:, 0:384],
                                              c_two("ret", 384, h * 384), ALU.mult))
                dve.wait_ge(sg_ready, l + 1)
                head_norm(1 + l, oR, lambda h: v(3, V_RETG + 4 * l + h), sgr, mix2)
                residual([(A, (("xo2", l), dt), 0) for dt in range(KT)], m2[:, l, 16:24])
                norm(n0 + 2)
                if l == 0:
                    for f in range(FT + 3):
                        if f < FT:
                            n = ("ffn2", "gu", f)
                            bank = A.full(dve, n)
                            dve.wait_ge(silu_ready, FT + f + 1)
                            A.free(n, V.tensor_tensor(gT[:, f % 4, :], yc[:, f % 3, 0:T], bank[:, T:512], ALU.mult))
                        if f < 24:
                            fill(2, f)
                        if f:
                            ada(2, f - 1)
                    residual(acc_jobs("ffn2"), m2[:, 0, 40:48])
                    gains2(1)

            bank = A.full(dve, "logits")
            A.free("logits", V.tensor_copy(rout[:, 0:2, :], bank[:, 0:16].rearrange("p (a b) -> p a b", a=2)))
            A.moved(dve, "logits")
            R = lambda i, tt, a=0, b=8: rout[:, i + tt, a:b]
            both = range(TT)
            for tt in both:
                ins = V.max(R(2, tt), R(0, tt))
            step(ins)
            for tt in both:
                V.max_index(idx_u[:, tt, :], R(2, tt), R(0, tt))
                ins = V.tensor_tensor(R(12, tt, 0, 1), R(2, tt, 0, 1), R(2, tt, 1, 2), ALU.subtract)
            ins.then_inc(top_ready, 1)
            dve.wait_ge(top_ready, 1)
            for tt in both:
                ins = V.tensor_copy(R(6, tt), idx_u[:, tt, :])
            step(ins)
            for tt in both:
                V.tensor_scalar(R(8, tt), c_all("iota", 8), R(6, tt, 0, 1), None, ALU.is_equal)
                ins = V.tensor_scalar(R(10, tt), c_all("iota", 8), R(6, tt, 1, 2), None, ALU.is_equal)
            step(ins)
            for tt in both:
                ins = V.tensor_tensor(R(4, tt), R(8, tt), R(10, tt), ALU.add)
            ins.then_inc(sel_ready, 1)
            dve.wait_ge(wt_ready, 1)
            for tt in both:
                ins = V.tensor_scalar(R(16, tt), R(8, tt), R(14, tt, 0, 1), None, ALU.mult)
            step(ins)
            for tt in both:
                ins = V.scalar_tensor_tensor(out=R(16, tt), in0=R(10, tt), scalar=R(14, tt, 1, 2), in1=R(16, tt),
                                             op0=ALU.mult, op1=ALU.add)
            step(ins)
            dve.wait_ge(sel_ready, 1)
            bank = A.full(dve, "pos")
            for tt in both:
                V.scalar_tensor_tensor(out=R(18, tt), in0=bank[:, tt * 8:(tt + 1) * 8], scalar=1.0, in1=R(4, tt),
                                       op0=ALU.add, op1=ALU.mult)
            A.free("pos", V.tensor_copy(cnt_i[:, :], bank[:, 16:24]))
            A.moved(dve, "pos")
            for tt in both:
                ins = V.tensor_scalar(R(18, tt), R(18, tt), -1.0, None, ALU.add)
            step(ins)
            for e in range(NE):
                for tt in both:
                    V.tensor_scalar(Pg[:, tt, e, :], c_all("iota", 256), R(18, tt, e, e + 1), None, ALU.is_equal)
                if e >= 2:
                    A.full(dve, ("pwT", e - 2))
                for tt in both:
                    ins = V.tensor_scalar(Pw[:, e % 2, tt * 256:(tt + 1) * 256], c_all("iota", 256), R(18, tt, e, e + 1),
                                          R(16, tt, e, e + 1), ALU.is_equal, ALU.mult)
                ins.then_inc(pw_ready, 1)
            V.memset(facc, 0.0).then_inc(moved, 2)
            V.memset(stat[:, 0, 0:1], 0.0).then_inc(gated, 2)
            V.memset(stat[:, 1, 0:1], 0.0).then_inc(pair_used, 3)

            def split_half(e, i):
                n = i // 2
                dve.wait_ge(wh_ready, e * (2 * EU) + (i + 1))
                V.tensor_tensor(half_of(wL[n % 3], i), raw[i % HALVES], half_of(wH[n % 3], i), ALU.subtract).then_inc(split_ready, 1)

            def split(e, n):
                split_half(e, 2 * n)
                split_half(e, 2 * n + 1)
            split(0, 0)
            split(0, 1)

            def expert(e, ns):
                wide = ns == T
                for j in range(KT):
                    dve.wait_ge(xh_ready, e * KT + (j + 1))
                    V.tensor_tensor(xgL[:, j, 0:ns], gather_bank(j)[:, 0:ns], xgH[:, j, 0:ns], ALU.subtract).then_inc(moved, 1)
                split(e, 2)
                for what, c in e_steps:
                    if what == "turn":
                        dve.wait_ge(gh_ready, e * FC + (c + 1))
                        V.tensor_tensor(gL[:, c % 2, 0:2 * ns], hid[:, c % 2, :] if wide else banks[2 + c % 2][:, 0:T],
                                        gH[:, c % 2, 0:2 * ns], ALU.subtract).then_inc(gl_ready, 1)
                        continue
                    if what == "u":
                        dve.wait_ge(sge_ready, e * FC + (c + 1))
                        if wide and c >= 2:
                            dve.wait_ge(gl_ready, e * FC + (c - 1))
                        V.tensor_tensor(hid[:, c % 2, 0:2 * ns], sge[:, c % 2, 0:2 * ns],
                                        banks[1][:, :] if wide else banks[c % 2][:, T:512], ALU.mult).then_inc(gated, 1)
                    n = e_order[what, c]
                    if n + 3 < EU:
                        split(e, n + 3)
                with dve.If(e < NE - 1):
                    split(e, EU)
                dve.wait_ge(pair_used, e * EU + (EU + 3))
                for i in range(ns // P):
                    ins = V.tensor_copy(ye[:, i, 512:1024], banks[5 + 2 * i][:, :])
                ins.then_inc(ye_ready[1], 1)
                with dve.If(e < NE - 1):
                    split(e, EU + 1)
                for j in range(KT):
                    dve.wait_ge(xj_full, e * 16 + (KT + j + 1))
                    V.tensor_tensor(facc[:, j, :], banks[2 + j % 2][:, 0:T], facc[:, j, :], ALU.add).then_inc(moved, 1)

            with dve.Fori(0, NE) as e:
                count = dve.value_load(cnt_i[0:1, bass.ts(e, 1)], min_val=0, max_val=T)
                with dve.If(count > NARROW):
                    expert(e, T)
                with dve.Else():
                    expert(e, NARROW)
                dve.nop()
            dve.wait_ge(moved, 16 * NE + 2)
            for dt in range(KT):
                V.scalar_tensor_tensor(out=xT[:, dt, :], in0=facc[:, dt, :], scalar=m2[:, 1, 40 + dt:41 + dt],
                                       in1=xT[:, dt, :], op0=ALU.mult, op1=ALU.add).then_inc(x_updated, 1)
            norm(11)
            for i in range(4):
                dve.wait_ge(fin_ready, i + 2)
                V.tensor_copy(outT[:, i // 2, (i % 2) * 512:(i % 2 + 1) * 512], banks[4 + i][:, :]).then_inc(out_ready, 1)

        @block.gpsimd
        def _(pool):
            steps = [0]
            G = nc.gpsimd

            def step(ins):
                steps[0] += 1
                ins.then_inc(pool_step, 1)
                pool.wait_ge(pool_step, steps[0])
            heads = lambda ap: ap.rearrange("p (a b) -> p a b", a=4)
            pool.wait_ge(con_landed, 16)
            pool.wait_ge(con1_landed, 16)
            pool.wait_ge(ngl_ready, 1)
            for h in range(4):
                A.moved(pool, ("ktm", h))

            def seeds(half):
                for s, d in GROUPS[half]:
                    g = 2 * s + d
                    nb, eye = over(c_one("level"), 4), over(ident, 4)
                    A.moved(pool, ("kk", g))
                    G.tensor_tensor(heads(Tm[:, g % 4, :]), heads(dec[:, g % 4, :]), nb, ALU.mult)
                    A.moved(pool, ("lt", g))
                    step(G.tensor_tensor(heads(TTm[:, g, :]), heads(LTm[:, g % 4, :]), nb, ALU.mult))
                    G.tensor_tensor(heads(Tm[:, g % 4, :]), heads(Tm[:, g % 4, :]), eye, ALU.add)
                    G.tensor_tensor(heads(TTm[:, g, :]), heads(TTm[:, g, :]), eye, ALU.add).then_inc(seed_ready, 1)

            def keys(s):
                for d in range(2):
                    g, tt = 2 * s + d, TILE[d][s]
                    if s:
                        A.full(pool, ("st", g - 2))
                    for h in range(4):
                        c = slice(h * P, (h + 1) * P)
                        G.tensor_scalar(kbe[:, d, c], k_tm[:, tt, h, :], gcol(G_NEG, d, tt, h), None, ALU.mult)
                        ins = G.tensor_scalar(kdec[:, d, c], k_tm[:, tt, h, :], gcol(G_KD, d, tt, h), None, ALU.mult)
                    ins.then_inc(kb_ready, 1)
            seeds(0)
            keys(0)
            seeds(1)
            for g in range(4, 8):
                tt = TILE[g % 2][g // 2]
                A.moved(pool, ("gb", g))
                G.tensor_tensor(heads(qdec[:, g % 4, :]), qF[:, :, tt * P:(tt + 1) * P], heads(egb[:, g % 4, :]),
                                ALU.mult).then_inc(qdec_ready, 1)
            for s in range(1, 4):
                keys(s)

        @block.sync
        def _(sp):
            sp.dma_start(con[:, :], t["constants"][:, 0:C_ALL_W]).then_inc(con_landed, 16)
            sp.dma_start(xraw[:, 0:2, :], t["x"][0].rearrange("(a p) n -> p a n", p=P)).then_inc(x_landed, 16)
            sp.dma_start(xraw[:, 2:4, :], t["ctx"][0].rearrange("(a p) n -> p a n", p=P)).then_inc(x_landed, 16)
            for k, (name, ap) in enumerate(units):
                if k == 1:
                    sp.wait_ge(v0_landed, 16 * 12)
                if need[k]:
                    sp.wait_ge(unit_used, need[k])
                n = ap.shape[1]
                sp.dma_start(ring[:, slot[k], :].rearrange("p (a b) -> p a b", a=n), ap).then_inc(landed[slot[k]], 16)
            src = dict(g=t["moe_w_gate_2"], u=t["moe_w_up_2"], d=t["moe_w_down_2"])
            sp.wait_ge(unit_used, U0 - RING + (HALVES - 1) // 2)
            sp.wait_ge(hn_out, 12)
            with sp.Fori(0, NE) as e:
                for (m, c), n in e_order.items():
                    w = src[m][0][e, :, :]
                    ap = w_rows(w, c) if m == "d" else w_cols(w, c)
                    rows = ap.shape[1] // 2
                    for i in range(2):
                        h = 2 * n + i
                        sp.wait_ge(split_ready, e * (2 * EU) + (h + 1))
                        sp.dma_start(raw[h % HALVES].rearrange("p (a b) -> p a b", a=rows),
                                     ap[:, i * rows:(i + 1) * rows, :]).then_inc(raw_landed[h % HALVES], 16)
            for tt in range(TT):
                sp.wait_ge(out_ready, 2 * tt + 2)
                sp.dma_start(out[0, tt * P:(tt + 1) * P, :], outT[:, tt, :]).then_inc(out_landed, 16)
            sp.wait_ge(out_landed, 16 * TT)


_INS = ["x", "c", "ctx", "c_ctx", "w_mod", "b_mod", "norm1_g", "w_in", "q_norm_g", "k_norm_g", "attn_out_g",
        "conv_qkv_w", "a_log_f", "a_log_b", "dt_bias_f", "dt_bias_b", "gdn_norm_g", "w_out", "norm2_g", "w_up",
        "ffn_conv_w", "ffn_conv_b", "w_down", "final_norm_g", "c_2", "norm_mix_g_2", "norm_ffn_g_2", "ada_w_2",
        "ada_b_2", "w_in_2", "w_out_2", "att_out_g_2", "ret_out_g_2", "ffn_w_gate_2", "ffn_w_up_2",
        "ffn_w_down_2", "router_w_2", "moe_w_gate_2", "moe_w_up_2", "moe_w_down_2", "final_norm_g_2"]


def kernel(**inputs):
    import concourse.bacc as _bacc
    from concourse.bass_utils import run_bass_kernel_spmd as _run

    nc = _bacc.Bacc("TRN2", target_bir_lowering=False, num_devices=1, dynamic_dma_scratch_size=1024)
    arrays, t = {}, {}
    for name in _INS + ["constants"]:
        a = shape_constants() if name == "constants" else np.ascontiguousarray(inputs[name])
        arrays[f"in_{name}_dram"] = a
        t[name] = nc.dram_tensor(f"in_{name}_dram", a.shape, mybir.dt.from_np(a.dtype), kind="ExternalInput").ap()
    out = nc.dram_tensor("out_0_dram", (1, T, D), F32, kind="ExternalOutput").ap()
    build(nc, t, out)
    r = _run(nc, [arrays], core_ids=[0])
    return r.results[0]["out_0_dram"]
```
